# Optimizing a Trainium2 kernel written in Bass

```python
import math
import jax, jax.numpy as jnp
from jax import lax
import numpy as np

D_MODEL = 1024
BATCH = 1
SEQ = 512
DEPTH = 2

CHUNK = 64
N_MIXERS = 3
DEEPNORM_ALPHA = (2 * DEPTH) ** 0.25
DEEPNORM_BETA = (8 * DEPTH) ** -0.25
LN_EPS = 1e-5
RMS_EPS = 1e-6
NEG_INF = -1e30

GLA_HEADS = 4
GLA_DK = D_MODEL // 2 // GLA_HEADS
GLA_DV = D_MODEL // GLA_HEADS
GLA_GATE_RANK = 16
GLA_TAU = 16.0
GLA_HK = GLA_HEADS * GLA_DK
GLA_HV = GLA_HEADS * GLA_DV

RPA_HEADS = 16
RPA_HEAD_DIM = D_MODEL // RPA_HEADS
RPA_LEFT_CHUNKS = 8
RPA_BAND = (RPA_LEFT_CHUNKS + 1) * CHUNK
RPA_MAX_REL = 128

MLA_HEADS = 8
MLA_NOPE = 128
MLA_ROPE = 64
MLA_V = 128
MLA_Q_RANK = 384
MLA_KV_RANK = 256
MLA_QK = MLA_NOPE + MLA_ROPE
ROPE_BASE = 10000.0
Q_BLOCK = 128

FFN_HIDDEN = -(-8 * D_MODEL // (3 * 256)) * 256

N_GLA = len(range(0, DEPTH, N_MIXERS))
N_RPA = len(range(1, DEPTH, N_MIXERS))
N_MLA = len(range(2, DEPTH, N_MIXERS))

kernel_name = "hybrid_gla_chunkrel_mla_deepnorm"

def layer_norm(x, g, b):
    xf = x.astype(jnp.float32)
    mu = jnp.mean(xf, -1, keepdims=True)
    var = jnp.mean(jnp.square(xf - mu), -1, keepdims=True)
    y = (xf - mu) * lax.rsqrt(var + LN_EPS)
    return (y * g.astype(jnp.float32) + b.astype(jnp.float32)).astype(x.dtype)

def rms_norm(x, g):
    xf = x.astype(jnp.float32)
    y = xf * lax.rsqrt(jnp.mean(jnp.square(xf), -1, keepdims=True) + RMS_EPS)
    return (y * g.astype(jnp.float32)).astype(x.dtype)

def gla_mixer(x, w_in, w_gate_up, b_gate, norm_g, w_out):
    B, S, _ = x.shape
    nc = S // CHUNK
    f32 = jnp.float32
    q, k, v, r, g_low = jnp.split(
        x @ w_in, [GLA_HK, 2 * GLA_HK, 2 * GLA_HK + GLA_HV, 2 * GLA_HK + 2 * GLA_HV], axis=-1)
    log_a = jax.nn.log_sigmoid((g_low @ w_gate_up + b_gate).astype(f32)) / GLA_TAU

    def to_chunks(t, d):
        return t.astype(f32).reshape(B, nc, CHUNK, GLA_HEADS, d).transpose(0, 3, 1, 2, 4)

    q = to_chunks(q, GLA_DK) * (GLA_DK ** -0.5)
    k = to_chunks(k, GLA_DK)
    v = to_chunks(v, GLA_DV)
    cum = jnp.cumsum(to_chunks(log_a, GLA_DK), axis=3)
    total = cum[:, :, :, -1:, :]
    q_dec = q * jnp.exp(cum)
    k_inv = k * jnp.exp(-cum)
    k_end = k * jnp.exp(total - cum)
    causal = jnp.tril(jnp.ones((CHUNK, CHUNK), dtype=bool))
    a = jnp.where(causal, jnp.einsum('bhcid,bhcjd->bhcij', q_dec, k_inv), 0.0)
    o_intra = jnp.einsum('bhcij,bhcjv->bhciv', a, v)
    decay = jnp.swapaxes(jnp.exp(total), -1, -2)

    def step(state, inp):
        qd, ke, vc, dc = inp
        o = jnp.einsum('bhid,bhdv->bhiv', qd, state)
        state = state * dc + jnp.einsum('bhjd,bhjv->bhdv', ke, vc)
        return state, o

    state0 = jnp.zeros((B, GLA_HEADS, GLA_DK, GLA_DV), f32)
    xs = (jnp.moveaxis(q_dec, 2, 0), jnp.moveaxis(k_end, 2, 0),
          jnp.moveaxis(v, 2, 0), jnp.moveaxis(decay, 2, 0))
    _, o_inter = lax.scan(step, state0, xs)
    o = o_intra + jnp.moveaxis(o_inter, 0, 2)
    o = o.transpose(0, 2, 3, 1, 4).reshape(B, S, GLA_HEADS, GLA_DV)
    mu = jnp.mean(o, -1, keepdims=True)
    var = jnp.mean(jnp.square(o - mu), -1, keepdims=True)
    o = ((o - mu) * lax.rsqrt(var + LN_EPS)).reshape(B, S, GLA_HV) * norm_g.astype(f32)
    y = jax.nn.silu(r.astype(f32)) * o
    return y.astype(x.dtype) @ w_out

def rpa_mixer(x, w_in, rel_bias, w_out):
    B, S, _ = x.shape
    nc = S // CHUNK
    pad = RPA_LEFT_CHUNKS * CHUNK
    q, k, v = jnp.split(x @ w_in, 3, axis=-1)
    q = q.reshape(B, nc, CHUNK, RPA_HEADS, RPA_HEAD_DIM) * (RPA_HEAD_DIM ** -0.5)
    padw = ((0, 0), (pad, 0), (0, 0), (0, 0))
    k = jnp.pad(k.reshape(B, S, RPA_HEADS, RPA_HEAD_DIM), padw)
    v = jnp.pad(v.reshape(B, S, RPA_HEADS, RPA_HEAD_DIM), padw)
    band_pos = jnp.arange(RPA_BAND)
    rel = jnp.clip(pad + jnp.arange(CHUNK)[:, None] - band_pos[None, :],
                   -RPA_MAX_REL, RPA_MAX_REL) + RPA_MAX_REL
    bias = rel_bias[:, rel].astype(jnp.float32)

    def one_chunk(c):
        q_c = lax.dynamic_index_in_dim(q, c, axis=1, keepdims=False)
        k_c = lax.dynamic_slice_in_dim(k, c * CHUNK, RPA_BAND, axis=1)
        v_c = lax.dynamic_slice_in_dim(v, c * CHUNK, RPA_BAND, axis=1)
        s = jnp.einsum('bihd,bjhd->bhij', q_c, k_c).astype(jnp.float32) + bias
        valid = (c * CHUNK - pad + band_pos) >= 0
        p = jax.nn.softmax(jnp.where(valid, s, NEG_INF), axis=-1)
        return jnp.einsum('bhij,bjhd->bihd', p.astype(v_c.dtype), v_c)

    o = lax.map(one_chunk, jnp.arange(nc))
    o = o.transpose(1, 0, 2, 3, 4).reshape(B, S, RPA_HEADS * RPA_HEAD_DIM)
    return o @ w_out

def rope_tables(S):
    inv = ROPE_BASE ** (-jnp.arange(0, MLA_ROPE, 2, dtype=jnp.float32) / MLA_ROPE)
    ang = jnp.arange(S, dtype=jnp.float32)[:, None] * inv[None, :]
    return jnp.cos(ang), jnp.sin(ang)

def apply_rope(t, cos, sin):
    extra = t.ndim - 3
    c = cos.reshape(cos.shape[0], *([1] * extra), cos.shape[1])
    s = sin.reshape(sin.shape[0], *([1] * extra), sin.shape[1])
    t1, t2 = jnp.split(t.astype(jnp.float32), 2, axis=-1)
    return jnp.concatenate([t1 * c - t2 * s, t1 * s + t2 * c], -1).astype(t.dtype)

def mla_mixer(x, w_in, q_norm_g, kv_norm_g, w_uq, w_ukv, w_out):
    B, S, _ = x.shape
    c_q, c_kv, k_rope = jnp.split(x @ w_in, [MLA_Q_RANK, MLA_Q_RANK + MLA_KV_RANK], axis=-1)
    q = (rms_norm(c_q, q_norm_g) @ w_uq).reshape(B, S, MLA_HEADS, MLA_QK)
    kv = (rms_norm(c_kv, kv_norm_g) @ w_ukv).reshape(B, S, MLA_HEADS, MLA_NOPE + MLA_V)
    q_nope, q_rope = jnp.split(q, [MLA_NOPE], axis=-1)
    k_nope, v = jnp.split(kv, [MLA_NOPE], axis=-1)
    cos, sin = rope_tables(S)
    q_rope = apply_rope(q_rope, cos, sin)
    k_rope = apply_rope(k_rope, cos, sin)
    scale = MLA_QK ** -0.5
    nqb = S // Q_BLOCK
    qn_b = jnp.moveaxis((q_nope * scale).reshape(B, nqb, Q_BLOCK, MLA_HEADS, MLA_NOPE), 1, 0)
    qr_b = jnp.moveaxis((q_rope * scale).reshape(B, nqb, Q_BLOCK, MLA_HEADS, MLA_ROPE), 1, 0)
    k_chunk = jnp.arange(S) // CHUNK

    def one_block(args):
        qn, qr, i = args
        s = (jnp.einsum('bqhd,bkhd->bhqk', qn, k_nope)
             + jnp.einsum('bqhr,bkr->bhqk', qr, k_rope)).astype(jnp.float32)
        q_chunk = (i * Q_BLOCK + jnp.arange(Q_BLOCK)) // CHUNK
        mask = k_chunk[None, :] <= q_chunk[:, None]
        p = jax.nn.softmax(jnp.where(mask, s, NEG_INF), axis=-1)
        return jnp.einsum('bhqk,bkhd->bqhd', p.astype(v.dtype), v)

    o = lax.map(one_block, (qn_b, qr_b, jnp.arange(nqb)))
    o = jnp.moveaxis(o, 0, 1).reshape(B, S, MLA_HEADS * MLA_V)
    return o @ w_out

def swiglu(x, w_in, w_out):
    gate, up = jnp.split(x @ w_in, 2, axis=-1)
    return (jax.nn.silu(gate) * up) @ w_out

def _w(k, shape, fan_in, scale=1.0):
    return jax.random.normal(k, shape, jnp.float32) * (scale * fan_in ** -0.5)

def setup_inputs(seed: int = 0) -> dict:
    key = jax.random.key(seed)
    ks = jax.random.split(key, 20)
    D = D_MODEL
    gla_cols = 2 * GLA_HK + 2 * GLA_HV + GLA_GATE_RANK
    mla_cols = MLA_Q_RANK + MLA_KV_RANK + MLA_ROPE
    return {
        "x": jax.random.normal(ks[0], (BATCH, SEQ, D), jnp.float32),
        "gla_w_in": _w(ks[1], (N_GLA, D, gla_cols), D),
        "gla_w_gate_up": _w(ks[2], (N_GLA, GLA_GATE_RANK, GLA_HK), GLA_GATE_RANK),
        "gla_b_gate": 0.1 * jax.random.normal(ks[3], (N_GLA, GLA_HK), jnp.float32),
        "gla_norm_g": 1.0 + 0.02 * jax.random.normal(ks[4], (N_GLA, GLA_HV), jnp.float32),
        "gla_w_out": _w(ks[5], (N_GLA, GLA_HV, D), GLA_HV, DEEPNORM_BETA),
        "rpa_w_in": _w(ks[6], (N_RPA, D, 3 * D), D),
        "rpa_rel_bias": 0.5 * jax.random.normal(ks[7], (N_RPA, RPA_HEADS, 2 * RPA_MAX_REL + 1), jnp.float32),
        "rpa_w_out": _w(ks[8], (N_RPA, D, D), D, DEEPNORM_BETA),
        "mla_w_in": _w(ks[9], (N_MLA, D, mla_cols), D),
        "mla_q_norm_g": 1.0 + 0.02 * jax.random.normal(ks[10], (N_MLA, MLA_Q_RANK), jnp.float32),
        "mla_kv_norm_g": 1.0 + 0.02 * jax.random.normal(ks[11], (N_MLA, MLA_KV_RANK), jnp.float32),
        "mla_w_uq": _w(ks[12], (N_MLA, MLA_Q_RANK, MLA_HEADS * MLA_QK), MLA_Q_RANK),
        "mla_w_ukv": _w(ks[13], (N_MLA, MLA_KV_RANK, MLA_HEADS * (MLA_NOPE + MLA_V)), MLA_KV_RANK),
        "mla_w_out": _w(ks[14], (N_MLA, MLA_HEADS * MLA_V, D), MLA_HEADS * MLA_V, DEEPNORM_BETA),
        "ffn_w_in": _w(ks[15], (DEPTH, D, 2 * FFN_HIDDEN), D),
        "ffn_w_out": _w(ks[16], (DEPTH, FFN_HIDDEN, D), FFN_HIDDEN, DEEPNORM_BETA),
        "ln_g": 1.0 + 0.02 * jax.random.normal(ks[17], (DEPTH, 2, D), jnp.float32),
        "ln_b": 0.02 * jax.random.normal(ks[18], (DEPTH, 2, D), jnp.float32),
    }

def reference(x, gla_w_in, gla_w_gate_up, gla_b_gate, gla_norm_g, gla_w_out,
              rpa_w_in, rpa_rel_bias, rpa_w_out,
              mla_w_in, mla_q_norm_g, mla_kv_norm_g, mla_w_uq, mla_w_ukv, mla_w_out,
              ffn_w_in, ffn_w_out, ln_g, ln_b):
    h = x
    for i in range(DEPTH):
        m, j = i % N_MIXERS, i // N_MIXERS
        if m == 0:
            y = gla_mixer(h, gla_w_in[j], gla_w_gate_up[j], gla_b_gate[j], gla_norm_g[j], gla_w_out[j])
        elif m == 1:
            y = rpa_mixer(h, rpa_w_in[j], rpa_rel_bias[j], rpa_w_out[j])
        else:
            y = mla_mixer(h, mla_w_in[j], mla_q_norm_g[j], mla_kv_norm_g[j],
                          mla_w_uq[j], mla_w_ukv[j], mla_w_out[j])
        h = layer_norm(DEEPNORM_ALPHA * h + y, ln_g[i, 0], ln_b[i, 0])
        h = layer_norm(DEEPNORM_ALPHA * h + swiglu(h, ffn_w_in[i], ffn_w_out[i]), ln_g[i, 1], ln_b[i, 1])
    return h


_drawn_inputs = setup_inputs


def setup_inputs(seed=0):
    import zlib

    import numpy as np

    out = dict(_drawn_inputs(seed))
    spreads = {}
    factors = {'gla_b_gate': 6.384, 'gla_norm_g': 8.0, 'rpa_rel_bias': 2.886}
    for name, (base, spread) in spreads.items():
        noise = np.random.default_rng([zlib.crc32(name.encode()), seed]).standard_normal(out[name].shape)
        drawn = base * np.exp(spread * noise) if base else spread * noise
        out[name] = __import__('jax').numpy.asarray(drawn.astype(out[name].dtype))
    for name, factor in factors.items():
        out[name] = (out[name] * factor).astype(out[name].dtype)
    return out
```

```python
from contextlib import ExitStack

import numpy as np
import concourse.bass as bass
from concourse import mybir

F32 = mybir.dt.float32
F32R = mybir.dt.float32r
I32 = mybir.dt.int32
ALU = mybir.AluOpType
ACT = mybir.ActivationFunctionType
AX = mybir.AxisListType

P = 128
D_MODEL = 1024
SEQ = 512
DEPTH = 2
CHUNK = 64
ALPHA = (2 * DEPTH) ** 0.25
LN_EPS = 1e-5
NEG_INF = -1e30

KD = D_MODEL // P
TILES = SEQ // P
HALF = 512
CHUNKS = SEQ // CHUNK

GLA_HEADS = 4
GLA_DK = D_MODEL // 2 // GLA_HEADS
GLA_DV = D_MODEL // GLA_HEADS
GLA_RANK = 16
GLA_TAU = 16.0
GLA_HK = GLA_HEADS * GLA_DK
GLA_HV = GLA_HEADS * GLA_DV

RPA_HEADS = 16
RPA_D = D_MODEL // RPA_HEADS
RPA_PAIRS = RPA_HEADS // 2
RPA_MAX_REL = 128

FFN = -(-8 * D_MODEL // (3 * 256)) * 256
KF = FFN // P

SLAB = 1024
RING = 4
RAWS = 2

GLA_V = 0
GLA_R = GLA_V + KD
GLA_QK = GLA_R + KD
GLA_OUT = GLA_QK + 2 * GLA_HEADS
FFN_IN = [GLA_OUT + KD, 0]
FFN_OUT = [FFN_IN[0] + 2 * KF, 0]
RPA_V = FFN_OUT[0] + KF
RPA_QK = RPA_V + KD
RPA_OUT = RPA_QK + 2 * RPA_PAIRS
FFN_IN[1] = RPA_OUT + KD
FFN_OUT[1] = FFN_IN[1] + 2 * KF
SLABS = FFN_OUT[1] + KF
TAIL = 4


def build_program(nc, a):
    ctx = ExitStack()
    with ctx:
        place = [(nc.sbuf_base + 31) // 32 * 32]

        def sb_at(name, shape, dt, offset):
            return nc.alloc_sbuf_tensor_at("s_" + name, shape, dt, offset=offset)

        def sb(name, shape, dt=F32):
            size = 4
            for s in shape[1:]:
                size *= s
            at = place[0]
            place[0] += (size + 31) // 32 * 32
            return sb_at(name, shape, dt, at)

        def sem(name):
            return ctx.enter_context(nc.semaphore(name))

        raw = sb("raw", [P, RAWS, 2, SLAB])
        w_hi = sb("w_hi", [P, RING, SLAB], F32R)
        w_lo = sb("w_lo", [P, RING, SLAB], F32R)
        t_hi = sb("t_hi", [P, KD, SEQ], F32R)
        t_lo = sb("t_lo", [P, KD, SEQ], F32R)
        h = sb("h", [P, TILES, D_MODEL])
        ln_gb = sb("ln_gb", [P, 2, D_MODEL])
        region = place[0]
        a_hi = sb("a_hi", [P, KF, SEQ], F32R)
        a_lo = sb("a_lo", [P, KF, SEQ], F32R)
        region_end = place[0]
        gate_at = place[0]
        gate_s = sb("gate_s", [P, 2, SEQ])
        prod_at = place[0]
        prod = sb("prod", [P, 2, SEQ])
        ident = sb("ident", [P, P])
        flip = sb("flip", [P, P], F32R)
        flip_f = sb("flip_f", [P, P])
        causal = sb("causal", [P, GLA_HEADS, P])
        minus_half = sb("minus_half", [P, GLA_HEADS])
        bn = sb("bn", [P, TILES, 12])
        mv = sb("mv", [P, TILES, 2])
        var_eps = sb("var_eps", [P, TILES])
        rstd = sb("rstd", [P, TILES])
        bn_o = sb("bn_o", [P, TILES, GLA_HEADS, 6])
        mv_o = sb("mv_o", [P, TILES, GLA_HEADS, 2])
        var_eps_o = sb("var_eps_o", [P, TILES, GLA_HEADS])
        rstd_o = sb("rstd_o", [P, TILES, GLA_HEADS])
        decay = sb("decay", [P, GLA_HEADS * CHUNKS])
        b_gate = sb("b_gate", [P, GLA_HEADS])
        far_bias = sb("far_bias", [P, RPA_HEADS])
        UNITS = RPA_HEADS * TILES
        neg_max = sb("neg_max", [P, UNITS])
        row_sum = sb("row_sum", [P, UNITS])
        inv_sum = sb("inv_sum", [P, UNITS])

        def carve(start):
            at = [start]

            def get(name, shape, dt=F32):
                size = 4
                for s in shape[1:]:
                    size *= s
                t = sb_at(name, shape, dt, at[0])
                at[0] += size
                assert at[0] <= region_end, name
                return t
            return get, at

        get, at = carve(region)
        g_v = get("g_v", [P, TILES, D_MODEL])
        g_q = get("g_q", [P, GLA_HEADS, SEQ])
        g_ki = get("g_ki", [P, GLA_HEADS, SEQ])
        g_ke = get("g_ke", [P, GLA_HEADS, SEQ])
        rg_at = at[0]
        g_rg = get("g_rg", [P, TILES, D_MODEL])
        on_at = at[0]
        g_on = get("g_on", [P, TILES, D_MODEL])
        kt_at = at[0]
        g_kt = get("g_kt", [P, 2, GLA_HK])
        g_state = get("g_state", [P, 2, GLA_HEADS, GLA_DV])
        g_am = get("g_am", [P, 2, GLA_HEADS * P])
        get, _ = carve(rg_at)
        wg_hi = get("wg_hi", [P, KD, P], F32R)
        wg_lo = get("wg_lo", [P, KD, P], F32R)
        wg_raw = get("wg_raw", [P, KD, GLA_RANK])
        get, _ = carve(on_at)
        x_t = get("x_t", [P, KD, SEQ])
        get, _ = carve(on_at)
        g_e = get("g_e", [P, GLA_HEADS, SEQ])
        g_c = get("g_c", [P, GLA_HEADS, SEQ])
        get, _ = carve(kt_at)
        g_low = get("g_low", [GLA_RANK, SEQ])
        w_up = get("w_up", [GLA_RANK, GLA_HK])
        norm_g = sb_at("norm_g", [P, D_MODEL], F32, gate_at)
        keep = sb_at("keep", [P, SEQ], F32, prod_at)
        get, _ = carve(region)
        r_v = get("r_v", [P, TILES, D_MODEL])
        r_q_hi = get("r_q_hi", [P, 2, SEQ], F32R)
        r_q_lo = get("r_q_lo", [P, 2, SEQ], F32R)
        r_k_hi = get("r_k_hi", [P, 2, SEQ], F32R)
        r_k_lo = get("r_k_lo", [P, 2, SEQ], F32R)
        b_raw = get("b_raw", [P, 2, 2, 2 * P])
        b_hi = get("b_hi", [P, 2, 2, 2 * P], F32R)
        b_lo = get("b_lo", [P, 2, 2, 2 * P], F32R)
        r_p = get("r_p", [P, 3, SEQ])
        r_pt = get("r_pt", [P, 3, SEQ])
        r_o = get("r_o", [P, TILES, D_MODEL])
        assert place[0] <= nc.sbuf_usable_end, (place[0], nc.sbuf_usable_end)

        bank = [ctx.enter_context(nc.psum_tensor(f"bank{i}", [P, HALF], F32)) for i in range(8)]

        raw_full = [sem(f"raw_full{i}") for i in range(RAWS)]
        hi_done = sem("hi_done")
        lo_done = sem("lo_done")
        slab_done = sem("slab_done")
        consts = sem("consts")
        flip_done = sem("flip_done")
        x_full = [sem(f"x_full{i}") for i in range(4)]
        x_hi = sem("x_hi")
        x_lo = sem("x_lo")
        h_full = sem("h_full")
        small_full = sem("small_full")
        gb_full = sem("gb_full")
        dve_step = sem("dve_step")
        pool_step = sem("pool_step")
        act_step = sem("act_step")
        out_full = sem("out_full")
        acc_done = [sem(f"acc_done{n}") for n in range(4)]
        stats = [sem(f"stats{n}") for n in range(4)]
        rstd_done = [sem(f"rstd_done{n}") for n in range(4)]
        normed = [sem(f"normed{n}") for n in range(4)]
        turned = [sem(f"turned{n}") for n in range(5)]
        turned_hi = [sem(f"turned_hi{n}") for n in range(5)]
        turned_lo = [sem(f"turned_lo{n}") for n in range(5)]
        silu_done = [sem(f"silu_done{n}") for n in range(2)]
        prod_done = [sem(f"prod_done{n}") for n in range(2)]
        a_hi_done = [sem(f"a_hi_done{n}") for n in range(2)]
        a_lo_done = [sem(f"a_lo_done{n}") for n in range(2)]
        tok_done = [sem(f"tok_done{n}") for n in range(3)]
        tok_out = [sem(f"tok_out{n}") for n in range(3)]
        wg_ready = sem("wg_ready")
        low_done = sem("low_done")
        low_out = sem("low_out")
        up_done = sem("up_done")
        abs_done = sem("abs_done")
        min_done = sem("min_done")
        log_done = sem("log_done")
        cum_done = sem("cum_done")
        rest_done = sem("rest_done")
        exps_done = sem("exps_done")
        rg_done = sem("rg_done")
        qk_scaled = sem("qk_scaled")
        zeroed = sem("zeroed")
        ke_turned = sem("ke_turned")
        ke_out = sem("ke_out")
        sc_done = sem("sc_done")
        sc_masked = sem("sc_masked")
        upd_done = sem("upd_done")
        state_done = sem("state_done")
        intra_done = sem("intra_done")
        inter_done = sem("inter_done")
        o_stats = sem("o_stats")
        o_rstd = sem("o_rstd")
        o_out = sem("o_out")
        y_done = [sem("y_done0"), sem("y_done1")]
        far_full = sem("far_full")
        bias_full = [sem("bias_full0"), sem("bias_full1")]
        bias_sub = sem("bias_sub")
        bias_hi = sem("bias_hi")
        bias_lo = sem("bias_lo")
        rqk_hi = sem("rqk_hi")
        rqk_lo = sem("rqk_lo")
        s_done = sem("s_done")
        max_done = sem("max_done")
        exp_done = sem("exp_done")
        p_turned = sem("p_turned")
        p_out = sem("p_out")
        pv_done = sem("pv_done")
        o_scaled = sem("o_scaled")

        block = ctx.enter_context(nc.Block())

        GLA_YT, RPA_YT = 3, 4
        LN_BANKS = [(2 * t, 2 * t + 1) for t in range(TILES)]
        GLA_BANKS = [(4, 5)] * TILES

        @block.sync
        def _(sp):
            def load_pair(pair, slot):
                sp.dma_start(raw[:, slot, :, :], a["stream"][pair]).then_inc(raw_full[slot], 16)

            load_pair(0, 0)
            for i in range(4):
                sp.dma_start(x_t[:, 2 * i:2 * i + 2, :], a["x_t"][:, 2 * i:2 * i + 2, :]).then_inc(x_full[i], 16)
                if i == 0:
                    load_pair(1, 1)
            sp.dma_start(wg_raw[:, :, :], a["w_gate_down"]).then_inc(small_full, 16)
            sp.dma_start(w_up[:, :], a["w_gate_up"]).then_inc(small_full, 16)
            sp.dma_start(b_gate[:, :], a["b_gate"]).then_inc(small_full, 16)
            sp.dma_start(norm_g[:, :], a["norm_g"].partition_broadcast(P)).then_inc(small_full, 16)
            sp.dma_start(h[:, :, :], a["x"].rearrange("(t p) d -> p t d", p=P)).then_inc(h_full, 16)
            with sp.Fori(1, SLABS // (2 * RAWS)) as i:
                for slot in range(RAWS):
                    sp.wait_ge(hi_done, i * (2 * RAWS) + (2 * slot + 2 - 2 * RAWS))
                    sp.wait_ge(lo_done, i * (2 * RAWS) + (2 * slot + 2 - 2 * RAWS))
                    load_pair(i * RAWS + slot, slot)
            for t in range(TILES):
                sp.wait_ge(normed[3], t + 1)
                sp.dma_start(a["out"][t * P:(t + 1) * P, :], h[:, t, :]).then_inc(out_full, 16)
            sp.wait_ge(out_full, 16 * TILES)

        @block.scalar
        def _(act):
            def split_hi(n, i=None):
                if n >= SLABS:
                    return
                pair = n // 2
                more = 0 if i is None else i
                act.wait_ge(raw_full[pair % RAWS], more * 16 + 16 * (pair // RAWS + 1))
                if n >= RING:
                    act.wait_ge(slab_done, more * RING + (n - RING + 1))
                nc.scalar.activation(w_hi[:, n % RING, :], raw[:, pair % RAWS, n % 2, :], ACT.Copy).then_inc(hi_done, 1)

            def turned_high(which, t, banks):
                for half in range(2):
                    act.wait_ge(turned[which], 2 * t + half + 1)
                    nc.scalar.activation(
                        t_hi[:, 4 * half:4 * half + 4, t * P:(t + 1) * P],
                        bank[banks[t][half]][:, :].rearrange("p (k c) -> p k c", k=4),
                        ACT.Copy).then_inc(turned_hi[which], 1)

            def load_gb(n):
                if n > 0:
                    act.wait_ge(normed[n - 1], TILES)
                act.dma_start(ln_gb[:, :, :], a["ln_gb"][n].partition_broadcast(P)).then_inc(gb_full, 16)

            def token_major(which, n0, bank_of, copy_out):
                for half in range(2):
                    for k in range(KD // 2):
                        n = n0 + half * (KD // 2) + k
                        split_hi(n + RING)
                    for t in range(TILES):
                        if t < TILES - 1:
                            act.wait_ge(tok_done[which], half * (TILES - 1) + t + 1)
                        else:
                            act.wait_ge(slab_done, n0 + (half + 1) * (KD // 2))
                        copy_out(half, t, bank[bank_of(half, t)]).then_inc(tok_out[which], 1)

            def out_projection(n0, slabs, ln, last):
                for k in range(slabs - TAIL):
                    split_hi(n0 + k + RING)
                for t in range(TILES - 1):
                    if not last:
                        if t >= 1:
                            turned_high(ln, t - 1, LN_BANKS)
                split_hi(n0 + slabs - TAIL + RING)
                if not last:
                    turned_high(ln, TILES - 2, LN_BANKS)
                for k in range(1, TAIL):
                    split_hi(n0 + slabs - TAIL + k + RING)
                if not last:
                    turned_high(ln, TILES - 1, LN_BANKS)

            def feed_forward(f, n0):
                def body(i, first):
                    for c in range(2):
                        act.wait_ge(slab_done, i * RING + (n0 + 2 * c + 1))
                        if not first:
                            act.wait_ge(prod_done[f], i * 2 + (c - 1))
                        nc.scalar.activation(gate_s[:, c, :], bank[c][:, :], ACT.Silu).then_inc(silu_done[f], 1)
                        split_hi(n0 + 2 * c + RING, i)
                        split_hi(n0 + 2 * c + 1 + RING, i)
                        act.wait_ge(prod_done[f], i * 2 + (c + 1))
                        nc.scalar.activation(a_hi[:, bass.ds(i * 2 + c, 1), :], prod[:, bass.ds(c, 1), :],
                                             ACT.Copy).then_inc(a_hi_done[f], 1)
                body(0, True)
                with act.Fori(1, KF // 2) as i:
                    body(i, False)

            load_gb(0)
            for i in range(4):
                act.wait_ge(x_full[i], 16)
                nc.scalar.activation(t_hi[:, 2 * i:2 * i + 2, :], x_t[:, 2 * i:2 * i + 2, :], ACT.Copy).then_inc(x_hi, 1)
                split_hi(i)
            act.wait_ge(consts, 8)
            nc.scalar.activation(flip[:, :], flip_f[:, :], ACT.Copy).then_inc(flip_done, 1)
            act.wait_ge(small_full, 64)
            act.wait_ge(zeroed, 2)
            nc.scalar.activation(wg_hi[:, :, 0:GLA_RANK], wg_raw[:, :, :], ACT.Copy).then_inc(wg_ready, 1)

            token_major(0, GLA_V, lambda half, t: 4 * half + t, lambda half, t, b: nc.scalar.activation(
                g_v[:, t, half * HALF:(half + 1) * HALF], b[:, :], ACT.Copy))
            act.wait_ge(low_done, 1)
            nc.scalar.activation(g_low[:, :], bank[0][0:GLA_RANK, :], ACT.Copy).then_inc(low_out, 1)
            for hd in range(GLA_HEADS):
                act.wait_ge(up_done, hd + 1)
                nc.scalar.activation(g_e[:, hd, :], bank[hd][:, :], ACT.Abs, bias=b_gate[:, hd:hd + 1]).then_inc(abs_done, 1)
            act.wait_ge(abs_done, GLA_HEADS)
            nc.scalar.activation(g_e[:, :, :], g_e[:, :, :], ACT.Exp, scale=-1.0).then_inc(act_step, 1)
            act.wait_ge(act_step, 1)
            nc.scalar.activation(g_e[:, :, :], g_e[:, :, :], ACT.Ln, bias=1.0).then_inc(log_done, 1)
            split_hi(GLA_R + RING)
            act.wait_ge(cum_done, GLA_HEADS)
            nc.scalar.activation(g_q[:, :, :], g_c[:, :, :], ACT.Exp, scale=1.0 / GLA_TAU).then_inc(exps_done, 1)
            split_hi(GLA_R + 1 + RING)
            nc.scalar.activation(g_ki[:, :, :], g_c[:, :, :], ACT.Exp, scale=-1.0 / GLA_TAU).then_inc(exps_done, 1)
            chunk_ends = g_c[:, :, :].rearrange("p h (c i) -> p (h c) i", i=CHUNK)[:, :, CHUNK - 1]
            nc.scalar.activation(decay[:, :], chunk_ends, ACT.Exp, scale=1.0 / GLA_TAU).then_inc(exps_done, 1)
            act.wait_ge(rest_done, 1)
            nc.scalar.activation(g_ke[:, :, :], g_e[:, :, :], ACT.Exp, scale=1.0 / GLA_TAU).then_inc(exps_done, 1)
            for half in range(2):
                for k in range(KD // 2):
                    n = GLA_R + half * (KD // 2) + k
                    if n >= GLA_R + 2:
                        split_hi(n + RING)
                for t in range(TILES):
                    if t < TILES - 1:
                        act.wait_ge(tok_done[1], half * (TILES - 1) + t + 1)
                    else:
                        act.wait_ge(slab_done, GLA_R + (half + 1) * (KD // 2))
                    nc.scalar.activation(g_rg[:, t, half * HALF:(half + 1) * HALF],
                                         bank[4 - 4 * half + t][:, :], ACT.Silu).then_inc(tok_out[1], 1)
            for n in range(GLA_QK, GLA_OUT):
                split_hi(n + RING)
            def ke_tile_out(t):
                act.wait_ge(ke_turned, t + 1)
                if t >= 2:
                    act.wait_ge(upd_done, 2 * (t - 2) + 2)
                nc.scalar.activation(g_kt[:, t % 2, :], bank[5][:, :], ACT.Copy).then_inc(ke_out, 1)
            ke_tile_out(0)
            for t in range(TILES):
                if t + 1 < TILES:
                    ke_tile_out(t + 1)
                if t >= 1:
                    turned_high(GLA_YT, t - 1, GLA_BANKS)
            turned_high(GLA_YT, TILES - 1, GLA_BANKS)
            out_projection(GLA_OUT, KD, 0, False)
            load_gb(1)
            feed_forward(0, FFN_IN[0])
            out_projection(FFN_OUT[0], KF, 1, False)
            load_gb(2)

            def load_bias(p):
                if p >= 2:
                    act.wait_ge(bias_hi, p - 1)
                    act.wait_ge(bias_lo, p - 1)
                for hd in range(2):
                    tab = a["rel_bias"]
                    start = (2 * p + hd) * 3 * P + 1
                    act.dma_start(b_raw[:, p % 2, hd, :], bass.AP(tab.tensor, start, [[1, P], [1, 2 * P]])).then_inc(
                        bias_full[p % 2], 16)

            def bias_high(p):
                act.wait_ge(bias_sub, p + 1)
                if p >= 2:
                    act.wait_ge(s_done, 2 * TILES * (p - 1))
                nc.scalar.activation(b_hi[:, p % 2, :, :], b_raw[:, p % 2, :, :], ACT.Copy).then_inc(bias_hi, 1)

            def rpa_high(p, is_k):
                n = RPA_QK + 2 * p + is_k
                act.wait_ge(slab_done, n + 1)
                if p >= 2:
                    act.wait_ge(s_done, 2 * TILES * (p - 1))
                if is_k:
                    nc.scalar.activation(r_k_hi[:, p % 2, :], bank[1][:, :], ACT.Copy).then_inc(rqk_hi, 1)
                else:
                    nc.scalar.activation(r_q_hi[:, p % 2, :], bank[0][:, :], ACT.Copy, scale=RPA_D ** -0.5).then_inc(rqk_hi, 1)
                split_hi(n + RING)

            act.dma_start(far_bias[:, :], a["far_bias"].partition_broadcast(P)).then_inc(far_full, 16)
            load_bias(0)
            load_bias(1)
            token_major(2, RPA_V, lambda half, t: 4 * half + t, lambda half, t, b: nc.scalar.activation(
                r_v[:, t, half * HALF:(half + 1) * HALF], b[:, :], ACT.Copy))
            bias_high(0)
            rpa_high(0, 0)
            rpa_high(0, 1)
            for s in range(UNITS):
                p, step, t = s // (2 * TILES), s % (2 * TILES), s % TILES
                act.wait_ge(max_done, s + 1)
                if s >= 3:
                    act.wait_ge(p_turned, s - 2)
                nc.scalar.activation(r_p[:, s % 3, 0:(t + 1) * P], bank[2 + s % 2][:, 0:(t + 1) * P], ACT.Exp,
                                     bias=neg_max[:, s:s + 1], accum_out=row_sum[:, s:s + 1]).then_inc(exp_done, 1)
                if p + 1 < RPA_PAIRS:
                    if step == 1:
                        bias_high(p + 1)
                    if step == 3:
                        rpa_high(p + 1, 0)
                        if p + 2 < RPA_PAIRS:
                            load_bias(p + 2)
                    if step == 6:
                        rpa_high(p + 1, 1)
            for t in range(TILES):
                turned_high(RPA_YT, t, LN_BANKS)
            out_projection(RPA_OUT, KD, 2, False)
            load_gb(3)
            feed_forward(1, FFN_IN[1])
            out_projection(FFN_OUT[1], KF, 3, True)

        @block.gpsimd
        def _(pool):
            steps = [0]

            def own(ins):
                steps[0] += 1
                ins.then_inc(pool_step, 1)
                pool.wait_ge(pool_step, steps[0])

            def split_lo(n, i=None):
                if n >= SLABS:
                    return
                more = 0 if i is None else i
                pair = n // 2
                pool.wait_ge(hi_done, more * RING + (n + 1))
                nc.gpsimd.tensor_tensor(w_lo[:, n % RING, :], raw[:, pair % RAWS, n % 2, :],
                                        w_hi[:, n % RING, :].bitcast(F32), ALU.subtract).then_inc(lo_done, 1)

            def ln_rstd(ln, t):
                pool.wait_ge(stats[ln], t + 1)
                own(nc.gpsimd.tensor_scalar(var_eps[:, t:t + 1], mv[:, t, 1:2], LN_EPS, None, ALU.add))
                nc.gpsimd.tensor_tensor(rstd[:, t:t + 1], var_eps[:, t:t + 1], minus_half[:, 0:1], ALU.pow).then_inc(rstd_done[ln], 1)

            def out_projection(n0, slabs, ln):
                for k in range(slabs - TAIL):
                    split_lo(n0 + k + RING)
                for t in range(TILES - 1):
                    ln_rstd(ln, t)
                split_lo(n0 + slabs - TAIL + RING)
                ln_rstd(ln, TILES - 1)
                for k in range(1, TAIL):
                    split_lo(n0 + slabs - TAIL + k + RING)

            def feed_forward(n0):
                with pool.Fori(0, KF // 2) as i:
                    for c in range(RING):
                        split_lo(n0 + c + RING, i)

            nc.gpsimd.memset(ident[:, :], 0.0).then_inc(consts, 1)
            nc.gpsimd.memset(flip_f[:, :], 0.0).then_inc(consts, 1)
            nc.gpsimd.memset(causal[:, :, :], 1.0).then_inc(consts, 1)
            nc.gpsimd.memset(minus_half[:, :], -0.5).then_inc(consts, 1)
            nc.gpsimd.memset(keep[:, :], 1.0).then_inc(consts, 1)
            pool.wait_ge(consts, 5)
            nc.gpsimd.affine_select(out=ident[:, :], in_=ident[:, :], compare_op=ALU.not_equal, fill=1.0, base=0,
                                    pattern=[[-1, P]], channel_multiplier=1).then_inc(consts, 1)
            nc.gpsimd.affine_select(out=causal[:, :, :], in_=causal[:, :, :], compare_op=ALU.is_ge, fill=0.0, base=0,
                                    pattern=[[0, GLA_HEADS], [1, P]], channel_multiplier=-1).then_inc(consts, 1)
            nc.gpsimd.affine_select(out=flip_f[:, :], in_=flip_f[:, :], compare_op=ALU.not_equal, fill=1.0,
                                    base=-(P - 1), pattern=[[1, P]], channel_multiplier=1).then_inc(consts, 1)
            pool.wait_ge(consts, 8)
            nc.gpsimd.memset(causal[0:CHUNK, :, CHUNK:P], 0.0).then_inc(consts, 1)
            nc.gpsimd.memset(keep[:, :].rearrange("p (c i) -> p c i", i=CHUNK)[:, :, 0:1], 0.0).then_inc(consts, 1)
            for n in range(RING):
                split_lo(n)
            for n in range(GLA_V, GLA_R):
                split_lo(n + RING)
            for half in range(2):
                for k in range(KD // 2):
                    split_lo(GLA_R + half * (KD // 2) + k + RING)
                for t in range(TILES):
                    cols = slice(half * HALF, (half + 1) * HALF)
                    pool.wait_ge(tok_out[1], half * TILES + t + 1)
                    nc.gpsimd.tensor_tensor(g_rg[:, t, cols], g_rg[:, t, cols], norm_g[:, cols], ALU.mult).then_inc(rg_done, 1)
            for n in range(GLA_QK, GLA_OUT):
                split_lo(n + RING)
            for t in range(TILES):
                pool.wait_ge(o_stats, t + 1)
                own(nc.gpsimd.tensor_scalar(var_eps_o[:, t, :], mv_o[:, t, :, 1], LN_EPS, None, ALU.add))
                nc.gpsimd.tensor_tensor(rstd_o[:, t, :], var_eps_o[:, t, :], minus_half[:, :], ALU.pow).then_inc(o_rstd, 1)
            out_projection(GLA_OUT, KD, 0)
            feed_forward(FFN_IN[0])
            out_projection(FFN_OUT[0], KF, 1)
            for n in range(RPA_V, RPA_OUT):
                split_lo(n + RING)
            out_projection(RPA_OUT, KD, 2)
            feed_forward(FFN_IN[1])
            out_projection(FFN_OUT[1], KF, 3)

        @block.vector
        def _(dve):
            steps = [0]

            def own(ins):
                steps[0] += 1
                ins.then_inc(dve_step, 1)
                dve.wait_ge(dve_step, steps[0])

            def turned_low(which, t, banks):
                for half in range(2):
                    dve.wait_ge(turned_hi[which], 2 * t + half + 1)
                    nc.vector.tensor_tensor(
                        t_lo[:, 4 * half:4 * half + 4, t * P:(t + 1) * P],
                        bank[banks[t][half]][:, :].rearrange("p (k c) -> p k c", k=4),
                        t_hi[:, 4 * half:4 * half + 4, t * P:(t + 1) * P].bitcast(F32),
                        ALU.subtract).then_inc(turned_lo[which], 1)

            def layer_norm(ln, n_end, last):
                for t in range(TILES):
                    if t < TILES - 1:
                        dve.wait_ge(acc_done[ln], t + 1)
                    else:
                        dve.wait_ge(slab_done, n_end)
                    if ln == 0 and t == 0:
                        dve.wait_ge(h_full, 16)
                    for half in range(2):
                        cols = slice(half * HALF, (half + 1) * HALF)
                        own(nc.vector.scalar_tensor_tensor(out=h[:, t, cols], in0=h[:, t, cols], scalar=ALPHA,
                                                           in1=bank[2 * t + half][:, :], op0=ALU.mult, op1=ALU.add))
                        own(nc.vector.bn_stats(bn[:, t, 6 * half:6 * half + 6], h[:, t, cols]))
                    nc.vector.bn_aggr(mv[:, t, :], bn[:, t, :]).then_inc(stats[ln], 1)
                    if t >= 1 and not last:
                        turned_low(ln, t - 1, LN_BANKS)
                    if t == 0:
                        dve.wait_ge(gb_full, 16 * (ln + 1))
                    dve.wait_ge(rstd_done[ln], t + 1)
                    own(nc.vector.tensor_scalar(h[:, t, :], h[:, t, :], mv[:, t, 0:1], rstd[:, t:t + 1], ALU.subtract, ALU.mult))
                    own(nc.vector.tensor_tensor(h[:, t, :], h[:, t, :], ln_gb[:, 0, :], ALU.mult))
                    nc.vector.tensor_tensor(h[:, t, :], h[:, t, :], ln_gb[:, 1, :], ALU.add).then_inc(normed[ln], 1)
                if not last:
                    turned_low(ln, TILES - 1, LN_BANKS)

            def feed_forward(f, n0):
                def body(i):
                    for c in range(2):
                        dve.wait_ge(slab_done, i * RING + (n0 + 2 * c + 2))
                        dve.wait_ge(silu_done[f], i * 2 + (c + 1))
                        nc.vector.tensor_tensor(prod[:, c, :], gate_s[:, c, :], bank[2 + c][:, :], ALU.mult).then_inc(prod_done[f], 1)
                        dve.wait_ge(a_hi_done[f], i * 2 + (c + 1))
                        nc.vector.tensor_tensor(a_lo[:, bass.ds(i * 2 + c, 1), :], prod[:, bass.ds(c, 1), :],
                                                a_hi[:, bass.ds(i * 2 + c, 1), :].bitcast(F32), ALU.subtract).then_inc(a_lo_done[f], 1)
                body(0)
                with dve.Fori(1, KF // 2) as i:
                    body(i)

            nc.vector.memset(wg_hi[:, :, :].bitcast(F32), 0.0).then_inc(zeroed, 1)
            nc.vector.memset(wg_lo[:, :, :].bitcast(F32), 0.0).then_inc(zeroed, 1)
            nc.vector.memset(g_am[:, :, :], 0.0).then_inc(zeroed, 1)
            for i in range(4):
                dve.wait_ge(x_hi, i + 1)
                nc.vector.tensor_tensor(t_lo[:, 2 * i:2 * i + 2, :], x_t[:, 2 * i:2 * i + 2, :],
                                        t_hi[:, 2 * i:2 * i + 2, :].bitcast(F32), ALU.subtract).then_inc(x_lo, 1)
            dve.wait_ge(wg_ready, 1)
            dve.wait_ge(zeroed, 2)
            nc.vector.tensor_tensor(wg_lo[:, :, 0:GLA_RANK], wg_raw[:, :, :], wg_hi[:, :, 0:GLA_RANK].bitcast(F32),
                                    ALU.subtract).then_inc(wg_ready, 1)
            for hd in range(GLA_HEADS):
                dve.wait_ge(abs_done, hd + 1)
                if hd == 0:
                    dve.wait_ge(x_lo, 4)
                nc.vector.tensor_scalar(g_c[:, hd, :], bank[hd][:, :], b_gate[:, hd:hd + 1], 0.0, ALU.add, ALU.min).then_inc(min_done, 1)
            dve.wait_ge(min_done, GLA_HEADS)
            dve.wait_ge(log_done, 1)
            own(nc.vector.tensor_tensor(g_c[:, :, :], g_c[:, :, :], g_e[:, :, :], ALU.subtract))
            dve.wait_ge(consts, 10)
            for hd in range(GLA_HEADS):
                nc.vector.tensor_tensor_scan(g_c[:, hd, :], keep[:, :], g_c[:, hd, :], 0.0, ALU.mult, ALU.add).then_inc(cum_done, 1)
            dve.wait_ge(cum_done, GLA_HEADS)
            cum = g_c[:, :, :].rearrange("p h (c i) -> p (h c) i", i=CHUNK)
            nc.vector.tensor_tensor(g_e[:, :, :].rearrange("p h (c i) -> p (h c) i", i=CHUNK),
                                    cum[:, :, CHUNK - 1:CHUNK].to_broadcast([P, GLA_HEADS * CHUNKS, CHUNK]), cum,
                                    ALU.subtract).then_inc(rest_done, 1)
            dve.wait_ge(exps_done, 4)
            for hd in range(GLA_HEADS):
                b_q, b_k = bank[4 + 2 * (hd % 2)], bank[5 + 2 * (hd % 2)]
                dve.wait_ge(slab_done, GLA_QK + 2 * hd + 1)
                nc.vector.scalar_tensor_tensor(out=g_q[:, hd, :], in0=b_q[:, :], scalar=GLA_DK ** -0.5, in1=g_q[:, hd, :],
                                               op0=ALU.mult, op1=ALU.mult).then_inc(qk_scaled, 1)
                dve.wait_ge(slab_done, GLA_QK + 2 * hd + 2)
                nc.vector.tensor_tensor(g_ki[:, hd, :], b_k[:, :], g_ki[:, hd, :], ALU.mult).then_inc(qk_scaled, 1)
                nc.vector.tensor_tensor(g_ke[:, hd, :], b_k[:, :], g_ke[:, hd, :], ALU.mult).then_inc(qk_scaled, 1)

            def mask_scores(t):
                dve.wait_ge(sc_done, t + 1)
                if t >= 2:
                    dve.wait_ge(intra_done, t - 1)
                nc.vector.copy_predicated(g_am[:, t % 2, :], causal[:, :, :].rearrange("p h i -> p (h i)").bitcast(I32),
                                          bank[4][:, :]).then_inc(sc_masked, 1)

            def update_state(c):
                if c == CHUNKS - 1:
                    return
                dve.wait_ge(upd_done, c + 1)
                if c >= 2:
                    dve.wait_ge(inter_done, c - 1)
                if c >= 1:
                    dve.wait_ge(state_done, c)
                banks = (6, 7) if c % 2 == 0 else (2, 3)
                for hd in range(GLA_HEADS):
                    new = g_state[:, (c + 1) % 2, hd, :]
                    upd = bank[banks[hd // 2]][:, (hd % 2) * GLA_DV:(hd % 2 + 1) * GLA_DV]
                    if c == 0:
                        last = nc.vector.tensor_copy(new, upd)
                    else:
                        last = nc.vector.scalar_tensor_tensor(
                            out=new, in0=g_state[:, c % 2, hd, :], scalar=decay[:, hd * CHUNKS + c:hd * CHUNKS + c + 1],
                            in1=upd, op0=ALU.mult, op1=ALU.add)
                last.then_inc(state_done, 1)

            dve.wait_ge(zeroed, 3)
            dve.wait_ge(consts, 10)
            mask_scores(0)
            for t in range(TILES):
                update_state(2 * t)
                if t + 1 < TILES:
                    mask_scores(t + 1)
                dve.wait_ge(inter_done, 2 * t + 1)
                for hd in range(GLA_HEADS):
                    o = bank[hd // 2][:, (hd % 2) * GLA_DV:(hd % 2 + 1) * GLA_DV]
                    last = nc.vector.bn_stats(bn_o[:, t, hd, :], o)
                own(last)
                for hd in range(GLA_HEADS):
                    last = nc.vector.bn_aggr(mv_o[:, t, hd, :], bn_o[:, t, hd, :])
                last.then_inc(o_stats, 1)
                if t < TILES - 1:
                    update_state(2 * t + 1)
                dve.wait_ge(o_rstd, t + 1)
                for hd in range(GLA_HEADS):
                    o = bank[hd // 2][:, (hd % 2) * GLA_DV:(hd % 2 + 1) * GLA_DV]
                    last = nc.vector.tensor_scalar(g_on[:, t, hd * GLA_DV:(hd + 1) * GLA_DV], o, mv_o[:, t, hd, 0:1],
                                                   rstd_o[:, t, hd:hd + 1], ALU.subtract, ALU.mult)
                last.then_inc(o_out, 1)
                dve.wait_ge(o_out, t + 1)
                if t == 0:
                    dve.wait_ge(rg_done, 2 * TILES)
                nc.vector.tensor_tensor(g_on[:, t, :], g_on[:, t, :], g_rg[:, t, :], ALU.mult).then_inc(y_done[0], 1)
                if t >= 1:
                    turned_low(GLA_YT, t - 1, GLA_BANKS)
            turned_low(GLA_YT, TILES - 1, GLA_BANKS)
            layer_norm(0, FFN_IN[0], False)
            feed_forward(0, FFN_IN[0])
            layer_norm(1, RPA_V, False)

            def bias_relative(p):
                dve.wait_ge(bias_full[p % 2], 32 * (p // 2 + 1))
                for hd in range(2):
                    own(nc.vector.tensor_scalar(b_raw[:, p % 2, hd, :], b_raw[:, p % 2, hd, :],
                                                far_bias[:, 2 * p + hd:2 * p + hd + 1], None, ALU.subtract))
                nc.vector.memset(b_raw[0:CHUNK, p % 2, :, 0:CHUNK], NEG_INF).then_inc(bias_sub, 1)

            def bias_low(p):
                dve.wait_ge(bias_hi, p + 1)
                nc.vector.tensor_tensor(b_lo[:, p % 2, :, :], b_raw[:, p % 2, :, :], b_hi[:, p % 2, :, :].bitcast(F32),
                                        ALU.subtract).then_inc(bias_lo, 1)

            def rpa_low(p, is_k):
                dve.wait_ge(rqk_hi, 2 * p + is_k + 1)
                if is_k:
                    ins = nc.vector.tensor_tensor(r_k_lo[:, p % 2, :], bank[1][:, :], r_k_hi[:, p % 2, :].bitcast(F32), ALU.subtract)
                else:
                    ins = nc.vector.scalar_tensor_tensor(out=r_q_lo[:, p % 2, :], in0=bank[0][:, :], scalar=RPA_D ** -0.5,
                                                         in1=r_q_hi[:, p % 2, :].bitcast(F32), op0=ALU.mult, op1=ALU.subtract)
                ins.then_inc(rqk_lo, 1)

            def weights_out(s):
                t = s % TILES
                dve.wait_ge(p_turned, s + 1)
                if s >= 3:
                    dve.wait_ge(pv_done, s - 2)
                nc.vector.tensor_copy(r_pt[:, s % 3, 0:(t + 1) * P], bank[4 + s % 2][:, 0:(t + 1) * P]).then_inc(p_out, 1)

            def scale_o(s):
                hd, t = s // TILES, s % TILES
                own(nc.vector.reciprocal(inv_sum[:, s:s + 1], row_sum[:, s:s + 1]))
                dve.wait_ge(pv_done, s + 1)
                nc.vector.tensor_scalar(r_o[:, t, hd * RPA_D:(hd + 1) * RPA_D], bank[6 + s % 2][:, 0:RPA_D],
                                        inv_sum[:, s:s + 1], None, ALU.mult).then_inc(o_scaled, 1)

            dve.wait_ge(far_full, 16)
            bias_relative(0)
            bias_low(0)
            rpa_low(0, 0)
            rpa_low(0, 1)
            for s in range(UNITS + 2):
                if s < UNITS:
                    p, step, t = s // (2 * TILES), s % (2 * TILES), s % TILES
                    dve.wait_ge(s_done, s + 1)
                    nc.vector.tensor_reduce(neg_max[:, s:s + 1], bank[2 + s % 2][:, 0:(t + 1) * P], AX.X, ALU.max,
                                            negate=True).then_inc(max_done, 1)
                    if p + 1 < RPA_PAIRS:
                        if step == 0:
                            bias_relative(p + 1)
                        if step == 2:
                            bias_low(p + 1)
                        if step == 4:
                            rpa_low(p + 1, 0)
                        if step == 7:
                            rpa_low(p + 1, 1)
                if 1 <= s <= UNITS:
                    weights_out(s - 1)
                if s >= 2:
                    scale_o(s - 2)
            for t in range(TILES):
                turned_low(RPA_YT, t, LN_BANKS)
            layer_norm(2, FFN_IN[1], False)
            feed_forward(1, FFN_IN[1])
            layer_norm(3, SLABS, True)

        @block.tensor
        def _(pe):
            def three(out, l_hi, l_lo, r_hi, r_lo, start, stop, skip=False):
                nc.tensor.matmul(out, l_hi, r_hi, start=start, stop=False, skip_group_check=skip)
                nc.tensor.matmul(out, l_hi, r_lo, start=False, stop=False, skip_group_check=skip)
                return nc.tensor.matmul(out, l_lo, r_hi, start=False, stop=stop, skip_group_check=skip)

            def columns_piece(n, b, ks, slot=None):
                s = n % RING
                for k in ks:
                    cols = slice(k * P, (k + 1) * P)
                    last = three(bank[b][:, :], w_hi[:, s, cols], w_lo[:, s, cols], t_hi[:, k, :], t_lo[:, k, :],
                                 k == 0, k == KD - 1)
                return last

            def token_major(which, n0, bank_of, free=None):
                for half in range(2):
                    for kk in range(KD // 2):
                        n = n0 + half * (KD // 2) + kk
                        pe.wait_ge(lo_done, n + 1)
                        for t in range(TILES):
                            if kk == 0 and free is not None:
                                free(half, t)
                            for j in range(2):
                                k = 2 * kk + j
                                if which == 0 and half == 0 and t == 0 and j == 0:
                                    pe.wait_ge(x_lo, kk + 1)
                                toks = slice(t * P, (t + 1) * P)
                                cols = slice(j * HALF, (j + 1) * HALF)
                                last = three(bank[bank_of(half, t)][:, :], t_hi[:, k, toks], t_lo[:, k, toks],
                                             w_hi[:, n % RING, cols], w_lo[:, n % RING, cols], k == 0, k == KD - 1)
                            if kk == KD // 2 - 1 and t < TILES - 1:
                                last.then_inc(tok_done[which], 1)
                        last.then_inc(slab_done, 1)

            def turn(which, t, src, banks):
                for half in range(2):
                    for k in range(4):
                        last = nc.tensor.transpose(bank[banks[t][half]][:, k * P:(k + 1) * P],
                                                   src[:, t, (4 * half + k) * P:(4 * half + k + 1) * P], ident[:, :])
                    last.then_inc(turned[which], 1)

            def out_projection(n0, slabs, l_hi, l_lo, ln, ready, free, last_ln):
                def part(k, t):
                    toks = slice(t * P, (t + 1) * P)
                    s = (n0 + k) % RING
                    for half in range(2):
                        cols = slice(half * HALF, (half + 1) * HALF)
                        last = three(bank[2 * t + half][:, :], l_hi[:, k, toks], l_lo[:, k, toks],
                                     w_hi[:, s, cols], w_lo[:, s, cols], k == 0, k == slabs - 1)
                    return last

                for k in range(slabs - TAIL):
                    pe.wait_ge(lo_done, n0 + k + 1)
                    ready(k)
                    for t in range(TILES):
                        if k == 0:
                            free(t)
                        last = part(k, t)
                    last.then_inc(slab_done, 1)
                for t in range(TILES):
                    for k in range(slabs - TAIL, slabs):
                        if t == 0:
                            pe.wait_ge(lo_done, n0 + k + 1)
                            ready(k)
                        last = part(k, t)
                        if t == TILES - 1:
                            last.then_inc(slab_done, 1)
                    if t < TILES - 1:
                        last.then_inc(acc_done[ln], 1)
                    if t >= 1 and not last_ln:
                        pe.wait_ge(normed[ln], t)
                        turn(ln, t - 1, h, LN_BANKS)
                if not last_ln:
                    pe.wait_ge(normed[ln], TILES)
                    turn(ln, TILES - 1, h, LN_BANKS)

            def feed_forward(f, n0, ln):
                def body(i, first):
                    for c in range(RING):
                        j, up = c // 2, c % 2
                        pe.wait_ge(lo_done, i * RING + (n0 + c + 1))
                        if not first:
                            pe.wait_ge((prod_done if up else silu_done)[f], i * 2 + (j - 1))
                        columns_piece(n0 + c, 2 * up + j, range(KD)).then_inc(slab_done, 1)
                pe.wait_ge(turned_lo[ln], 2 * TILES)
                body(0, True)
                with pe.Fori(1, KF // 2) as i:
                    body(i, False)

            token_major(0, GLA_V, lambda half, t: 4 * half + t)
            pe.wait_ge(wg_ready, 2)
            pe.wait_ge(tok_out[0], 1)
            for k in range(KD):
                last = three(bank[0][:, :], wg_hi[:, k, :], wg_lo[:, k, :], t_hi[:, k, :], t_lo[:, k, :], k == 0, k == KD - 1)
            last.then_inc(low_done, 1)
            pe.wait_ge(low_out, 1)
            pe.wait_ge(small_full, 64)
            pe.wait_ge(tok_out[0], TILES)
            for hd in range(GLA_HEADS):
                nc.tensor.matmul(bank[hd][:, :], w_up[:, hd * GLA_DK:(hd + 1) * GLA_DK], g_low[:, :],
                                 start=True, stop=True).then_inc(up_done, 1)

            def r_free(half, t):
                if half == 0:
                    pe.wait_ge(tok_out[0], TILES + t + 1)
                else:
                    pe.wait_ge(abs_done, t + 1)
                    pe.wait_ge(min_done, t + 1)
            token_major(1, GLA_R, lambda half, t: 4 - 4 * half + t, r_free)
            for hd in range(GLA_HEADS):
                for is_k in range(2):
                    n = GLA_QK + 2 * hd + is_k
                    pe.wait_ge(lo_done, n + 1)
                    if hd < 2:
                        pe.wait_ge(tok_out[1], 2 * hd + is_k + 1)
                    else:
                        pe.wait_ge(qk_scaled, 3 * (hd - 2) + 1 + 2 * is_k)
                    columns_piece(n, 4 + 2 * (hd % 2) + is_k, range(KD)).then_inc(slab_done, 1)

            def ke_and_scores(t):
                toks = slice(t * P, (t + 1) * P)
                for hd in range(GLA_HEADS):
                    last = nc.tensor.transpose(bank[5][:, hd * P:(hd + 1) * P], g_ke[:, hd, toks], ident[:, :])
                last.then_inc(ke_turned, 1)
                for hd in range(GLA_HEADS):
                    last = nc.tensor.matmul(bank[4][:, hd * P:(hd + 1) * P], g_ki[:, hd, toks], g_q[:, hd, toks],
                                            start=True, stop=True)
                last.then_inc(sc_done, 1)

            def updates(c):
                t, rows = c // 2, slice((c % 2) * CHUNK, (c % 2 + 1) * CHUNK)
                banks = (6, 7) if c % 2 == 0 else (2, 3)
                for hd in range(GLA_HEADS):
                    last = nc.tensor.matmul(bank[banks[hd // 2]][:, (hd % 2) * GLA_DV:(hd % 2 + 1) * GLA_DV],
                                            g_kt[rows, t % 2, hd * GLA_DK:(hd + 1) * GLA_DK],
                                            g_v[rows, t, hd * GLA_DV:(hd + 1) * GLA_DV], start=True, stop=True)
                last.then_inc(upd_done, 1)

            def inter(c):
                rows = slice((c % 2) * CHUNK, (c % 2 + 1) * CHUNK)
                for hd in range(GLA_HEADS):
                    last = nc.tensor.matmul(bank[hd // 2][rows, (hd % 2) * GLA_DV:(hd % 2 + 1) * GLA_DV],
                                            g_q[:, hd, c * CHUNK:(c + 1) * CHUNK], g_state[:, c % 2, hd, :],
                                            start=False, stop=True, skip_group_check=True)
                last.then_inc(inter_done, 1)

            pe.wait_ge(consts, 10)
            pe.wait_ge(qk_scaled, 3 * GLA_HEADS)
            pe.wait_ge(tok_out[0], 2 * TILES)
            ke_and_scores(0)
            pe.wait_ge(tok_out[1], 2 * TILES)
            for t in range(TILES):
                pe.wait_ge(ke_out, t + 1)
                if t >= 1:
                    pe.wait_ge(state_done, 2 * t - 1)
                updates(2 * t)
                if t + 1 < TILES:
                    pe.wait_ge(sc_masked, t + 1)
                    if t >= 2:
                        pe.wait_ge(turned_lo[GLA_YT], 2 * (t - 1))
                    ke_and_scores(t + 1)
                pe.wait_ge(sc_masked, t + 1)
                if t >= 1:
                    pe.wait_ge(o_out, t)
                for hd in range(GLA_HEADS):
                    last = nc.tensor.matmul(bank[hd // 2][:, (hd % 2) * GLA_DV:(hd % 2 + 1) * GLA_DV],
                                            g_am[:, t % 2, hd * P:(hd + 1) * P], g_v[:, t, hd * GLA_DV:(hd + 1) * GLA_DV],
                                            start=(hd % 2 == 0), stop=False, skip_group_check=True)
                last.then_inc(intra_done, 1)
                if t >= 1:
                    pe.wait_ge(state_done, 2 * t)
                    inter(2 * t)
                pe.wait_ge(state_done, 2 * t + 1)
                inter(2 * t + 1)
                if t + 1 < TILES:
                    updates(2 * t + 1)
                if t >= 1:
                    pe.wait_ge(y_done[0], t)
                    pe.wait_ge(ke_out, min(t + 2, TILES))
                    pe.wait_ge(sc_masked, min(t + 2, TILES))
                    turn(GLA_YT, t - 1, g_on, GLA_BANKS)
            pe.wait_ge(y_done[0], TILES)
            pe.wait_ge(turned_lo[GLA_YT], 2 * (TILES - 1))
            turn(GLA_YT, TILES - 1, g_on, GLA_BANKS)

            def gla_out_free(t):
                if t == 0:
                    pe.wait_ge(o_out, TILES)
                    pe.wait_ge(state_done, CHUNKS - 1)
                    pe.wait_ge(turned_lo[GLA_YT], 2 * TILES)
            out_projection(GLA_OUT, KD, t_hi, t_lo, 0, lambda k: None, gla_out_free, False)
            feed_forward(0, FFN_IN[0], 0)

            def ffn_out(f, ln):
                def hidden_ready(k):
                    pe.wait_ge(a_lo_done[f], k + 1)

                def banks_free(t):
                    if t == 0:
                        pe.wait_ge(prod_done[f], KF)
                out_projection(FFN_OUT[f], KF, a_hi, a_lo, ln, hidden_ready, banks_free, ln == 3)
            ffn_out(0, 1)

            pe.wait_ge(turned_lo[1], 2 * TILES)
            token_major(2, RPA_V, lambda half, t: 4 * half + t)

            def qk_pieces(p):
                for is_k in range(2):
                    n = RPA_QK + 2 * p + is_k
                    for k in range(KD):
                        yield n, is_k, k, p

            def qk_piece(n, is_k, k, p):
                if k == 0:
                    pe.wait_ge(lo_done, n + 1)
                    if p >= 1:
                        pe.wait_ge(rqk_lo, 2 * (p - 1) + is_k + 1)
                    else:
                        pe.wait_ge(tok_out[2], is_k + 1)
                last = columns_piece(n, is_k, [k])
                if k == KD - 1:
                    last.then_inc(slab_done, 1)

            def scores(s):
                p, hd, t = s // (2 * TILES), s // TILES % 2, s % TILES
                rows = slice(hd * RPA_D, (hd + 1) * RPA_D)
                toks = slice(t * P, (t + 1) * P)
                keys = (t + 1) * P
                out = bank[2 + s % 2]
                if s % (2 * TILES) == 0:
                    pe.wait_ge(rqk_lo, 2 * p + 2)
                    pe.wait_ge(bias_lo, p + 1)
                if s >= 2:
                    pe.wait_ge(exp_done, s - 1)
                three(out[:, 0:keys], r_q_hi[rows, p % 2, toks], r_q_lo[rows, p % 2, toks],
                      r_k_hi[rows, p % 2, 0:keys], r_k_lo[rows, p % 2, 0:keys], True, False, True)
                for back in range(min(t + 1, 2)):
                    blk = out[:, keys - (back + 1) * P:keys - back * P]
                    nc.tensor.matmul(blk, b_hi[:, p % 2, hd, back * P:(back + 1) * P], flip[:, :],
                                     start=False, stop=False, skip_group_check=True)
                    last = nc.tensor.matmul(blk, b_lo[:, p % 2, hd, back * P:(back + 1) * P], flip[:, :],
                                            start=False, stop=(back == min(t, 1)), skip_group_check=True)
                last.then_inc(s_done, 1)

            def turn_weights(s):
                t = s % TILES
                pe.wait_ge(exp_done, s + 1)
                if s >= 2:
                    pe.wait_ge(p_out, s - 1)
                for j in range(t + 1):
                    last = nc.tensor.transpose(bank[4 + s % 2][:, j * P:(j + 1) * P], r_p[:, s % 3, j * P:(j + 1) * P], ident[:, :])
                last.then_inc(p_turned, 1)

            def weights_v(s):
                hd, t = s // TILES, s % TILES
                pe.wait_ge(p_out, s + 1)
                if s >= 2:
                    pe.wait_ge(o_scaled, s - 1)
                for j in range(t + 1):
                    last = nc.tensor.matmul(bank[6 + s % 2][:, 0:RPA_D], r_pt[:, s % 3, j * P:(j + 1) * P],
                                            r_v[:, j, hd * RPA_D:(hd + 1) * RPA_D], start=(j == 0), stop=(j == t))
                last.then_inc(pv_done, 1)

            for piece in qk_pieces(0):
                qk_piece(*piece)
            pe.wait_ge(flip_done, 1)
            pe.wait_ge(tok_out[2], 2 * TILES)
            for s in range(UNITS + 2):
                p, step = s // (2 * TILES), s % (2 * TILES)
                if s < UNITS:
                    scores(s)
                    if p + 1 < RPA_PAIRS:
                        if step == 0:
                            pieces = list(qk_pieces(p + 1))
                        for piece in pieces[(16 * step) // 7:(16 * (step + 1)) // 7]:
                            qk_piece(*piece)
                if 1 <= s <= UNITS:
                    turn_weights(s - 1)
                if s >= 2:
                    weights_v(s - 2)
            for t in range(TILES):
                pe.wait_ge(o_scaled, UNITS - TILES + t + 1)
                if t == 3:
                    pe.wait_ge(o_scaled, UNITS)
                turn(RPA_YT, t, r_o, LN_BANKS)

            def rpa_out_free(t):
                pe.wait_ge(turned_lo[RPA_YT], 2 * t + 2)
            out_projection(RPA_OUT, KD, t_hi, t_lo, 2, lambda k: None, rpa_out_free, False)
            feed_forward(1, FFN_IN[1], 2)
            ffn_out(1, 3)


def _columns(w):
    m = w.shape[1] // P
    return w.reshape(KD, P, m, P).transpose(2, 1, 0, 3).reshape(m, P, SLAB)


def _rows(w):
    return w.reshape(-1, P, SLAB)


def _token_major(w):
    return w.reshape(KD // 2, 2, P, 2, HALF).transpose(3, 0, 2, 1, 4).reshape(KD, P, SLAB)


def _paired(x, y):
    return np.stack([x, y], axis=1).reshape(-1, P, SLAB)


def kernel(x, gla_w_in, gla_w_gate_up, gla_b_gate, gla_norm_g, gla_w_out,
           rpa_w_in, rpa_rel_bias, rpa_w_out,
           mla_w_in, mla_q_norm_g, mla_kv_norm_g, mla_w_uq, mla_w_ukv, mla_w_out,
           ffn_w_in, ffn_w_out, ln_g, ln_b):
    import concourse.bacc as bacc
    from concourse.bass_utils import run_bass_kernel_spmd

    x2 = np.asarray(x)[0]
    g_in = np.asarray(gla_w_in)[0]
    q_end, k_end = GLA_HK, 2 * GLA_HK
    v_end, r_end = k_end + GLA_HV, k_end + 2 * GLA_HV
    r_in = np.asarray(rpa_w_in)[0]
    ffn_in, ffn_out = np.asarray(ffn_w_in), np.asarray(ffn_w_out)

    def ffn(i):
        return [_paired(_columns(ffn_in[i][:, :FFN]), _columns(ffn_in[i][:, FFN:])), _rows(ffn_out[i])]

    stream = np.concatenate(
        [_token_major(g_in[:, k_end:v_end]), _token_major(g_in[:, v_end:r_end]),
         _paired(_columns(g_in[:, :q_end]), _columns(g_in[:, q_end:k_end])), _rows(np.asarray(gla_w_out)[0])]
        + ffn(0)
        + [_token_major(r_in[:, 2 * D_MODEL:]),
           _paired(_columns(r_in[:, :D_MODEL]), _columns(r_in[:, D_MODEL:2 * D_MODEL])), _rows(np.asarray(rpa_w_out)[0])]
        + ffn(1))
    assert stream.shape == (SLABS, P, SLAB)
    rel = np.asarray(rpa_rel_bias)[0]
    last = rel[:, 2 * RPA_MAX_REL:]
    arrays = {
        "stream": np.ascontiguousarray(stream.reshape(SLABS // 2, 2, P, SLAB).transpose(0, 2, 1, 3)),
        "x": np.ascontiguousarray(x2),
        "x_t": np.ascontiguousarray(x2.T.reshape(KD, P, SEQ).transpose(1, 0, 2)),
        "w_gate_down": np.ascontiguousarray(g_in[:, r_end:].reshape(KD, P, GLA_RANK).transpose(1, 0, 2)),
        "w_gate_up": np.ascontiguousarray(np.asarray(gla_w_gate_up)[0]),
        "b_gate": np.ascontiguousarray(np.asarray(gla_b_gate)[0].reshape(GLA_HEADS, P).T),
        "norm_g": np.ascontiguousarray(np.asarray(gla_norm_g)[0]),
        "rel_bias": np.ascontiguousarray(np.concatenate([rel, np.repeat(last, 3 * P - rel.shape[1], axis=1)], axis=1)),
        "far_bias": np.ascontiguousarray(last[:, 0]),
        "ln_gb": np.ascontiguousarray(np.stack([np.asarray(ln_g), np.asarray(ln_b)], axis=2).reshape(2 * DEPTH, 2, D_MODEL)),
    }
    nc = bacc.Bacc("TRN2", target_bir_lowering=False, num_devices=1)
    aps = {n: nc.dram_tensor(n, v.shape, mybir.dt.from_np(v.dtype), kind="ExternalInput").ap() for n, v in arrays.items()}
    aps["out"] = nc.dram_tensor("out", (SEQ, D_MODEL), F32, kind="ExternalOutput").ap()
    build_program(nc, aps)
    r = run_bass_kernel_spmd(nc, [arrays], core_ids=[0])
    return r.results[0]["out"].reshape(1, SEQ, D_MODEL)
```

```python
from contextlib import ExitStack

import numpy as np
import concourse.bass as bass
from concourse import mybir

F32 = mybir.dt.float32
F32R = mybir.dt.float32r
I32 = mybir.dt.int32
ALU = mybir.AluOpType
ACT = mybir.ActivationFunctionType
AX = mybir.AxisListType

P = 128
D_MODEL = 1024
SEQ = 512
DEPTH = 2
CHUNK = 64
ALPHA = (2 * DEPTH) ** 0.25
LN_EPS = 1e-5
NEG_INF = -1e30

KD = D_MODEL // P
TILES = SEQ // P
HALF = 512
CHUNKS = SEQ // CHUNK

GLA_HEADS = 4
GLA_DK = D_MODEL // 2 // GLA_HEADS
GLA_DV = D_MODEL // GLA_HEADS
GLA_RANK = 16
GLA_TAU = 16.0
GLA_HK = GLA_HEADS * GLA_DK
GLA_HV = GLA_HEADS * GLA_DV

RPA_HEADS = 16
RPA_D = D_MODEL // RPA_HEADS
RPA_PAIRS = RPA_HEADS // 2
RPA_MAX_REL = 128

FFN = -(-8 * D_MODEL // (3 * 256)) * 256
KF = FFN // P

SLAB = 1024
RING = 4
RAWS = 2

GLA_V = 0
GLA_R = GLA_V + KD
GLA_QK = GLA_R + KD
GLA_OUT = GLA_QK + 2 * GLA_HEADS
FFN_IN = [GLA_OUT + KD, 0]
FFN_OUT = [FFN_IN[0] + 2 * KF, 0]
RPA_V = FFN_OUT[0] + KF
RPA_QK = RPA_V + KD
RPA_OUT = RPA_QK + 2 * RPA_PAIRS
FFN_IN[1] = RPA_OUT + KD
FFN_OUT[1] = FFN_IN[1] + 2 * KF
SLABS = FFN_OUT[1] + KF
TAIL = 4


def build_program(nc, a):
    ctx = ExitStack()
    with ctx:
        place = [(nc.sbuf_base + 31) // 32 * 32]

        def sb_at(name, shape, dt, offset):
            return nc.alloc_sbuf_tensor_at("s_" + name, shape, dt, offset=offset)

        def sb(name, shape, dt=F32):
            size = 4
            for s in shape[1:]:
                size *= s
            at = place[0]
            place[0] += (size + 31) // 32 * 32
            return sb_at(name, shape, dt, at)

        def sem(name):
            return ctx.enter_context(nc.semaphore(name))

        raw = sb("raw", [P, RAWS, 2, SLAB])
        w_hi = sb("w_hi", [P, RING, SLAB], F32R)
        w_lo = sb("w_lo", [P, RING, SLAB], F32R)
        t_hi = sb("t_hi", [P, KD, SEQ], F32R)
        t_lo = sb("t_lo", [P, KD, SEQ], F32R)
        h = sb("h", [P, TILES, D_MODEL])
        ln_gb = sb("ln_gb", [P, 2, D_MODEL])
        region = place[0]
        a_hi = sb("a_hi", [P, KF, SEQ], F32R)
        a_lo = sb("a_lo", [P, KF, SEQ], F32R)
        region_end = place[0]
        gate_at = place[0]
        gate_s = sb("gate_s", [P, 2, SEQ])
        prod_at = place[0]
        prod = sb("prod", [P, 2, SEQ])
        ident = sb("ident", [P, P])
        flip = sb("flip", [P, P], F32R)
        flip_f = sb("flip_f", [P, P])
        causal = sb("causal", [P, GLA_HEADS, P])
        minus_half = sb("minus_half", [P, GLA_HEADS])
        bn = sb("bn", [P, TILES, 12])
        mv = sb("mv", [P, TILES, 2])
        var_eps = sb("var_eps", [P, TILES])
        rstd = sb("rstd", [P, TILES])
        bn_o = sb("bn_o", [P, TILES, GLA_HEADS, 6])
        mv_o = sb("mv_o", [P, TILES, GLA_HEADS, 2])
        var_eps_o = sb("var_eps_o", [P, TILES, GLA_HEADS])
        rstd_o = sb("rstd_o", [P, TILES, GLA_HEADS])
        shift_o = sb("shift_o", [P, TILES, GLA_HEADS])
        decay = sb("decay", [P, GLA_HEADS * CHUNKS])
        b_gate = sb("b_gate", [P, GLA_HEADS])
        far_bias = sb("far_bias", [P, RPA_HEADS])
        UNITS = RPA_HEADS * TILES
        neg_max = sb("neg_max", [P, UNITS])
        row_sum = sb("row_sum", [P, UNITS])
        inv_sum = sb("inv_sum", [P, UNITS])

        def carve(start):
            at = [start]

            def get(name, shape, dt=F32):
                size = 4
                for s in shape[1:]:
                    size *= s
                t = sb_at(name, shape, dt, at[0])
                at[0] += size
                assert at[0] <= region_end, name
                return t
            return get, at

        get, at = carve(region)
        g_v = get("g_v", [P, TILES, D_MODEL])
        g_q = get("g_q", [P, GLA_HEADS, SEQ])
        g_ki = get("g_ki", [P, GLA_HEADS, SEQ])
        g_ke = get("g_ke", [P, GLA_HEADS, SEQ])
        rg_at = at[0]
        g_rg = get("g_rg", [P, TILES, D_MODEL])
        on_at = at[0]
        g_on = get("g_on", [P, TILES, D_MODEL])
        kt_at = at[0]
        g_kt = get("g_kt", [P, 2, GLA_HK])
        g_state = get("g_state", [P, 2, GLA_HEADS, GLA_DV])
        g_am = get("g_am", [P, 2, GLA_HEADS * P])
        get, _ = carve(rg_at)
        wg_hi = get("wg_hi", [P, KD, P], F32R)
        wg_lo = get("wg_lo", [P, KD, P], F32R)
        wg_raw = get("wg_raw", [P, KD, GLA_RANK])
        get, _ = carve(on_at)
        x_t = get("x_t", [P, KD, SEQ])
        get, _ = carve(on_at)
        g_e = get("g_e", [P, GLA_HEADS, SEQ])
        g_c = get("g_c", [P, GLA_HEADS, SEQ])
        get, _ = carve(kt_at)
        g_low = get("g_low", [GLA_RANK, SEQ])
        w_up = get("w_up", [GLA_RANK, GLA_HK])
        norm_g = sb_at("norm_g", [P, D_MODEL], F32, gate_at)
        keep = sb_at("keep", [P, SEQ], F32, prod_at)
        get, _ = carve(region)
        r_v = get("r_v", [P, TILES, D_MODEL])
        r_q_hi = get("r_q_hi", [P, 2, SEQ], F32R)
        r_q_lo = get("r_q_lo", [P, 2, SEQ], F32R)
        r_k_hi = get("r_k_hi", [P, 2, SEQ], F32R)
        r_k_lo = get("r_k_lo", [P, 2, SEQ], F32R)
        b_raw = get("b_raw", [P, 2, 2, 2 * P])
        b_hi = get("b_hi", [P, 2, 2, 2 * P], F32R)
        b_lo = get("b_lo", [P, 2, 2, 2 * P], F32R)
        r_p = get("r_p", [P, 3, SEQ])
        r_pt = get("r_pt", [P, 3, SEQ])
        r_o = get("r_o", [P, TILES, D_MODEL])
        assert place[0] <= nc.sbuf_usable_end, (place[0], nc.sbuf_usable_end)

        bank = [ctx.enter_context(nc.psum_tensor(f"bank{i}", [P, HALF], F32)) for i in range(8)]

        raw_full = [sem(f"raw_full{i}") for i in range(RAWS)]
        first_full = sem("first_full")
        hi_done = sem("hi_done")
        lo_done = sem("lo_done")
        slab_done = sem("slab_done")
        consts = sem("consts")
        flip_done = sem("flip_done")
        x_full = [sem(f"x_full{i}") for i in range(4)]
        x_hi = sem("x_hi")
        x_lo = sem("x_lo")
        h_full = sem("h_full")
        small_full = sem("small_full")
        gb_full = sem("gb_full")
        dve_step = sem("dve_step")
        pool_step = sem("pool_step")
        act_step = sem("act_step")
        out_full = sem("out_full")
        acc_done = [sem(f"acc_done{n}") for n in range(4)]
        stats = [sem(f"stats{n}") for n in range(4)]
        rstd_done = [sem(f"rstd_done{n}") for n in range(4)]
        normed = [sem(f"normed{n}") for n in range(4)]
        turned = [sem(f"turned{n}") for n in range(5)]
        turned_hi = [sem(f"turned_hi{n}") for n in range(5)]
        turned_lo = [sem(f"turned_lo{n}") for n in range(5)]
        silu_done = [sem(f"silu_done{n}") for n in range(2)]
        prod_done = [sem(f"prod_done{n}") for n in range(2)]
        a_hi_done = [sem(f"a_hi_done{n}") for n in range(2)]
        a_lo_done = [sem(f"a_lo_done{n}") for n in range(2)]
        tok_done = [sem(f"tok_done{n}") for n in range(3)]
        tok_out = [sem(f"tok_out{n}") for n in range(3)]
        wg_ready = sem("wg_ready")
        low_done = sem("low_done")
        low_out = sem("low_out")
        up_done = sem("up_done")
        abs_done = sem("abs_done")
        min_done = sem("min_done")
        log_done = sem("log_done")
        cum_done = sem("cum_done")
        rest_done = sem("rest_done")
        exps_done = sem("exps_done")
        rg_done = sem("rg_done")
        qk_scaled = sem("qk_scaled")
        zeroed = sem("zeroed")
        ke_turned = sem("ke_turned")
        ke_out = sem("ke_out")
        sc_done = sem("sc_done")
        sc_masked = sem("sc_masked")
        upd_done = sem("upd_done")
        state_done = sem("state_done")
        intra_done = sem("intra_done")
        inter_done = sem("inter_done")
        o_stats = sem("o_stats")
        o_rstd = sem("o_rstd")
        shift_done = sem("shift_done")
        o_out = sem("o_out")
        y_done = sem("y_done")
        far_full = sem("far_full")
        bias_full = [sem("bias_full0"), sem("bias_full1")]
        bias_sub = sem("bias_sub")
        bias_hi = sem("bias_hi")
        bias_lo = sem("bias_lo")
        rqk_hi = sem("rqk_hi")
        rqk_lo = sem("rqk_lo")
        s_done = sem("s_done")
        max_done = sem("max_done")
        exp_done = sem("exp_done")
        p_turned = sem("p_turned")
        p_out = sem("p_out")
        pv_done = sem("pv_done")
        o_scaled = sem("o_scaled")

        block = ctx.enter_context(nc.Block())

        GLA_YT, RPA_YT = 3, 4
        LN_BANKS = [[(6, 7), (2, 3), (4, 5), (0, 1)], [(4, 5), (0, 1), (2, 3), (6, 7)],
                    [(0, 1), (2, 3), (4, 5), (6, 7)], [(4, 5), (6, 7), (0, 1), (2, 3)]]
        GLA_Y_BANKS = [(4, 5), (2, 3), (4, 5), (0, 1)]
        RPA_Y_BANKS = LN_BANKS[2]
        GATE_BANKS, UP_BANKS = [(6, 7), (0, 1)], [(2, 3), (2, 3)]
        RPA_V_BANKS = [4, 5, 0, 1, 2, 3, 6, 7]

        @block.sync
        def _(sp):
            def load_pair(pair, slot):
                sp.dma_start(raw[:, slot, :, :], a["stream"][pair]).then_inc(raw_full[slot], 16)

            sp.dma_start(raw[:, 0, 0, :], a["stream"][0][:, 0, :]).then_inc(first_full, 16)
            for i in range(4):
                sp.dma_start(x_t[:, 2 * i:2 * i + 2, :], a["x_t"][:, 2 * i:2 * i + 2, :]).then_inc(x_full[i], 16)
                if i == 0:
                    sp.dma_start(raw[:, 0, 1, :], a["stream"][0][:, 1, :]).then_inc(raw_full[0], 16)
                    load_pair(1, 1)
            sp.dma_start(wg_raw[:, :, :], a["w_gate_down"]).then_inc(small_full, 16)
            sp.dma_start(w_up[:, :], a["w_gate_up"]).then_inc(small_full, 16)
            sp.dma_start(b_gate[:, :], a["b_gate"]).then_inc(small_full, 16)
            sp.dma_start(norm_g[:, :], a["norm_g"].partition_broadcast(P)).then_inc(small_full, 16)
            sp.dma_start(h[:, :, :], a["x"].rearrange("(t p) d -> p t d", p=P)).then_inc(h_full, 16)
            with sp.Fori(1, SLABS // (2 * RAWS)) as i:
                for slot in range(RAWS):
                    sp.wait_ge(hi_done, i * (2 * RAWS) + (2 * slot + 2 - 2 * RAWS))
                    sp.wait_ge(lo_done, i * (2 * RAWS) + (2 * slot + 2 - 2 * RAWS))
                    load_pair(i * RAWS + slot, slot)
            for t in range(TILES):
                sp.wait_ge(normed[3], t + 1)
                sp.dma_start(a["out"][t * P:(t + 1) * P, :], h[:, t, :]).then_inc(out_full, 16)
            sp.wait_ge(out_full, 16 * TILES)

        @block.scalar
        def _(act):
            def split_hi(n, i=None):
                if n >= SLABS:
                    return
                pair = n // 2
                more = 0 if i is None else i
                if n == 0:
                    act.wait_ge(first_full, 16)
                else:
                    act.wait_ge(raw_full[pair % RAWS], more * 16 + 16 * (pair // RAWS + 1))
                if n >= RING:
                    act.wait_ge(slab_done, more * RING + (n - RING + 1))
                nc.scalar.activation(w_hi[:, n % RING, :], raw[:, pair % RAWS, n % 2, :], ACT.Copy).then_inc(hi_done, 1)

            def turned_high(which, t, banks):
                for half in range(2):
                    act.wait_ge(turned[which], 2 * t + half + 1)
                    nc.scalar.activation(
                        t_hi[:, 4 * half:4 * half + 4, t * P:(t + 1) * P],
                        bank[banks[t][half]][:, :].rearrange("p (k c) -> p k c", k=4),
                        ACT.Copy).then_inc(turned_hi[which], 1)

            def load_gb(n):
                if n > 0:
                    act.wait_ge(normed[n - 1], TILES)
                act.dma_start(ln_gb[:, :, :], a["ln_gb"][n].partition_broadcast(P)).then_inc(gb_full, 16)

            def token_major(which, n0, bank_of, copy_out):
                for half in range(2):
                    for k in range(KD // 2):
                        n = n0 + half * (KD // 2) + k
                        split_hi(n + RING)
                    for t in range(TILES):
                        if t < TILES - 1:
                            act.wait_ge(tok_done[which], half * (TILES - 1) + t + 1)
                        else:
                            act.wait_ge(slab_done, n0 + (half + 1) * (KD // 2))
                        copy_out(half, t, bank[bank_of(half, t)]).then_inc(tok_out[which], 1)

            def out_projection(n0, slabs, ln):
                banks = LN_BANKS[ln]
                for k in range(slabs - TAIL):
                    split_hi(n0 + k + RING)
                behind = n0 + slabs - TAIL + RING
                if ln == 3:
                    return
                turned_high(ln, 0, banks)
                split_hi(behind)
                split_hi(behind + 1)
                turned_high(ln, 1, banks)
                split_hi(behind + 2)
                split_hi(behind + 3)
                turned_high(ln, 2, banks)
                turned_high(ln, 3, banks)

            def feed_forward(f, n0):
                def body(i, first):
                    for c in range(2):
                        act.wait_ge(slab_done, i * RING + (n0 + 2 * c + 1))
                        if not first:
                            act.wait_ge(prod_done[f], i * 2 + (c - 1))
                        nc.scalar.activation(gate_s[:, c, :], bank[GATE_BANKS[f][c]][:, :], ACT.Silu).then_inc(silu_done[f], 1)
                        split_hi(n0 + 2 * c + RING, i)
                        split_hi(n0 + 2 * c + 1 + RING, i)
                        act.wait_ge(prod_done[f], i * 2 + (c + 1))
                        nc.scalar.activation(a_hi[:, bass.ds(i * 2 + c, 1), :], prod[:, bass.ds(c, 1), :],
                                             ACT.Copy).then_inc(a_hi_done[f], 1)
                body(0, True)
                with act.Fori(1, KF // 2) as i:
                    body(i, False)

            load_gb(0)
            for i in range(4):
                split_hi(i)
                act.wait_ge(x_full[i], 16)
                nc.scalar.activation(t_hi[:, 2 * i:2 * i + 2, :], x_t[:, 2 * i:2 * i + 2, :], ACT.Copy).then_inc(x_hi, 1)
            act.wait_ge(consts, 8)
            nc.scalar.activation(flip[:, :], flip_f[:, :], ACT.Copy).then_inc(flip_done, 1)
            act.wait_ge(small_full, 64)
            act.wait_ge(zeroed, 2)
            nc.scalar.activation(wg_hi[:, :, 0:GLA_RANK], wg_raw[:, :, :], ACT.Copy).then_inc(wg_ready, 1)

            token_major(0, GLA_V, lambda half, t: 4 * half + t, lambda half, t, b: nc.scalar.activation(
                g_v[:, t, half * HALF:(half + 1) * HALF], b[:, :], ACT.Copy))
            act.wait_ge(low_done, 1)
            nc.scalar.activation(g_low[:, :], bank[0][0:GLA_RANK, :], ACT.Copy).then_inc(low_out, 1)
            for hd in range(GLA_HEADS):
                act.wait_ge(up_done, hd + 1)
                nc.scalar.activation(g_e[:, hd, :], bank[hd][:, :], ACT.Abs, bias=b_gate[:, hd:hd + 1]).then_inc(abs_done, 1)
            act.wait_ge(abs_done, GLA_HEADS)
            nc.scalar.activation(g_e[:, :, :], g_e[:, :, :], ACT.Exp, scale=-1.0).then_inc(act_step, 1)
            act.wait_ge(act_step, 1)
            nc.scalar.activation(g_e[:, :, :], g_e[:, :, :], ACT.Ln, bias=1.0).then_inc(log_done, 1)
            split_hi(GLA_R + RING)
            act.wait_ge(cum_done, GLA_HEADS)
            nc.scalar.activation(g_q[:, :, :], g_c[:, :, :], ACT.Exp, scale=1.0 / GLA_TAU).then_inc(exps_done, 1)
            split_hi(GLA_R + 1 + RING)
            nc.scalar.activation(g_ki[:, :, :], g_c[:, :, :], ACT.Exp, scale=-1.0 / GLA_TAU).then_inc(exps_done, 1)
            chunk_ends = g_c[:, :, :].rearrange("p h (c i) -> p (h c) i", i=CHUNK)[:, :, CHUNK - 1]
            nc.scalar.activation(decay[:, :], chunk_ends, ACT.Exp, scale=1.0 / GLA_TAU).then_inc(exps_done, 1)
            act.wait_ge(rest_done, 1)
            nc.scalar.activation(g_ke[:, :, :], g_e[:, :, :], ACT.Exp, scale=1.0 / GLA_TAU).then_inc(exps_done, 1)
            for half in range(2):
                for k in range(KD // 2):
                    n = GLA_R + half * (KD // 2) + k
                    if n >= GLA_R + 2:
                        split_hi(n + RING)
                for t in range(TILES):
                    if t < TILES - 1:
                        act.wait_ge(tok_done[1], half * (TILES - 1) + t + 1)
                    else:
                        act.wait_ge(slab_done, GLA_R + (half + 1) * (KD // 2))
                    nc.scalar.activation(g_rg[:, t, half * HALF:(half + 1) * HALF],
                                         bank[4 - 4 * half + t][:, :], ACT.Silu).then_inc(tok_out[1], 1)
            for n in range(GLA_QK, GLA_OUT):
                split_hi(n + RING)
            def ke_tile_out(t):
                act.wait_ge(ke_turned, t + 1)
                if t >= 2:
                    act.wait_ge(upd_done, 2 * (t - 2) + 2)
                nc.scalar.activation(g_kt[:, t % 2, :], bank[5][:, :], ACT.Copy).then_inc(ke_out, 1)

            def normalise_o(t):
                act.wait_ge(shift_done, t + 1)
                for hd in range(GLA_HEADS):
                    o = bank[hd // 2][:, (hd % 2) * GLA_DV:(hd % 2 + 1) * GLA_DV]
                    last = nc.scalar.activation(g_on[:, t, hd * GLA_DV:(hd + 1) * GLA_DV], o, ACT.Identity,
                                                bias=shift_o[:, t, hd:hd + 1], scale=rstd_o[:, t, hd:hd + 1])
                last.then_inc(o_out, 1)

            ke_tile_out(0)
            for t in range(TILES):
                if t + 1 < TILES:
                    ke_tile_out(t + 1)
                else:
                    for done in range(3):
                        turned_high(GLA_YT, done, GLA_Y_BANKS)
                normalise_o(t)
            turned_high(GLA_YT, TILES - 1, GLA_Y_BANKS)
            out_projection(GLA_OUT, KD, 0)
            load_gb(1)
            feed_forward(0, FFN_IN[0])
            out_projection(FFN_OUT[0], KF, 1)
            load_gb(2)

            def load_bias(p):
                if p >= 2:
                    act.wait_ge(bias_hi, p - 1)
                    act.wait_ge(bias_lo, p - 1)
                for hd in range(2):
                    tab = a["rel_bias"]
                    start = (2 * p + hd) * 3 * P + 1
                    act.dma_start(b_raw[:, p % 2, hd, :], bass.AP(tab.tensor, start, [[1, P], [1, 2 * P]])).then_inc(
                        bias_full[p % 2], 16)

            def bias_high(p):
                act.wait_ge(bias_sub, p + 1)
                if p >= 2:
                    act.wait_ge(s_done, 2 * TILES * (p - 1))
                nc.scalar.activation(b_hi[:, p % 2, :, :], b_raw[:, p % 2, :, :], ACT.Copy).then_inc(bias_hi, 1)

            def rpa_high(p, is_k):
                n = RPA_QK + 2 * p + is_k
                act.wait_ge(slab_done, n + 1)
                if p >= 2:
                    act.wait_ge(s_done, 2 * TILES * (p - 1))
                if is_k:
                    nc.scalar.activation(r_k_hi[:, p % 2, :], bank[1][:, :], ACT.Copy).then_inc(rqk_hi, 1)
                else:
                    nc.scalar.activation(r_q_hi[:, p % 2, :], bank[0][:, :], ACT.Copy, scale=RPA_D ** -0.5).then_inc(rqk_hi, 1)
                split_hi(n + RING)

            act.dma_start(far_bias[:, :], a["far_bias"].partition_broadcast(P)).then_inc(far_full, 16)
            load_bias(0)
            load_bias(1)
            token_major(2, RPA_V, lambda half, t: RPA_V_BANKS[4 * half + t], lambda half, t, b: nc.scalar.activation(
                r_v[:, t, half * HALF:(half + 1) * HALF], b[:, :], ACT.Copy))
            bias_high(0)
            rpa_high(0, 0)
            rpa_high(0, 1)
            for s in range(UNITS):
                p, step, t = s // (2 * TILES), s % (2 * TILES), s % TILES
                act.wait_ge(max_done, s + 1)
                if s >= 3:
                    act.wait_ge(p_turned, s - 2)
                nc.scalar.activation(r_p[:, s % 3, 0:(t + 1) * P], bank[2 + s % 2][:, 0:(t + 1) * P], ACT.Exp,
                                     bias=neg_max[:, s:s + 1], accum_out=row_sum[:, s:s + 1]).then_inc(exp_done, 1)
                if p + 1 < RPA_PAIRS:
                    if step == 1:
                        bias_high(p + 1)
                    if step == 3:
                        rpa_high(p + 1, 0)
                        if p + 2 < RPA_PAIRS:
                            load_bias(p + 2)
                    if step == 6:
                        rpa_high(p + 1, 1)
            for t in range(TILES):
                turned_high(RPA_YT, t, RPA_Y_BANKS)
            out_projection(RPA_OUT, KD, 2)
            load_gb(3)
            feed_forward(1, FFN_IN[1])
            out_projection(FFN_OUT[1], KF, 3)

        @block.gpsimd
        def _(pool):
            steps = [0]

            def own(ins):
                steps[0] += 1
                ins.then_inc(pool_step, 1)
                pool.wait_ge(pool_step, steps[0])

            def split_lo(n, i=None):
                if n >= SLABS:
                    return
                more = 0 if i is None else i
                pair = n // 2
                pool.wait_ge(hi_done, more * RING + (n + 1))
                nc.gpsimd.tensor_tensor(w_lo[:, n % RING, :], raw[:, pair % RAWS, n % 2, :],
                                        w_hi[:, n % RING, :].bitcast(F32), ALU.subtract).then_inc(lo_done, 1)

            def ln_rstd(ln, t):
                pool.wait_ge(stats[ln], t + 1)
                own(nc.gpsimd.tensor_scalar(var_eps[:, t:t + 1], mv[:, t, 1:2], LN_EPS, None, ALU.add))
                nc.gpsimd.tensor_tensor(rstd[:, t:t + 1], var_eps[:, t:t + 1], minus_half[:, 0:1], ALU.pow).then_inc(rstd_done[ln], 1)

            def out_projection(n0, slabs, ln):
                for k in range(slabs - TAIL):
                    split_lo(n0 + k + RING)
                behind = n0 + slabs - TAIL + RING
                ln_rstd(ln, 0)
                ln_rstd(ln, 1)
                split_lo(behind)
                ln_rstd(ln, 2)
                split_lo(behind + 1)
                split_lo(behind + 2)
                ln_rstd(ln, 3)
                split_lo(behind + 3)

            def feed_forward(n0):
                with pool.Fori(0, KF // 2) as i:
                    for c in range(RING):
                        split_lo(n0 + c + RING, i)

            nc.gpsimd.memset(ident[:, :], 0.0).then_inc(consts, 1)
            nc.gpsimd.memset(flip_f[:, :], 0.0).then_inc(consts, 1)
            nc.gpsimd.memset(causal[:, :, :], 1.0).then_inc(consts, 1)
            nc.gpsimd.memset(minus_half[:, :], -0.5).then_inc(consts, 1)
            nc.gpsimd.memset(keep[:, :], 1.0).then_inc(consts, 1)
            pool.wait_ge(consts, 5)
            nc.gpsimd.affine_select(out=ident[:, :], in_=ident[:, :], compare_op=ALU.not_equal, fill=1.0, base=0,
                                    pattern=[[-1, P]], channel_multiplier=1).then_inc(consts, 1)
            nc.gpsimd.affine_select(out=causal[:, :, :], in_=causal[:, :, :], compare_op=ALU.is_ge, fill=0.0, base=0,
                                    pattern=[[0, GLA_HEADS], [1, P]], channel_multiplier=-1).then_inc(consts, 1)
            nc.gpsimd.affine_select(out=flip_f[:, :], in_=flip_f[:, :], compare_op=ALU.not_equal, fill=1.0,
                                    base=-(P - 1), pattern=[[1, P]], channel_multiplier=1).then_inc(consts, 1)
            pool.wait_ge(consts, 8)
            nc.gpsimd.memset(causal[0:CHUNK, :, CHUNK:P], 0.0).then_inc(consts, 1)
            nc.gpsimd.memset(keep[:, :].rearrange("p (c i) -> p c i", i=CHUNK)[:, :, 0:1], 0.0).then_inc(consts, 1)
            for n in range(RING):
                split_lo(n)
            for n in range(GLA_V, GLA_R):
                split_lo(n + RING)
            for half in range(2):
                for k in range(KD // 2):
                    split_lo(GLA_R + half * (KD // 2) + k + RING)
                for t in range(TILES):
                    cols = slice(half * HALF, (half + 1) * HALF)
                    pool.wait_ge(tok_out[1], half * TILES + t + 1)
                    nc.gpsimd.tensor_tensor(g_rg[:, t, cols], g_rg[:, t, cols], norm_g[:, cols], ALU.mult).then_inc(rg_done, 1)
            for n in range(GLA_QK, GLA_OUT):
                split_lo(n + RING)
            for t in range(TILES):
                pool.wait_ge(o_stats, t + 1)
                own(nc.gpsimd.tensor_scalar(var_eps_o[:, t, :], mv_o[:, t, :, 1], LN_EPS, None, ALU.add))
                nc.gpsimd.tensor_tensor(rstd_o[:, t, :], var_eps_o[:, t, :], minus_half[:, :], ALU.pow).then_inc(o_rstd, 1)
            out_projection(GLA_OUT, KD, 0)
            feed_forward(FFN_IN[0])
            out_projection(FFN_OUT[0], KF, 1)
            for n in range(RPA_V, RPA_OUT):
                split_lo(n + RING)
            out_projection(RPA_OUT, KD, 2)
            feed_forward(FFN_IN[1])
            out_projection(FFN_OUT[1], KF, 3)

        @block.vector
        def _(dve):
            steps = [0]

            def own(ins):
                steps[0] += 1
                ins.then_inc(dve_step, 1)
                dve.wait_ge(dve_step, steps[0])

            def turned_low(which, t, banks):
                for half in range(2):
                    dve.wait_ge(turned_hi[which], 2 * t + half + 1)
                    nc.vector.tensor_tensor(
                        t_lo[:, 4 * half:4 * half + 4, t * P:(t + 1) * P],
                        bank[banks[t][half]][:, :].rearrange("p (k c) -> p k c", k=4),
                        t_hi[:, 4 * half:4 * half + 4, t * P:(t + 1) * P].bitcast(F32),
                        ALU.subtract).then_inc(turned_lo[which], 1)

            def layer_norm(ln, n_end):
                banks = LN_BANKS[ln]

                def residual(t):
                    if t < TILES - 1:
                        dve.wait_ge(acc_done[ln], t + 1)
                    else:
                        dve.wait_ge(slab_done, n_end)
                    if ln == 0 and t == 0:
                        dve.wait_ge(h_full, 16)
                    for half in range(2):
                        cols = slice(half * HALF, (half + 1) * HALF)
                        own(nc.vector.scalar_tensor_tensor(out=h[:, t, cols], in0=h[:, t, cols], scalar=ALPHA,
                                                           in1=bank[banks[t][half]][:, :], op0=ALU.mult, op1=ALU.add))
                        own(nc.vector.bn_stats(bn[:, t, 6 * half:6 * half + 6], h[:, t, cols]))
                    ins = nc.vector.bn_aggr(mv[:, t, :], bn[:, t, :])
                    ins.then_inc(stats[ln], 1)
                    dve.wait_ge(stats[ln], t + 1)

                def normalise(t):
                    if t == 0:
                        dve.wait_ge(gb_full, 16 * (ln + 1))
                    own(nc.vector.scalar_tensor_tensor(out=h[:, t, :], in0=h[:, t, :], scalar=mv[:, t, 0:1],
                                                       in1=ln_gb[:, 0, :], op0=ALU.subtract, op1=ALU.mult))
                    dve.wait_ge(rstd_done[ln], t + 1)
                    nc.vector.scalar_tensor_tensor(out=h[:, t, :], in0=h[:, t, :], scalar=rstd[:, t:t + 1],
                                                   in1=ln_gb[:, 1, :], op0=ALU.mult, op1=ALU.add).then_inc(normed[ln], 1)

                residual(0)
                normalise(0)
                residual(1)
                normalise(1)
                if ln < 3:
                    turned_low(ln, 0, banks)
                residual(2)
                if ln < 3:
                    turned_low(ln, 1, banks)
                normalise(2)
                residual(3)
                normalise(3)
                if ln < 3:
                    turned_low(ln, 2, banks)
                    turned_low(ln, 3, banks)

            def feed_forward(f, n0):
                def body(i):
                    for c in range(2):
                        dve.wait_ge(slab_done, i * RING + (n0 + 2 * c + 2))
                        dve.wait_ge(silu_done[f], i * 2 + (c + 1))
                        nc.vector.tensor_tensor(prod[:, c, :], gate_s[:, c, :], bank[UP_BANKS[f][c]][:, :], ALU.mult).then_inc(prod_done[f], 1)
                        dve.wait_ge(a_hi_done[f], i * 2 + (c + 1))
                        nc.vector.tensor_tensor(a_lo[:, bass.ds(i * 2 + c, 1), :], prod[:, bass.ds(c, 1), :],
                                                a_hi[:, bass.ds(i * 2 + c, 1), :].bitcast(F32), ALU.subtract).then_inc(a_lo_done[f], 1)
                body(0)
                with dve.Fori(1, KF // 2) as i:
                    body(i)

            nc.vector.memset(wg_hi[:, :, :].bitcast(F32), 0.0).then_inc(zeroed, 1)
            nc.vector.memset(wg_lo[:, :, :].bitcast(F32), 0.0).then_inc(zeroed, 1)
            nc.vector.memset(g_am[:, :, :], 0.0).then_inc(zeroed, 1)
            for i in range(4):
                dve.wait_ge(x_hi, i + 1)
                nc.vector.tensor_tensor(t_lo[:, 2 * i:2 * i + 2, :], x_t[:, 2 * i:2 * i + 2, :],
                                        t_hi[:, 2 * i:2 * i + 2, :].bitcast(F32), ALU.subtract).then_inc(x_lo, 1)
            dve.wait_ge(wg_ready, 1)
            dve.wait_ge(zeroed, 2)
            nc.vector.tensor_tensor(wg_lo[:, :, 0:GLA_RANK], wg_raw[:, :, :], wg_hi[:, :, 0:GLA_RANK].bitcast(F32),
                                    ALU.subtract).then_inc(wg_ready, 1)
            for hd in range(GLA_HEADS):
                dve.wait_ge(abs_done, hd + 1)
                if hd == 0:
                    dve.wait_ge(x_lo, 4)
                nc.vector.tensor_scalar(g_c[:, hd, :], bank[hd][:, :], b_gate[:, hd:hd + 1], 0.0, ALU.add, ALU.min).then_inc(min_done, 1)
            dve.wait_ge(min_done, GLA_HEADS)
            dve.wait_ge(log_done, 1)
            own(nc.vector.tensor_tensor(g_c[:, :, :], g_c[:, :, :], g_e[:, :, :], ALU.subtract))
            dve.wait_ge(consts, 10)
            for hd in range(GLA_HEADS):
                nc.vector.tensor_tensor_scan(g_c[:, hd, :], keep[:, :], g_c[:, hd, :], 0.0, ALU.mult, ALU.add).then_inc(cum_done, 1)
            dve.wait_ge(cum_done, GLA_HEADS)
            cum = g_c[:, :, :].rearrange("p h (c i) -> p (h c) i", i=CHUNK)
            nc.vector.tensor_tensor(g_e[:, :, :].rearrange("p h (c i) -> p (h c) i", i=CHUNK),
                                    cum[:, :, CHUNK - 1:CHUNK].to_broadcast([P, GLA_HEADS * CHUNKS, CHUNK]), cum,
                                    ALU.subtract).then_inc(rest_done, 1)
            dve.wait_ge(exps_done, 4)
            for hd in range(GLA_HEADS):
                b_q, b_k = bank[4 + 2 * (hd % 2)], bank[5 + 2 * (hd % 2)]
                dve.wait_ge(slab_done, GLA_QK + 2 * hd + 1)
                nc.vector.scalar_tensor_tensor(out=g_q[:, hd, :], in0=b_q[:, :], scalar=GLA_DK ** -0.5, in1=g_q[:, hd, :],
                                               op0=ALU.mult, op1=ALU.mult).then_inc(qk_scaled, 1)
                dve.wait_ge(slab_done, GLA_QK + 2 * hd + 2)
                nc.vector.tensor_tensor(g_ki[:, hd, :], b_k[:, :], g_ki[:, hd, :], ALU.mult).then_inc(qk_scaled, 1)
                nc.vector.tensor_tensor(g_ke[:, hd, :], b_k[:, :], g_ke[:, hd, :], ALU.mult).then_inc(qk_scaled, 1)

            def mask_scores(t):
                dve.wait_ge(sc_done, t + 1)
                if t >= 2:
                    dve.wait_ge(intra_done, t - 1)
                nc.vector.copy_predicated(g_am[:, t % 2, :], causal[:, :, :].rearrange("p h i -> p (h i)").bitcast(I32),
                                          bank[4][:, :]).then_inc(sc_masked, 1)

            def update_state(c):
                if c == CHUNKS - 1:
                    return
                dve.wait_ge(upd_done, c + 1)
                if c >= 2:
                    dve.wait_ge(inter_done, c - 1)
                if c >= 1:
                    dve.wait_ge(state_done, c)
                banks = (6, 7) if c % 2 == 0 else (2, 3)
                for hd in range(GLA_HEADS):
                    new = g_state[:, (c + 1) % 2, hd, :]
                    upd = bank[banks[hd // 2]][:, (hd % 2) * GLA_DV:(hd % 2 + 1) * GLA_DV]
                    if c == 0:
                        last = nc.vector.tensor_copy(new, upd)
                    else:
                        last = nc.vector.scalar_tensor_tensor(
                            out=new, in0=g_state[:, c % 2, hd, :], scalar=decay[:, hd * CHUNKS + c:hd * CHUNKS + c + 1],
                            in1=upd, op0=ALU.mult, op1=ALU.add)
                last.then_inc(state_done, 1)

            dve.wait_ge(zeroed, 3)
            dve.wait_ge(consts, 10)
            def gate_o(t):
                dve.wait_ge(o_out, t + 1)
                if t == 0:
                    dve.wait_ge(rg_done, 2 * TILES)
                nc.vector.tensor_tensor(g_on[:, t, :], g_on[:, t, :], g_rg[:, t, :], ALU.mult).then_inc(y_done, 1)

            mask_scores(0)
            for t in range(TILES):
                update_state(2 * t)
                if t + 1 < TILES:
                    mask_scores(t + 1)
                if t >= 1:
                    gate_o(t - 1)
                if t == TILES - 1:
                    turned_low(GLA_YT, 0, GLA_Y_BANKS)
                    turned_low(GLA_YT, 1, GLA_Y_BANKS)
                dve.wait_ge(inter_done, 2 * t + 1)
                for hd in range(GLA_HEADS):
                    o = bank[hd // 2][:, (hd % 2) * GLA_DV:(hd % 2 + 1) * GLA_DV]
                    last = nc.vector.bn_stats(bn_o[:, t, hd, :], o)
                own(last)
                for hd in range(GLA_HEADS):
                    last = nc.vector.bn_aggr(mv_o[:, t, hd, :], bn_o[:, t, hd, :])
                last.then_inc(o_stats, 1)
                dve.wait_ge(o_stats, t + 1)
                update_state(2 * t + 1)
                dve.wait_ge(o_rstd, t + 1)
                nc.vector.scalar_tensor_tensor(out=shift_o[:, t, :], in0=mv_o[:, t, :, 0], scalar=-1.0,
                                               in1=rstd_o[:, t, :], op0=ALU.mult, op1=ALU.mult).then_inc(shift_done, 1)
            turned_low(GLA_YT, 2, GLA_Y_BANKS)
            gate_o(TILES - 1)
            turned_low(GLA_YT, 3, GLA_Y_BANKS)
            layer_norm(0, FFN_IN[0])
            feed_forward(0, FFN_IN[0])
            layer_norm(1, RPA_V)

            def bias_relative(p):
                dve.wait_ge(bias_full[p % 2], 32 * (p // 2 + 1))
                for hd in range(2):
                    own(nc.vector.tensor_scalar(b_raw[:, p % 2, hd, :], b_raw[:, p % 2, hd, :],
                                                far_bias[:, 2 * p + hd:2 * p + hd + 1], None, ALU.subtract))
                nc.vector.memset(b_raw[0:CHUNK, p % 2, :, 0:CHUNK], NEG_INF).then_inc(bias_sub, 1)

            def bias_low(p):
                dve.wait_ge(bias_hi, p + 1)
                nc.vector.tensor_tensor(b_lo[:, p % 2, :, :], b_raw[:, p % 2, :, :], b_hi[:, p % 2, :, :].bitcast(F32),
                                        ALU.subtract).then_inc(bias_lo, 1)

            def rpa_low(p, is_k):
                dve.wait_ge(rqk_hi, 2 * p + is_k + 1)
                if is_k:
                    ins = nc.vector.tensor_tensor(r_k_lo[:, p % 2, :], bank[1][:, :], r_k_hi[:, p % 2, :].bitcast(F32), ALU.subtract)
                else:
                    ins = nc.vector.scalar_tensor_tensor(out=r_q_lo[:, p % 2, :], in0=bank[0][:, :], scalar=RPA_D ** -0.5,
                                                         in1=r_q_hi[:, p % 2, :].bitcast(F32), op0=ALU.mult, op1=ALU.subtract)
                ins.then_inc(rqk_lo, 1)

            def weights_out(s):
                t = s % TILES
                dve.wait_ge(p_turned, s + 1)
                if s >= 3:
                    dve.wait_ge(pv_done, s - 2)
                nc.vector.tensor_copy(r_pt[:, s % 3, 0:(t + 1) * P], bank[4 + s % 2][:, 0:(t + 1) * P]).then_inc(p_out, 1)

            def scale_o(s):
                hd, t = s // TILES, s % TILES
                own(nc.vector.reciprocal(inv_sum[:, s:s + 1], row_sum[:, s:s + 1]))
                dve.wait_ge(pv_done, s + 1)
                nc.vector.tensor_scalar(r_o[:, t, hd * RPA_D:(hd + 1) * RPA_D], bank[6 + s % 2][:, 0:RPA_D],
                                        inv_sum[:, s:s + 1], None, ALU.mult).then_inc(o_scaled, 1)

            dve.wait_ge(far_full, 16)
            bias_relative(0)
            bias_low(0)
            rpa_low(0, 0)
            rpa_low(0, 1)
            for s in range(UNITS + 2):
                if s < UNITS:
                    p, step, t = s // (2 * TILES), s % (2 * TILES), s % TILES
                    dve.wait_ge(s_done, s + 1)
                    nc.vector.tensor_reduce(neg_max[:, s:s + 1], bank[2 + s % 2][:, 0:(t + 1) * P], AX.X, ALU.max,
                                            negate=True).then_inc(max_done, 1)
                    if p + 1 < RPA_PAIRS:
                        if step == 0:
                            bias_relative(p + 1)
                        if step == 2:
                            bias_low(p + 1)
                        if step == 4:
                            rpa_low(p + 1, 0)
                if 1 <= s <= UNITS:
                    weights_out(s - 1)
                if s < UNITS and step == 6 and p + 1 < RPA_PAIRS:
                    rpa_low(p + 1, 1)
                if s == UNITS + 1:
                    turned_low(RPA_YT, 0, RPA_Y_BANKS)
                    turned_low(RPA_YT, 1, RPA_Y_BANKS)
                if s >= 2:
                    scale_o(s - 2)
            turned_low(RPA_YT, 2, RPA_Y_BANKS)
            turned_low(RPA_YT, 3, RPA_Y_BANKS)
            layer_norm(2, FFN_IN[1])
            feed_forward(1, FFN_IN[1])
            layer_norm(3, SLABS)

        @block.tensor
        def _(pe):
            def three(out, l_hi, l_lo, r_hi, r_lo, start, stop, skip=False):
                nc.tensor.matmul(out, l_hi, r_hi, start=start, stop=False, skip_group_check=skip)
                nc.tensor.matmul(out, l_hi, r_lo, start=False, stop=False, skip_group_check=skip)
                return nc.tensor.matmul(out, l_lo, r_hi, start=False, stop=stop, skip_group_check=skip)

            def columns_piece(n, b, ks, toks=slice(0, SEQ)):
                s = n % RING
                for k in ks:
                    cols = slice(k * P, (k + 1) * P)
                    last = three(bank[b][:, toks], w_hi[:, s, cols], w_lo[:, s, cols], t_hi[:, k, toks], t_lo[:, k, toks],
                                 k == 0, k == KD - 1)
                return last

            def token_major(which, n0, bank_of, free=None, behind_ln=None):
                def part(half, kk, t):
                    n = n0 + half * (KD // 2) + kk
                    for j in range(2):
                        k = 2 * kk + j
                        if which == 0 and half == 0 and t == 0 and j == 0:
                            pe.wait_ge(x_lo, kk + 1)
                        toks = slice(t * P, (t + 1) * P)
                        cols = slice(j * HALF, (j + 1) * HALF)
                        last = three(bank[bank_of(half, t)][:, :], t_hi[:, k, toks], t_lo[:, k, toks],
                                     w_hi[:, n % RING, cols], w_lo[:, n % RING, cols], k == 0, k == KD - 1)
                    if kk == KD // 2 - 1 and t < TILES - 1:
                        last.then_inc(tok_done[which], 1)
                    return last

                for half in range(2):
                    groups = [(0, 1), (2, 3)] if half == 0 and behind_ln is not None else [(0, 1, 2, 3)]
                    for g, tiles in enumerate(groups):
                        for kk in range(KD // 2):
                            n = n0 + half * (KD // 2) + kk
                            if g == 0:
                                pe.wait_ge(lo_done, n + 1)
                            for t in tiles:
                                if kk == 0 and free is not None:
                                    free(half, t)
                                if kk == 0 and len(groups) == 2 and t % 2 == 0:
                                    pe.wait_ge(turned_lo[behind_ln], 2 * t + 4)
                                last = part(half, kk, t)
                            if g == len(groups) - 1:
                                last.then_inc(slab_done, 1)
                            elif kk in (1, 2):
                                turn_normed(behind_ln, kk + 1)

            def turn(which, t, src, banks):
                for half in range(2):
                    for k in range(4):
                        last = nc.tensor.transpose(bank[banks[t][half]][:, k * P:(k + 1) * P],
                                                   src[:, t, (4 * half + k) * P:(4 * half + k + 1) * P], ident[:, :])
                    last.then_inc(turned[which], 1)

            def turn_normed(ln, t):
                pe.wait_ge(normed[ln], t + 1)
                turn(ln, t, h, LN_BANKS[ln])

            def out_projection(n0, slabs, l_hi, l_lo, ln, ready, free, first=None, beside=None):
                def part(k, t):
                    toks = slice(t * P, (t + 1) * P)
                    s = (n0 + k) % RING
                    for half in range(2):
                        cols = slice(half * HALF, (half + 1) * HALF)
                        last = three(bank[LN_BANKS[ln][t][half]][:, :], l_hi[:, k, toks], l_lo[:, k, toks],
                                     w_hi[:, s, cols], w_lo[:, s, cols], k == 0, k == slabs - 1)
                    return last

                groups = [(0, 1), (2, 3)] if first else [(0, 1, 2, 3)]
                for g, tiles in enumerate(groups):
                    for k in range(slabs - TAIL):
                        if g == 0:
                            pe.wait_ge(lo_done, n0 + k + 1)
                            ready(k)
                        for t in tiles:
                            if k == 0:
                                free(t)
                            last = part(k, t)
                        if g == len(groups) - 1:
                            last.then_inc(slab_done, 1)
                        else:
                            beside(k)
                for t in range(TILES):
                    for k in range(slabs - TAIL, slabs):
                        if t == 0:
                            pe.wait_ge(lo_done, n0 + k + 1)
                            ready(k)
                        last = part(k, t)
                        if t == TILES - 1:
                            last.then_inc(slab_done, 1)
                        if k == slabs - TAIL // 2 - 1 and t >= 2 and ln < 3:
                            turn_normed(ln, t - 2)
                    if t < TILES - 1:
                        last.then_inc(acc_done[ln], 1)

            def feed_forward(f, n0, ln):
                def bank_of(c):
                    return (UP_BANKS if c % 2 else GATE_BANKS)[f][c // 2]

                for g in range(2):
                    pe.wait_ge(turned_lo[ln], 4 * g + 4)
                    for c in range(RING):
                        if g == 0:
                            pe.wait_ge(lo_done, n0 + c + 1)
                        last = columns_piece(n0 + c, bank_of(c), range(KD), slice(g * 2 * P, (g + 1) * 2 * P))
                        if g == 1:
                            last.then_inc(slab_done, 1)
                        elif c in (1, 2):
                            turn_normed(ln, c + 1)
                with pe.Fori(1, KF // 2) as i:
                    for c in range(RING):
                        pe.wait_ge(lo_done, i * RING + (n0 + c + 1))
                        pe.wait_ge((prod_done if c % 2 else silu_done)[f], i * 2 + (c // 2 - 1))
                        columns_piece(n0 + c, bank_of(c), range(KD)).then_inc(slab_done, 1)

            token_major(0, GLA_V, lambda half, t: 4 * half + t)
            pe.wait_ge(wg_ready, 2)
            pe.wait_ge(tok_out[0], 1)
            for k in range(KD):
                last = three(bank[0][:, :], wg_hi[:, k, :], wg_lo[:, k, :], t_hi[:, k, :], t_lo[:, k, :], k == 0, k == KD - 1)
            last.then_inc(low_done, 1)
            pe.wait_ge(low_out, 1)
            pe.wait_ge(small_full, 64)
            pe.wait_ge(tok_out[0], TILES)
            for hd in range(GLA_HEADS):
                nc.tensor.matmul(bank[hd][:, :], w_up[:, hd * GLA_DK:(hd + 1) * GLA_DK], g_low[:, :],
                                 start=True, stop=True).then_inc(up_done, 1)

            def r_free(half, t):
                if half == 0:
                    pe.wait_ge(tok_out[0], TILES + t + 1)
                else:
                    pe.wait_ge(abs_done, t + 1)
                    pe.wait_ge(min_done, t + 1)
            token_major(1, GLA_R, lambda half, t: 4 - 4 * half + t, r_free)
            for hd in range(GLA_HEADS):
                for is_k in range(2):
                    n = GLA_QK + 2 * hd + is_k
                    pe.wait_ge(lo_done, n + 1)
                    if hd < 2:
                        pe.wait_ge(tok_out[1], 2 * hd + is_k + 1)
                    else:
                        pe.wait_ge(qk_scaled, 3 * (hd - 2) + 1 + 2 * is_k)
                    columns_piece(n, 4 + 2 * (hd % 2) + is_k, range(KD)).then_inc(slab_done, 1)

            def ke_and_scores(t):
                toks = slice(t * P, (t + 1) * P)
                for hd in range(GLA_HEADS):
                    last = nc.tensor.transpose(bank[5][:, hd * P:(hd + 1) * P], g_ke[:, hd, toks], ident[:, :])
                last.then_inc(ke_turned, 1)
                for hd in range(GLA_HEADS):
                    last = nc.tensor.matmul(bank[4][:, hd * P:(hd + 1) * P], g_ki[:, hd, toks], g_q[:, hd, toks],
                                            start=True, stop=True)
                last.then_inc(sc_done, 1)

            def updates(c):
                t, rows = c // 2, slice((c % 2) * CHUNK, (c % 2 + 1) * CHUNK)
                banks = (6, 7) if c % 2 == 0 else (2, 3)
                for hd in range(GLA_HEADS):
                    last = nc.tensor.matmul(bank[banks[hd // 2]][:, (hd % 2) * GLA_DV:(hd % 2 + 1) * GLA_DV],
                                            g_kt[rows, t % 2, hd * GLA_DK:(hd + 1) * GLA_DK],
                                            g_v[rows, t, hd * GLA_DV:(hd + 1) * GLA_DV], start=True, stop=True)
                last.then_inc(upd_done, 1)

            def inter(c):
                rows = slice((c % 2) * CHUNK, (c % 2 + 1) * CHUNK)
                for hd in range(GLA_HEADS):
                    last = nc.tensor.matmul(bank[hd // 2][rows, (hd % 2) * GLA_DV:(hd % 2 + 1) * GLA_DV],
                                            g_q[:, hd, c * CHUNK:(c + 1) * CHUNK], g_state[:, c % 2, hd, :],
                                            start=False, stop=True, skip_group_check=True)
                last.then_inc(inter_done, 1)

            def turn_y(t):
                pe.wait_ge(y_done, t + 1)
                turn(GLA_YT, t, g_on, GLA_Y_BANKS)

            pe.wait_ge(consts, 10)
            pe.wait_ge(qk_scaled, 3 * GLA_HEADS)
            pe.wait_ge(tok_out[0], 2 * TILES)
            ke_and_scores(0)
            pe.wait_ge(tok_out[1], 2 * TILES)
            for t in range(TILES):
                pe.wait_ge(ke_out, t + 1)
                if t >= 1:
                    pe.wait_ge(state_done, 2 * t - 1)
                updates(2 * t)
                if t + 1 < TILES:
                    pe.wait_ge(sc_masked, t + 1)
                    ke_and_scores(t + 1)
                pe.wait_ge(sc_masked, t + 1)
                if t >= 1:
                    pe.wait_ge(o_out, t)
                for hd in range(GLA_HEADS):
                    last = nc.tensor.matmul(bank[hd // 2][:, (hd % 2) * GLA_DV:(hd % 2 + 1) * GLA_DV],
                                            g_am[:, t % 2, hd * P:(hd + 1) * P], g_v[:, t, hd * GLA_DV:(hd + 1) * GLA_DV],
                                            start=(hd % 2 == 0), stop=False, skip_group_check=True)
                last.then_inc(intra_done, 1)
                if t >= 1:
                    pe.wait_ge(state_done, 2 * t)
                    inter(2 * t)
                if t == TILES - 1:
                    pe.wait_ge(state_done, CHUNKS - 2)
                    turn_y(1)
                pe.wait_ge(state_done, 2 * t + 1)
                inter(2 * t + 1)
                if t + 1 < TILES:
                    updates(2 * t + 1)
                if t == TILES - 2:
                    pe.wait_ge(ke_out, TILES)
                    pe.wait_ge(sc_masked, TILES)
                    turn_y(0)
            pe.wait_ge(turned_lo[GLA_YT], 2)
            turn_y(2)

            def gla_out_free(t):
                if t == 0:
                    pe.wait_ge(state_done, CHUNKS - 1)
                pe.wait_ge(turned_lo[GLA_YT], 2 * t + 2)

            def gla_beside(k):
                if k == 1:
                    pe.wait_ge(o_out, TILES)
                    turn_y(3)
            out_projection(GLA_OUT, KD, t_hi, t_lo, 0, lambda k: None, gla_out_free, TAIL, gla_beside)
            feed_forward(0, FFN_IN[0], 0)

            def ffn_out(f, ln):
                def hidden_ready(k):
                    pe.wait_ge(a_lo_done[f], k + 1)

                def banks_free(t):
                    if t == 2:
                        pe.wait_ge(prod_done[f], KF)
                out_projection(FFN_OUT[f], KF, a_hi, a_lo, ln, hidden_ready, banks_free)
            ffn_out(0, 1)

            token_major(2, RPA_V, lambda half, t: RPA_V_BANKS[4 * half + t], behind_ln=1)

            def qk_pieces(p):
                for is_k in range(2):
                    n = RPA_QK + 2 * p + is_k
                    for k in range(KD):
                        yield n, is_k, k, p

            def qk_piece(n, is_k, k, p):
                if k == 0:
                    pe.wait_ge(lo_done, n + 1)
                    if p >= 1:
                        pe.wait_ge(rqk_lo, 2 * (p - 1) + is_k + 1)
                    else:
                        pe.wait_ge(tok_out[2], is_k + 3)
                last = columns_piece(n, is_k, [k])
                if k == KD - 1:
                    last.then_inc(slab_done, 1)

            def scores(s):
                p, hd, t = s // (2 * TILES), s // TILES % 2, s % TILES
                rows = slice(hd * RPA_D, (hd + 1) * RPA_D)
                toks = slice(t * P, (t + 1) * P)
                keys = (t + 1) * P
                out = bank[2 + s % 2]
                if s % (2 * TILES) == 0:
                    pe.wait_ge(rqk_lo, 2 * p + 2)
                    pe.wait_ge(bias_lo, p + 1)
                if s >= 2:
                    pe.wait_ge(exp_done, s - 1)
                three(out[:, 0:keys], r_q_hi[rows, p % 2, toks], r_q_lo[rows, p % 2, toks],
                      r_k_hi[rows, p % 2, 0:keys], r_k_lo[rows, p % 2, 0:keys], True, False, True)
                for back in range(min(t + 1, 2)):
                    blk = out[:, keys - (back + 1) * P:keys - back * P]
                    nc.tensor.matmul(blk, b_hi[:, p % 2, hd, back * P:(back + 1) * P], flip[:, :],
                                     start=False, stop=False, skip_group_check=True)
                    last = nc.tensor.matmul(blk, b_lo[:, p % 2, hd, back * P:(back + 1) * P], flip[:, :],
                                            start=False, stop=(back == min(t, 1)), skip_group_check=True)
                last.then_inc(s_done, 1)

            def turn_weights(s):
                t = s % TILES
                pe.wait_ge(exp_done, s + 1)
                if s >= 2:
                    pe.wait_ge(p_out, s - 1)
                for j in range(t + 1):
                    last = nc.tensor.transpose(bank[4 + s % 2][:, j * P:(j + 1) * P], r_p[:, s % 3, j * P:(j + 1) * P], ident[:, :])
                last.then_inc(p_turned, 1)

            def weights_v(s):
                hd, t = s // TILES, s % TILES
                pe.wait_ge(p_out, s + 1)
                if s >= 2:
                    pe.wait_ge(o_scaled, s - 1)
                for j in range(t + 1):
                    last = nc.tensor.matmul(bank[6 + s % 2][:, 0:RPA_D], r_pt[:, s % 3, j * P:(j + 1) * P],
                                            r_v[:, j, hd * RPA_D:(hd + 1) * RPA_D], start=(j == 0), stop=(j == t))
                last.then_inc(pv_done, 1)

            def turn_y(t):
                pe.wait_ge(o_scaled, UNITS - TILES + t + 1)
                turn(RPA_YT, t, r_o, RPA_Y_BANKS)

            for piece in qk_pieces(0):
                qk_piece(*piece)
            pe.wait_ge(flip_done, 1)
            pe.wait_ge(tok_out[2], 2 * TILES)
            for s in range(UNITS + 2):
                p, step = s // (2 * TILES), s % (2 * TILES)
                if s < UNITS:
                    scores(s)
                    if p + 1 < RPA_PAIRS:
                        if step == 0:
                            pieces = list(qk_pieces(p + 1))
                        for piece in pieces[(16 * step) // 7:(16 * (step + 1)) // 7]:
                            qk_piece(*piece)
                if 1 <= s <= UNITS:
                    turn_weights(s - 1)
                if s == UNITS + 1:
                    turn_y(0)
                    turn_y(1)
                if s >= 2:
                    weights_v(s - 2)

            def rpa_out_free(t):
                pe.wait_ge(turned_lo[RPA_YT], 2 * t + 2)

            def rpa_beside(k):
                if k < 2:
                    turn_y(k + 2)
            out_projection(RPA_OUT, KD, t_hi, t_lo, 2, lambda k: None, rpa_out_free, TAIL, rpa_beside)
            feed_forward(1, FFN_IN[1], 2)
            ffn_out(1, 3)


def _columns(w):
    m = w.shape[1] // P
    return w.reshape(KD, P, m, P).transpose(2, 1, 0, 3).reshape(m, P, SLAB)


def _rows(w):
    return w.reshape(-1, P, SLAB)


def _token_major(w):
    return w.reshape(KD // 2, 2, P, 2, HALF).transpose(3, 0, 2, 1, 4).reshape(KD, P, SLAB)


def _paired(x, y):
    return np.stack([x, y], axis=1).reshape(-1, P, SLAB)


def kernel(x, gla_w_in, gla_w_gate_up, gla_b_gate, gla_norm_g, gla_w_out,
           rpa_w_in, rpa_rel_bias, rpa_w_out,
           mla_w_in, mla_q_norm_g, mla_kv_norm_g, mla_w_uq, mla_w_ukv, mla_w_out,
           ffn_w_in, ffn_w_out, ln_g, ln_b):
    import concourse.bacc as bacc
    from concourse.bass_utils import run_bass_kernel_spmd

    x2 = np.asarray(x)[0]
    g_in = np.asarray(gla_w_in)[0]
    q_end, k_end = GLA_HK, 2 * GLA_HK
    v_end, r_end = k_end + GLA_HV, k_end + 2 * GLA_HV
    r_in = np.asarray(rpa_w_in)[0]
    ffn_in, ffn_out = np.asarray(ffn_w_in), np.asarray(ffn_w_out)

    def ffn(i):
        return [_paired(_columns(ffn_in[i][:, :FFN]), _columns(ffn_in[i][:, FFN:])), _rows(ffn_out[i])]

    stream = np.concatenate(
        [_token_major(g_in[:, k_end:v_end]), _token_major(g_in[:, v_end:r_end]),
         _paired(_columns(g_in[:, :q_end]), _columns(g_in[:, q_end:k_end])), _rows(np.asarray(gla_w_out)[0])]
        + ffn(0)
        + [_token_major(r_in[:, 2 * D_MODEL:]),
           _paired(_columns(r_in[:, :D_MODEL]), _columns(r_in[:, D_MODEL:2 * D_MODEL])), _rows(np.asarray(rpa_w_out)[0])]
        + ffn(1))
    assert stream.shape == (SLABS, P, SLAB)
    rel = np.asarray(rpa_rel_bias)[0]
    last = rel[:, 2 * RPA_MAX_REL:]
    arrays = {
        "stream": np.ascontiguousarray(stream.reshape(SLABS // 2, 2, P, SLAB).transpose(0, 2, 1, 3)),
        "x": np.ascontiguousarray(x2),
        "x_t": np.ascontiguousarray(x2.T.reshape(KD, P, SEQ).transpose(1, 0, 2)),
        "w_gate_down": np.ascontiguousarray(g_in[:, r_end:].reshape(KD, P, GLA_RANK).transpose(1, 0, 2)),
        "w_gate_up": np.ascontiguousarray(np.asarray(gla_w_gate_up)[0]),
        "b_gate": np.ascontiguousarray(np.asarray(gla_b_gate)[0].reshape(GLA_HEADS, P).T),
        "norm_g": np.ascontiguousarray(np.asarray(gla_norm_g)[0]),
        "rel_bias": np.ascontiguousarray(np.concatenate([rel, np.repeat(last, 3 * P - rel.shape[1], axis=1)], axis=1)),
        "far_bias": np.ascontiguousarray(last[:, 0]),
        "ln_gb": np.ascontiguousarray(np.stack([np.asarray(ln_g), np.asarray(ln_b)], axis=2).reshape(2 * DEPTH, 2, D_MODEL)),
    }
    nc = bacc.Bacc("TRN2", target_bir_lowering=False, num_devices=1)
    aps = {n: nc.dram_tensor(n, v.shape, mybir.dt.from_np(v.dtype), kind="ExternalInput").ap() for n, v in arrays.items()}
    aps["out"] = nc.dram_tensor("out", (SEQ, D_MODEL), F32, kind="ExternalOutput").ap()
    build_program(nc, aps)
    r = run_bass_kernel_spmd(nc, [arrays], core_ids=[0])
    return r.results[0]["out"].reshape(1, SEQ, D_MODEL)
```

```python
from contextlib import ExitStack

import numpy as np
import concourse.bass as bass
from concourse import mybir

F32 = mybir.dt.float32
F32R = mybir.dt.float32r
I32 = mybir.dt.int32
ALU = mybir.AluOpType
ACT = mybir.ActivationFunctionType
AX = mybir.AxisListType

P = 128
D_MODEL = 1024
SEQ = 512
DEPTH = 2
CHUNK = 64
ALPHA = (2 * DEPTH) ** 0.25
LN_EPS = 1e-5
NEG_INF = -1e30

KD = D_MODEL // P
TILES = SEQ // P
HALF = 512
CHUNKS = SEQ // CHUNK

GLA_HEADS = 4
GLA_DK = D_MODEL // 2 // GLA_HEADS
GLA_DV = D_MODEL // GLA_HEADS
GLA_RANK = 16
LOW = 32
GLA_TAU = 16.0
GLA_HK = GLA_HEADS * GLA_DK
GLA_HV = GLA_HEADS * GLA_DV

RPA_HEADS = 16
RPA_D = D_MODEL // RPA_HEADS
RPA_PAIRS = RPA_HEADS // 2
RPA_MAX_REL = 128
BIAS_ROW = 3 * P

FFN = -(-8 * D_MODEL // (3 * 256)) * 256
KF = FFN // P

SLAB = 1024
RING = 4
RAWS = 2

GLA_V = 0
GLA_R = GLA_V + KD
GLA_QK = GLA_R + KD
GLA_OUT = GLA_QK + 2 * GLA_HEADS
FFN_IN = [GLA_OUT + KD, 0]
FFN_OUT = [FFN_IN[0] + 2 * KF, 0]
RPA_V = FFN_OUT[0] + KF
RPA_KQ = RPA_V + KD
RPA_OUT = RPA_KQ + 2 * RPA_PAIRS
FFN_IN[1] = RPA_OUT + KD
FFN_OUT[1] = FFN_IN[1] + 2 * KF
SLABS = FFN_OUT[1] + KF
TAIL = 4


def build_program(nc, a):
    ctx = ExitStack()
    with ctx:
        place = [(nc.sbuf_base + 31) // 32 * 32]

        def sb_at(name, shape, dt, offset):
            return nc.alloc_sbuf_tensor_at("s_" + name, shape, dt, offset=offset)

        def sb(name, shape, dt=F32):
            size = 4
            for s in shape[1:]:
                size *= s
            at = place[0]
            place[0] += (size + 31) // 32 * 32
            return sb_at(name, shape, dt, at)

        def sem(name):
            return ctx.enter_context(nc.semaphore(name))

        raw = sb("raw", [P, RAWS, 2, SLAB])
        w_hi = sb("w_hi", [P, RING, SLAB], F32R)
        w_lo = sb("w_lo", [P, RING, SLAB], F32R)
        t_hi = sb("t_hi", [P, KD, SEQ], F32R)
        t_lo = sb("t_lo", [P, KD, SEQ], F32R)
        h = sb("h", [P, TILES, D_MODEL])
        gb_at = place[0]
        ln_gb = sb("ln_gb", [P, 2, D_MODEL])
        region = place[0]
        a_hi = sb("a_hi", [P, KF, SEQ], F32R)
        a_lo = sb("a_lo", [P, KF, SEQ], F32R)
        region_end = place[0]
        gate_at = place[0]
        gate_s = sb("gate_s", [P, 2, SEQ])
        prod_at = place[0]
        prod = sb("prod", [P, 2, SEQ])
        prod_end = place[0]
        ident = sb("ident", [P, P])
        causal = sb("causal", [P, GLA_HEADS, P])
        minus_half = sb("minus_half", [P, GLA_HEADS])
        half_sum = sb("half_sum", [P, TILES, 2])
        neg_mean = sb("neg_mean", [P, TILES])
        sq_sum = sb("sq_sum", [P, TILES])
        bn = sb("bn", [P, TILES, 12])
        mv = sb("mv", [P, TILES, 2])
        var_eps = sb("var_eps", [P, TILES])
        rstd = sb("rstd", [P, TILES])
        bn_o = sb("bn_o", [P, TILES, GLA_HEADS, 6])
        mv_o = sb("mv_o", [P, TILES, GLA_HEADS, 2])
        var_eps_o = sb("var_eps_o", [P, TILES, GLA_HEADS])
        rstd_o = sb("rstd_o", [P, TILES, GLA_HEADS])
        shift_o = sb("shift_o", [P, TILES, GLA_HEADS])
        decay = sb("decay", [P, GLA_HEADS * CHUNKS])
        b_gate = sb("b_gate", [P, GLA_HEADS])
        far_bias = sb("far_bias", [P, RPA_HEADS])
        UNITS = RPA_HEADS * TILES
        neg_max = sb("neg_max", [P, UNITS])
        row_sum = sb("row_sum", [P, UNITS])
        inv_sum = sb("inv_sum", [P, UNITS])

        def carve(start, end):
            at = [start]

            def get(name, shape, dt=F32):
                size = 4
                for s in shape[1:]:
                    size *= s
                t = sb_at(name, shape, dt, at[0])
                at[0] += size
                assert at[0] <= end, name
                return t
            return get, at

        get, at = carve(region, region_end)
        g_v = get("g_v", [P, TILES, D_MODEL])
        g_q = get("g_q", [P, GLA_HEADS, SEQ])
        g_ki = get("g_ki", [P, GLA_HEADS, SEQ])
        g_ke = get("g_ke", [P, GLA_HEADS, SEQ])
        rg_at = at[0]
        g_rg = get("g_rg", [P, TILES, D_MODEL])
        on_at = at[0]
        g_on = get("g_on", [P, TILES, D_MODEL])
        kt_at = at[0]
        g_kt = get("g_kt", [P, 2, GLA_HK])
        g_state = get("g_state", [P, 2, GLA_HEADS, GLA_DV])
        g_am = get("g_am", [P, 2, GLA_HEADS * P])
        get, _ = carve(rg_at, region_end)
        wg = get("wg", [P, KD, P], F32R)
        wg_raw = get("wg_raw", [P, KD, GLA_RANK])
        get, _ = carve(on_at, region_end)
        x_t = get("x_t", [P, KD, SEQ])
        get, _ = carve(on_at, region_end)
        g_e = get("g_e", [P, GLA_HEADS, SEQ])
        g_c = get("g_c", [P, GLA_HEADS, SEQ])
        get, _ = carve(kt_at, region_end)
        w_up = get("w_up", [GLA_RANK, GLA_HK])
        g_part = get("g_part", [P, SEQ])
        low_rows = get("low_rows", [P, SEQ], F32R)
        up_rows = get("up_rows", [P, GLA_HK], F32R)
        norm_g = sb_at("norm_g", [P, D_MODEL], F32, gate_at)
        keep = sb_at("keep", [P, SEQ], F32, prod_at)
        squared = sb_at("squared", [P, D_MODEL], F32, gate_at)
        centred = sb_at("centred", [P, D_MODEL], F32, prod_at)
        get, _ = carve(region, prod_end)
        r_v = get("r_v", [P, TILES, RPA_HEADS, 2, RPA_D], F32R)
        r_q = get("r_q", [P, 2, 2, SEQ], F32R)
        r_k_hi = get("r_k_hi", [P, 2, 2, SEQ], F32R)
        r_k_lo = get("r_k_lo", [P, 2, 2, SEQ], F32R)
        r_b = get("r_b", [P, 2, 2, 2 * P])
        pt_hi = get("pt_hi", [P, TILES * (TILES + 1), P], F32R)
        pt_lo = get("pt_lo", [P, TILES * (TILES + 1), P], F32R)
        r_o = get("r_o", [P, RPA_PAIRS - 1, SEQ])
        r_half = get("r_half", [P, SEQ])
        get, _ = carve(gb_at, region)
        r_p = get("r_p", [P, 4, SEQ])
        assert place[0] <= nc.sbuf_usable_end, (place[0], nc.sbuf_usable_end)

        bank = [ctx.enter_context(nc.psum_tensor(f"bank{i}", [P, HALF], F32)) for i in range(8)]

        raw_full = [sem(f"raw_full{i}") for i in range(RAWS)]
        first_full = [sem(f"first_full{i}") for i in range(5)]
        first_hi = sem("first_hi")
        first_lo = sem("first_lo")
        hi_done = sem("hi_done")
        lo_done = sem("lo_done")
        slab_done = sem("slab_done")
        consts = sem("consts")
        x_full = [sem(f"x_full{i}") for i in range(3)]
        x_hi = sem("x_hi")
        x_lo = sem("x_lo")
        h_full = sem("h_full")
        small_full = sem("small_full")
        gb_full = sem("gb_full")
        dve_step = sem("dve_step")
        pool_step = sem("pool_step")
        act_step = sem("act_step")
        out_full = sem("out_full")
        acc_done = [sem(f"acc_done{n}") for n in range(4)]
        stats = [sem(f"stats{n}") for n in range(4)]
        mean_done = sem("mean_done")
        squares = sem("squares")
        rstd_done = [sem(f"rstd_done{n}") for n in range(4)]
        normed = [sem(f"normed{n}") for n in range(4)]
        turned = [sem(f"turned{n}") for n in range(4)]
        turned_hi = [sem(f"turned_hi{n}") for n in range(4)]
        turned_lo = [sem(f"turned_lo{n}") for n in range(4)]
        silu_done = [sem(f"silu_done{n}") for n in range(2)]
        prod_done = [sem(f"prod_done{n}") for n in range(2)]
        a_hi_done = [sem(f"a_hi_done{n}") for n in range(2)]
        a_lo_done = [sem(f"a_lo_done{n}") for n in range(2)]
        tok_done = [sem(f"tok_done{n}") for n in range(3)]
        tok_out = [sem(f"tok_out{n}") for n in range(3)]
        wg_hi_done = sem("wg_hi_done")
        wg_lo_done = sem("wg_lo_done")
        up_hi_done = sem("up_hi_done")
        up_lo_done = sem("up_lo_done")
        low_done = sem("low_done")
        low_part = sem("low_part")
        low_sum = sem("low_sum")
        low_hi_done = sem("low_hi_done")
        low_lo_done = sem("low_lo_done")
        up_done = sem("up_done")
        abs_done = sem("abs_done")
        min_done = sem("min_done")
        log_done = sem("log_done")
        cum_done = sem("cum_done")
        rest_done = sem("rest_done")
        exps_done = sem("exps_done")
        rg_done = sem("rg_done")
        qk_scaled = sem("qk_scaled")
        zeroed = sem("zeroed")
        ke_turned = sem("ke_turned")
        ke_out = sem("ke_out")
        sc_done = sem("sc_done")
        sc_masked = sem("sc_masked")
        upd_done = sem("upd_done")
        state_done = sem("state_done")
        intra_done = sem("intra_done")
        inter_done = sem("inter_done")
        o_stats = sem("o_stats")
        o_rstd = sem("o_rstd")
        shift_done = sem("shift_done")
        o_raw = sem("o_raw")
        o_out = sem("o_out")
        y_done = sem("y_done")
        rows_full = sem("rows_full")
        far_full = sem("far_full")
        bias_full = [sem("bias_full0"), sem("bias_full1")]
        bias_ready = sem("bias_ready")
        s_biased = sem("s_biased")
        k_hi_done = sem("k_hi_done")
        k_lo_done = sem("k_lo_done")
        k_twice = sem("k_twice")
        q_hi_done = sem("q_hi_done")
        q_lo_done = sem("q_lo_done")
        s_done = sem("s_done")
        max_done = sem("max_done")
        exp_done = sem("exp_done")
        v_lo_done = sem("v_lo_done")
        inverted = sem("inverted")
        p_scaled = sem("p_scaled")
        p_turned = sem("p_turned")
        p_hi = sem("p_hi")
        p_lo = sem("p_lo")
        pv_done = sem("pv_done")
        o_half = sem("o_half")
        o_summed = sem("o_summed")
        o_hi = sem("o_hi")
        o_lo = sem("o_lo")
        last_hi = sem("last_hi")
        last_lo = sem("last_lo")

        block = ctx.enter_context(nc.Block())

        GLA_YT = 3
        LN_BANKS = [[(6, 7), (2, 3), (4, 5), (0, 1)], [(4, 5), (0, 1), (2, 3), (6, 7)],
                    [(0, 1), (2, 3), (4, 5), (6, 7)], [(4, 5), (6, 7), (0, 1), (2, 3)]]
        GLA_Y_BANKS = [(4, 5), (2, 3), (4, 5), (0, 1)]
        FIRST = [(True, 0, slice(0, HALF)), (False, 0, slice(0, SEQ // 2)), (False, 0, slice(SEQ // 2, SEQ)),
                 (True, 1, slice(HALF, SLAB)), (False, 1, slice(0, SEQ))]
        GATE_BANKS, UP_BANKS = [(6, 7), (0, 1)], [(2, 3), (2, 3)]
        V_HEADS = HALF // RPA_D
        RPA_V_BANKS = [4, 5, 0, 1, 2, 3, 6, 7]

        def own_half(hd):
            return slice(hd * RPA_D, (hd + 1) * RPA_D)

        def other_half(hd):
            return own_half(1 - hd)

        def weight_blocks(s):
            hd, t = s // TILES % 2, s % TILES
            if hd == 0:
                return slice(t + 1, t + 1 + 5 * t + 1, 5)
            return slice(15 - 5 * t, 15 + t + 1, 6)

        def key_blocks(hd, j):
            return slice(6 * j + 1, 5 * j + 5) if hd == 0 else slice(15 - 5 * j, 19 - 6 * j)

        @block.sync
        def _(sp):
            def load_pair(pair, slot):
                sp.dma_start(raw[:, slot, :, :], a["stream"][pair]).then_inc(raw_full[slot], 16)

            for i, (of_slab, j, cols) in enumerate(FIRST):
                if of_slab:
                    sp.dma_start(raw[:, 0, 0, cols], a["stream"][0][:, 0, cols]).then_inc(first_full[i], 16)
                else:
                    sp.dma_start(x_t[:, j, cols], a["x_t"][:, j, cols]).then_inc(first_full[i], 16)
            sp.dma_start(raw[:, 0, 1, :], a["stream"][0][:, 1, :]).then_inc(raw_full[0], 16)
            for i in range(3):
                sp.dma_start(x_t[:, 2 * i + 2:2 * i + 4, :], a["x_t"][:, 2 * i + 2:2 * i + 4, :]).then_inc(x_full[i], 16)
                if i == 0:
                    load_pair(1, 1)
            sp.dma_start(wg_raw[:, :, :], a["w_gate_down"]).then_inc(small_full, 16)
            sp.dma_start(w_up[:, :], a["w_gate_up"]).then_inc(small_full, 16)
            sp.dma_start(b_gate[:, :], a["b_gate"]).then_inc(small_full, 16)
            sp.dma_start(norm_g[:, :], a["norm_g"].partition_broadcast(P)).then_inc(small_full, 16)
            sp.dma_start(h[:, :, :], a["x"].rearrange("(t p) d -> p t d", p=P)).then_inc(h_full, 16)
            with sp.Fori(1, SLABS // (2 * RAWS)) as i:
                for slot in range(RAWS):
                    sp.wait_ge(hi_done, i * (2 * RAWS) + (2 * slot + 2 - 2 * RAWS))
                    sp.wait_ge(lo_done, i * (2 * RAWS) + (2 * slot + 2 - 2 * RAWS))
                    load_pair(i * RAWS + slot, slot)
            for t in range(TILES - 1):
                sp.wait_ge(normed[3], t + 1)
                sp.dma_start(a["out"][t * P:(t + 1) * P, :], h[:, t, :]).then_inc(out_full, 16)
            for half in range(2):
                sp.wait_ge(normed[3], TILES + half)
                cols = slice(half * HALF, (half + 1) * HALF)
                sp.dma_start(a["out"][(TILES - 1) * P:, cols], h[:, TILES - 1, cols]).then_inc(out_full, 16)
            sp.wait_ge(out_full, 16 * (TILES + 1))

        @block.scalar
        def _(act):
            def split_hi(n, i=None):
                if n >= SLABS:
                    return
                pair = n // 2
                more = 0 if i is None else i
                act.wait_ge(raw_full[pair % RAWS], more * 16 + 16 * (pair // RAWS + 1))
                if n >= RING:
                    act.wait_ge(slab_done, more * RING + (n - RING + 1))
                nc.scalar.activation(w_hi[:, n % RING, :], raw[:, pair % RAWS, n % 2, :],
                                     ACT.Copy).then_inc(hi_done, 2 if n == 1 else 1)

            def turned_high(which, t, banks):
                for half in range(2):
                    act.wait_ge(turned[which], 2 * t + half + 1)
                    nc.scalar.activation(
                        t_hi[:, 4 * half:4 * half + 4, t * P:(t + 1) * P],
                        bank[banks[t][half]][:, :].rearrange("p (k c) -> p k c", k=4),
                        ACT.Copy).then_inc(turned_hi[which], 1)

            def load_gb(n):
                if n > 0:
                    act.wait_ge(normed[n - 1], TILES)
                act.dma_start(ln_gb[:, :, :], a["ln_gb"][n].partition_broadcast(P)).then_inc(gb_full, 16)

            def token_major(which, n0, bank_of, copy_out):
                for half in range(2):
                    for k in range(KD // 2):
                        n = n0 + half * (KD // 2) + k
                        split_hi(n + RING)
                    for t in range(TILES):
                        if t < TILES - 1:
                            act.wait_ge(tok_done[which], half * (TILES - 1) + t + 1)
                        else:
                            act.wait_ge(slab_done, n0 + (half + 1) * (KD // 2))
                        copy_out(half, t, bank[bank_of(half, t)]).then_inc(tok_out[which], 1)

            def out_projection(n0, slabs, ln):
                banks = LN_BANKS[ln]
                for k in range(slabs - TAIL):
                    split_hi(n0 + k + RING)
                behind = n0 + slabs - TAIL + RING
                if ln == 3:
                    for t in range(TILES):
                        act.wait_ge(mean_done, t + 1)
                        nc.scalar.activation(squared[:, :], h[:, t, :], ACT.Square, bias=neg_mean[:, t:t + 1],
                                             accum_out=sq_sum[:, t:t + 1]).then_inc(squares, 1)
                    return
                turned_high(ln, 0, banks)
                split_hi(behind)
                split_hi(behind + 1)
                turned_high(ln, 1, banks)
                split_hi(behind + 2)
                split_hi(behind + 3)
                turned_high(ln, 2, banks)
                turned_high(ln, 3, banks)

            def feed_forward(f, n0):
                def body(i, first):
                    for c in range(2):
                        act.wait_ge(slab_done, i * RING + (n0 + 2 * c + 1))
                        if not first:
                            act.wait_ge(prod_done[f], i * 2 + (c - 1))
                        nc.scalar.activation(gate_s[:, c, :], bank[GATE_BANKS[f][c]][:, :], ACT.Silu).then_inc(silu_done[f], 1)
                        split_hi(n0 + 2 * c + RING, i)
                        split_hi(n0 + 2 * c + 1 + RING, i)
                        act.wait_ge(prod_done[f], i * 2 + (c + 1))
                        nc.scalar.activation(a_hi[:, bass.ds(i * 2 + c, 1), :], prod[:, bass.ds(c, 1), :],
                                             ACT.Copy).then_inc(a_hi_done[f], 1)
                body(0, True)
                with act.Fori(1, KF // 2) as i:
                    body(i, False)

            for i, (of_slab, j, cols) in enumerate(FIRST):
                act.wait_ge(first_full[i], 16)
                if of_slab:
                    nc.scalar.activation(w_hi[:, 0, cols], raw[:, 0, 0, cols], ACT.Copy).then_inc(first_hi, 1)
                else:
                    nc.scalar.activation(t_hi[:, j, cols], x_t[:, j, cols], ACT.Copy).then_inc(first_hi, 1)
            act.wait_ge(first_hi, len(FIRST))
            for i in range(3):
                split_hi(i + 1)
                act.wait_ge(x_full[i], 16)
                chunks = slice(2 * i + 2, 2 * i + 4)
                nc.scalar.activation(t_hi[:, chunks, :], x_t[:, chunks, :], ACT.Copy).then_inc(x_hi, 1)
            load_gb(0)
            act.wait_ge(small_full, 64)
            act.wait_ge(zeroed, 3)
            nc.scalar.activation(wg[:, :, 0:GLA_RANK], wg_raw[:, :, :], ACT.Copy).then_inc(wg_hi_done, 1)
            for group in (0, 2):
                nc.scalar.activation(up_rows[group * LOW:group * LOW + GLA_RANK, :], w_up[:, :], ACT.Copy).then_inc(up_hi_done, 1)

            token_major(0, GLA_V, lambda half, t: 4 * half + t, lambda half, t, b: nc.scalar.activation(
                g_v[:, t, half * HALF:(half + 1) * HALF], b[:, :], ACT.Copy))
            act.wait_ge(low_done, 1)
            nc.scalar.activation(g_part[LOW:LOW + GLA_RANK, :], bank[0][0:GLA_RANK, :], ACT.Copy).then_inc(low_part, 1)
            act.wait_ge(low_sum, 1)
            for group in (0, 1):
                nc.scalar.activation(low_rows[group * LOW:group * LOW + GLA_RANK, :], g_part[0:GLA_RANK, :],
                                     ACT.Copy).then_inc(low_hi_done, 1)
            for hd in range(GLA_HEADS):
                act.wait_ge(up_done, hd + 1)
                nc.scalar.activation(g_e[:, hd, :], bank[hd][:, :], ACT.Abs, bias=b_gate[:, hd:hd + 1]).then_inc(abs_done, 1)
            act.wait_ge(abs_done, GLA_HEADS)
            nc.scalar.activation(g_e[:, :, :], g_e[:, :, :], ACT.Exp, scale=-1.0).then_inc(act_step, 1)
            act.wait_ge(act_step, 1)
            nc.scalar.activation(g_e[:, :, :], g_e[:, :, :], ACT.Ln, bias=1.0).then_inc(log_done, 1)
            split_hi(GLA_R + RING)
            act.wait_ge(cum_done, GLA_HEADS)
            nc.scalar.activation(g_q[:, :, :], g_c[:, :, :], ACT.Exp, scale=1.0 / GLA_TAU).then_inc(exps_done, 1)
            split_hi(GLA_R + 1 + RING)
            nc.scalar.activation(g_ki[:, :, :], g_c[:, :, :], ACT.Exp, scale=-1.0 / GLA_TAU).then_inc(exps_done, 1)
            chunk_ends = g_c[:, :, :].rearrange("p h (c i) -> p (h c) i", i=CHUNK)[:, :, CHUNK - 1]
            nc.scalar.activation(decay[:, :], chunk_ends, ACT.Exp, scale=1.0 / GLA_TAU).then_inc(exps_done, 1)
            act.wait_ge(rest_done, 1)
            nc.scalar.activation(g_ke[:, :, :], g_e[:, :, :], ACT.Exp, scale=1.0 / GLA_TAU).then_inc(exps_done, 1)
            for half in range(2):
                for k in range(KD // 2):
                    n = GLA_R + half * (KD // 2) + k
                    if n >= GLA_R + 2:
                        split_hi(n + RING)
                for t in range(TILES):
                    if t < TILES - 1:
                        act.wait_ge(tok_done[1], half * (TILES - 1) + t + 1)
                    else:
                        act.wait_ge(slab_done, GLA_R + (half + 1) * (KD // 2))
                    nc.scalar.activation(g_rg[:, t, half * HALF:(half + 1) * HALF],
                                         bank[4 - 4 * half + t][:, :], ACT.Silu).then_inc(tok_out[1], 1)
            for n in range(GLA_QK, GLA_OUT):
                split_hi(n + RING)
            def ke_tile_out(t):
                act.wait_ge(ke_turned, t + 1)
                if t >= 2:
                    act.wait_ge(upd_done, 2 * (t - 2) + 2)
                nc.scalar.activation(g_kt[:, t % 2, :], bank[5][:, :], ACT.Copy).then_inc(ke_out, 1)

            def normalise_o(t):
                act.wait_ge(shift_done, t + 1)
                for hd in range(GLA_HEADS):
                    if t < TILES - 1:
                        o = g_on[:, t, hd * GLA_DV:(hd + 1) * GLA_DV]
                    else:
                        o = bank[hd // 2][:, (hd % 2) * GLA_DV:(hd % 2 + 1) * GLA_DV]
                    last = nc.scalar.activation(g_on[:, t, hd * GLA_DV:(hd + 1) * GLA_DV], o, ACT.Identity,
                                                bias=shift_o[:, t, hd:hd + 1], scale=rstd_o[:, t, hd:hd + 1])
                last.then_inc(o_out, 1)

            def copy_o(t):
                act.wait_ge(inter_done, 2 * t + 1)
                for half in range(2):
                    nc.scalar.activation(g_on[:, t, half * HALF:(half + 1) * HALF], bank[half][:, :], ACT.Copy).then_inc(o_raw, 1)
                act.wait_ge(o_raw, 2 * t + 2)

            ke_tile_out(0)
            for t in range(TILES):
                if t + 1 < TILES:
                    ke_tile_out(t + 1)
                else:
                    for done in range(2):
                        turned_high(GLA_YT, done, GLA_Y_BANKS)
                if t < TILES - 1:
                    copy_o(t)
                normalise_o(t)
            turned_high(GLA_YT, TILES - 2, GLA_Y_BANKS)
            turned_high(GLA_YT, TILES - 1, GLA_Y_BANKS)
            out_projection(GLA_OUT, KD, 0)
            load_gb(1)
            act.dma_start(a["bias_rows"], bass.AP(a["rel_bias"].tensor, 0, [[BIAS_ROW, RPA_HEADS], [0, P], [1, BIAS_ROW]])
                          ).then_inc(rows_full, 16)
            feed_forward(0, FFN_IN[0])
            out_projection(FFN_OUT[0], KF, 1)

            def load_bias(p):
                if p >= 2:
                    act.wait_ge(s_biased, 2 * TILES * (p - 1))
                for hd in range(2):
                    start = (2 * p + hd) * P * BIAS_ROW + P - 1
                    act.dma_start(r_b[:, p % 2, hd, :], bass.AP(a["bias_rows"].tensor, start, [[BIAS_ROW - 1, P], [1, 2 * P]])
                                  ).then_inc(bias_full[p % 2], 16)

            def k_high(p, hd):
                act.wait_ge(slab_done, RPA_KQ + 2 * p + 1)
                if p >= 2:
                    act.wait_ge(s_done, 2 * TILES * (p - 1))
                for out_rows in (own_half(hd), other_half(hd)):
                    nc.scalar.activation(r_k_hi[out_rows, p % 2, hd, :], bank[0][own_half(hd), :], ACT.Copy).then_inc(k_hi_done, 1)

            def k_low_twice(p, hd):
                act.wait_ge(k_lo_done, 2 * p + hd + 1)
                nc.scalar.activation(r_k_lo[other_half(hd), p % 2, hd, :], r_k_lo[own_half(hd), p % 2, hd, :].bitcast(F32),
                                     ACT.Copy).then_inc(k_twice, 1)

            def q_high(p, hd):
                act.wait_ge(slab_done, RPA_KQ + 2 * p + 2)
                rows = own_half(hd)
                nc.scalar.activation(r_q[rows, p % 2, hd, :], bank[1][rows, :], ACT.Copy, scale=RPA_D ** -0.5).then_inc(q_hi_done, 1)

            def head_half(hd):
                act.wait_ge(pv_done, hd + 1)
                if hd >= 2:
                    act.wait_ge(o_summed, hd - 1)
                own, other = own_half(hd % 2), other_half(hd % 2)
                nc.scalar.activation(r_half[own, :], bank[6 + hd % 2][other, :], ACT.Copy).then_inc(o_half, 1)

            act.wait_ge(rows_full, 16)
            act.dma_start(far_bias[:, :], a["far_bias"].partition_broadcast(P)).then_inc(far_full, 16)
            load_bias(0)
            load_bias(1)
            token_major(2, RPA_V, lambda half, t: RPA_V_BANKS[4 * half + t], lambda half, t, b: nc.scalar.activation(
                r_v[:, t, V_HEADS * half:V_HEADS * (half + 1), 0, :], b[:, :].rearrange("p (h d) -> p h d", d=RPA_D), ACT.Copy))
            for hd in range(2):
                k_high(0, hd)
            split_hi(RPA_KQ + RING)
            for hd in range(2):
                k_low_twice(0, hd)
            for hd in range(2):
                q_high(0, hd)
            split_hi(RPA_KQ + 1 + RING)

            def weights_high(s):
                hd, t = s // TILES, s % TILES
                act.wait_ge(p_turned, s + 1)
                if hd >= 2 and t == 0:
                    act.wait_ge(pv_done, hd - 1)
                nc.scalar.activation(pt_hi[:, weight_blocks(s), :],
                                     bank[4 + s % 2][:, 0:(t + 1) * P].rearrange("p (j c) -> p j c", c=P),
                                     ACT.Copy).then_inc(p_hi, 1)

            def pair_high(p):
                if p == 0:
                    act.wait_ge(slab_done, RPA_OUT)
                act.wait_ge(o_summed, 2 * p + 2)
                nc.scalar.activation(t_hi[:, p, :], r_o[:, p, :], ACT.Copy).then_inc(o_hi, 1)

            def last_pair_high(hd):
                rows = own_half(hd)
                act.wait_ge(o_summed, RPA_HEADS - 1 + hd)
                nc.scalar.activation(t_hi[rows, RPA_PAIRS - 1, :], r_o[rows, 0, :], ACT.Copy).then_inc(last_hi, 1)

            PAIR_HIGH = UNITS - 2 * TILES - 2
            act.wait_ge(normed[1], TILES)
            for s in range(UNITS + 2):
                p, step, t = s // (2 * TILES), s % (2 * TILES), s % TILES
                if s < UNITS:
                    act.wait_ge(max_done, s + 1)
                    if s >= 4:
                        act.wait_ge(p_turned, s - 3)
                    nc.scalar.activation(r_p[:, s % 4, 0:(t + 1) * P], bank[2 + s % 2][:, 0:(t + 1) * P], ACT.Exp,
                                         bias=neg_max[:, s:s + 1], accum_out=row_sum[:, s:s + 1]).then_inc(exp_done, 1)
                ahead = p + 1 < RPA_PAIRS
                if ahead and step == 3:
                    k_high(p + 1, 0)
                if ahead and step == 6:
                    q_high(p + 1, 0)
                if s >= 2:
                    weights_high(s - 2)
                if ahead and step == 3:
                    k_high(p + 1, 1)
                    split_hi(RPA_KQ + 2 * (p + 1) + RING)
                if ahead and step in (4, 5):
                    k_low_twice(p + 1, step - 4)
                if ahead and step == 6:
                    q_high(p + 1, 1)
                    split_hi(RPA_KQ + 2 * (p + 1) + 1 + RING)
                if s >= 2 * TILES and t == 0 and s < UNITS:
                    head_half(s // TILES - 2)
                if p >= 1 and step == 1 and p + 1 < RPA_PAIRS:
                    load_bias(p + 1)
                if 0 <= s - PAIR_HIGH < RPA_PAIRS - 2:
                    pair_high(s - PAIR_HIGH)
                if s == UNITS - 2:
                    pair_high(RPA_PAIRS - 2)
            act.wait_ge(p_turned, UNITS)
            load_gb(2)
            head_half(RPA_HEADS - 2)
            last_pair_high(0)
            head_half(RPA_HEADS - 1)
            last_pair_high(1)
            out_projection(RPA_OUT, KD, 2)
            load_gb(3)
            feed_forward(1, FFN_IN[1])
            out_projection(FFN_OUT[1], KF, 3)

        @block.gpsimd
        def _(pool):
            steps = [0]

            def own(ins):
                steps[0] += 1
                ins.then_inc(pool_step, 1)
                pool.wait_ge(pool_step, steps[0])

            def split_lo(n, i=None):
                if n >= SLABS:
                    return
                more = 0 if i is None else i
                pair = n // 2
                pool.wait_ge(hi_done, more * RING + (n + 1))
                nc.gpsimd.tensor_tensor(w_lo[:, n % RING, :], raw[:, pair % RAWS, n % 2, :],
                                        w_hi[:, n % RING, :].bitcast(F32), ALU.subtract
                                        ).then_inc(lo_done, 2 if n == 1 else 1)

            def ln_rstd(ln, t):
                if ln == 3:
                    pool.wait_ge(squares, t + 1)
                    own(nc.gpsimd.tensor_scalar(var_eps[:, t:t + 1], sq_sum[:, t:t + 1], 1.0 / D_MODEL, LN_EPS, ALU.mult, ALU.add))
                else:
                    pool.wait_ge(stats[ln], t + 1)
                    own(nc.gpsimd.tensor_scalar(var_eps[:, t:t + 1], mv[:, t, 1:2], LN_EPS, None, ALU.add))
                nc.gpsimd.tensor_tensor(rstd[:, t:t + 1], var_eps[:, t:t + 1], minus_half[:, 0:1], ALU.pow).then_inc(rstd_done[ln], 1)

            def out_projection(n0, slabs, ln):
                for k in range(slabs - TAIL):
                    split_lo(n0 + k + RING)
                behind = n0 + slabs - TAIL + RING
                ln_rstd(ln, 0)
                ln_rstd(ln, 1)
                split_lo(behind)
                ln_rstd(ln, 2)
                split_lo(behind + 1)
                split_lo(behind + 2)
                ln_rstd(ln, 3)
                split_lo(behind + 3)

            def feed_forward(n0):
                with pool.Fori(0, KF // 2) as i:
                    for c in range(RING):
                        split_lo(n0 + c + RING, i)

            nc.gpsimd.memset(ident[:, :], 0.0).then_inc(consts, 1)
            nc.gpsimd.memset(causal[:, :, :], 1.0).then_inc(consts, 1)
            nc.gpsimd.memset(minus_half[:, :], -0.5).then_inc(consts, 1)
            nc.gpsimd.memset(keep[:, :], 1.0).then_inc(consts, 1)
            pool.wait_ge(consts, 4)
            nc.gpsimd.affine_select(out=ident[:, :], in_=ident[:, :], compare_op=ALU.not_equal, fill=1.0, base=0,
                                    pattern=[[-1, P]], channel_multiplier=1).then_inc(consts, 1)
            nc.gpsimd.affine_select(out=causal[:, :, :], in_=causal[:, :, :], compare_op=ALU.is_ge, fill=0.0, base=0,
                                    pattern=[[0, GLA_HEADS], [1, P]], channel_multiplier=-1).then_inc(consts, 1)
            pool.wait_ge(consts, 6)
            nc.gpsimd.memset(causal[0:CHUNK, :, CHUNK:P], 0.0).then_inc(consts, 1)
            nc.gpsimd.memset(keep[:, :].rearrange("p (c i) -> p c i", i=CHUNK)[:, :, 0:1], 0.0).then_inc(consts, 1)
            pool.wait_ge(first_lo, len(FIRST))
            for n in range(1, RING):
                split_lo(n)
            for n in range(GLA_V, GLA_R):
                split_lo(n + RING)
            for half in range(2):
                for k in range(KD // 2):
                    split_lo(GLA_R + half * (KD // 2) + k + RING)
                for t in range(TILES):
                    cols = slice(half * HALF, (half + 1) * HALF)
                    pool.wait_ge(tok_out[1], half * TILES + t + 1)
                    nc.gpsimd.tensor_tensor(g_rg[:, t, cols], g_rg[:, t, cols], norm_g[:, cols], ALU.mult).then_inc(rg_done, 1)
            for n in range(GLA_QK, GLA_OUT):
                split_lo(n + RING)
            for t in range(TILES):
                pool.wait_ge(o_stats, t + 1)
                own(nc.gpsimd.tensor_scalar(var_eps_o[:, t, :], mv_o[:, t, :, 1], LN_EPS, None, ALU.add))
                nc.gpsimd.tensor_tensor(rstd_o[:, t, :], var_eps_o[:, t, :], minus_half[:, :], ALU.pow).then_inc(o_rstd, 1)
            out_projection(GLA_OUT, KD, 0)
            feed_forward(FFN_IN[0])
            out_projection(FFN_OUT[0], KF, 1)
            for n in range(RPA_V, RPA_KQ):
                split_lo(n + RING)

            def bias_relative(p):
                pool.wait_ge(bias_full[p % 2], 32 * (p // 2 + 1))
                for hd in range(2):
                    own(nc.gpsimd.tensor_scalar(r_b[:, p % 2, hd, :], r_b[:, p % 2, hd, :],
                                                far_bias[:, 2 * p + hd:2 * p + hd + 1], None, ALU.subtract))
                nc.gpsimd.memset(r_b[0:CHUNK, p % 2, :, P + CHUNK:2 * P], NEG_INF).then_inc(bias_ready, 1)

            pool.wait_ge(far_full, 16)
            bias_relative(0)
            split_lo(RPA_KQ + RING)
            split_lo(RPA_KQ + 1 + RING)
            bias_relative(1)
            for p in range(1, RPA_PAIRS - 1):
                split_lo(RPA_KQ + 2 * p + RING)
                split_lo(RPA_KQ + 2 * p + 1 + RING)
                bias_relative(p + 1)
            split_lo(RPA_OUT + RING - 2)
            for p in range(RPA_PAIRS - 1):
                pool.wait_ge(o_hi, p + 1)
                nc.gpsimd.tensor_tensor(t_lo[:, p, :], r_o[:, p, :], t_hi[:, p, :].bitcast(F32), ALU.subtract).then_inc(o_lo, 1)
                if p == 0:
                    split_lo(RPA_OUT + RING - 1)
            out_projection(RPA_OUT, KD, 2)
            feed_forward(FFN_IN[1])
            out_projection(FFN_OUT[1], KF, 3)

        @block.vector
        def _(dve):
            steps = [0]

            def own(ins):
                steps[0] += 1
                ins.then_inc(dve_step, 1)
                dve.wait_ge(dve_step, steps[0])

            def turned_low(which, t, banks):
                for half in range(2):
                    dve.wait_ge(turned_hi[which], 2 * t + half + 1)
                    nc.vector.tensor_tensor(
                        t_lo[:, 4 * half:4 * half + 4, t * P:(t + 1) * P],
                        bank[banks[t][half]][:, :].rearrange("p (k c) -> p k c", k=4),
                        t_hi[:, 4 * half:4 * half + 4, t * P:(t + 1) * P].bitcast(F32),
                        ALU.subtract).then_inc(turned_lo[which], 1)

            def layer_norm(ln, n_end):
                banks = LN_BANKS[ln]

                def add_half(t, half):
                    if ln == 3 and t == TILES - 1 and half == 1 or ln < 3 and t == TILES - 1:
                        dve.wait_ge(slab_done, n_end)
                    else:
                        dve.wait_ge(acc_done[ln], t + 1)
                    cols = slice(half * HALF, (half + 1) * HALF)
                    own(nc.vector.scalar_tensor_tensor(out=h[:, t, cols], in0=h[:, t, cols], scalar=ALPHA,
                                                       in1=bank[banks[t][half]][:, :], op0=ALU.mult, op1=ALU.add,
                                                       accum_out=half_sum[:, t, half:half + 1] if ln == 3 else None))

                def mean(t):
                    nc.vector.tensor_scalar(neg_mean[:, t:t + 1], half_sum[:, t, 0:1], half_sum[:, t, 1:2], -1.0 / D_MODEL,
                                            ALU.add, ALU.mult).then_inc(mean_done, 1)
                    own(nc.vector.tensor_scalar(mv[:, t, 0:1], half_sum[:, t, 0:1], half_sum[:, t, 1:2], 1.0 / D_MODEL,
                                                ALU.add, ALU.mult))

                def residual(t):
                    for half in range(2):
                        add_half(t, half)
                        own(nc.vector.bn_stats(bn[:, t, 6 * half:6 * half + 6], h[:, t, half * HALF:(half + 1) * HALF]))
                    nc.vector.bn_aggr(mv[:, t, :], bn[:, t, :]).then_inc(stats[ln], 1)
                    dve.wait_ge(stats[ln], t + 1)

                def centre(t, out):
                    if t == 0:
                        dve.wait_ge(gb_full, 16 * (ln + 1))
                    own(nc.vector.scalar_tensor_tensor(out=out, in0=h[:, t, :], scalar=mv[:, t, 0:1],
                                                       in1=ln_gb[:, 0, :], op0=ALU.subtract, op1=ALU.mult))

                def scale(t, centred, parts=1):
                    dve.wait_ge(rstd_done[ln], t + 1)
                    for part in range(parts):
                        cols = slice(part * D_MODEL // parts, (part + 1) * D_MODEL // parts)
                        nc.vector.scalar_tensor_tensor(out=h[:, t, cols], in0=centred[:, cols], scalar=rstd[:, t:t + 1],
                                                       in1=ln_gb[:, 1, cols], op0=ALU.mult, op1=ALU.add).then_inc(normed[ln], 1)

                def normalise(t):
                    centre(t, h[:, t, :])
                    scale(t, h[:, t, :])

                if ln == 0:
                    dve.wait_ge(h_full, 16)
                if ln < 3:
                    residual(0)
                    normalise(0)
                    residual(1)
                    normalise(1)
                    turned_low(ln, 0, banks)
                    residual(2)
                    turned_low(ln, 1, banks)
                    normalise(2)
                    residual(3)
                    normalise(3)
                    turned_low(ln, 2, banks)
                    turned_low(ln, 3, banks)
                    return
                for t in range(TILES):
                    add_half(t, 0)
                    add_half(t, 1)
                    mean(t)
                    if t > 0:
                        dve.wait_ge(normed[ln], t)
                    centre(t, centred[:, :])
                    scale(t, centred[:, :], 2 if t == TILES - 1 else 1)

            def feed_forward(f, n0):
                def body(i):
                    for c in range(2):
                        dve.wait_ge(slab_done, i * RING + (n0 + 2 * c + 2))
                        dve.wait_ge(silu_done[f], i * 2 + (c + 1))
                        nc.vector.tensor_tensor(prod[:, c, :], gate_s[:, c, :], bank[UP_BANKS[f][c]][:, :], ALU.mult).then_inc(prod_done[f], 1)
                        dve.wait_ge(a_hi_done[f], i * 2 + (c + 1))
                        nc.vector.tensor_tensor(a_lo[:, bass.ds(i * 2 + c, 1), :], prod[:, bass.ds(c, 1), :],
                                                a_hi[:, bass.ds(i * 2 + c, 1), :].bitcast(F32), ALU.subtract).then_inc(a_lo_done[f], 1)
                body(0)
                with dve.Fori(1, KF // 2) as i:
                    body(i)

            for i, (of_slab, j, cols) in enumerate(FIRST):
                dve.wait_ge(first_hi, i + 1)
                if of_slab:
                    nc.vector.tensor_tensor(w_lo[:, 0, cols], raw[:, 0, 0, cols], w_hi[:, 0, cols].bitcast(F32),
                                            ALU.subtract).then_inc(first_lo, 1)
                else:
                    nc.vector.tensor_tensor(t_lo[:, j, cols], x_t[:, j, cols], t_hi[:, j, cols].bitcast(F32),
                                            ALU.subtract).then_inc(first_lo, 1)
            for i in range(3):
                dve.wait_ge(x_hi, i + 1)
                chunks = slice(2 * i + 2, 2 * i + 4)
                nc.vector.tensor_tensor(t_lo[:, chunks, :], x_t[:, chunks, :], t_hi[:, chunks, :].bitcast(F32),
                                        ALU.subtract).then_inc(x_lo, 1)
            nc.vector.memset(wg[:, :, :].bitcast(F32), 0.0).then_inc(zeroed, 1)
            nc.vector.memset(low_rows[:, :].bitcast(F32), 0.0).then_inc(zeroed, 1)
            nc.vector.memset(up_rows[:, :].bitcast(F32), 0.0).then_inc(zeroed, 1)
            nc.vector.memset(g_am[:, :, :], 0.0).then_inc(zeroed, 1)
            dve.wait_ge(wg_hi_done, 1)
            dve.wait_ge(zeroed, 3)
            nc.vector.tensor_tensor(wg[:, :, LOW:LOW + GLA_RANK], wg_raw[:, :, :], wg[:, :, 0:GLA_RANK].bitcast(F32),
                                    ALU.subtract).then_inc(wg_lo_done, 1)
            dve.wait_ge(up_hi_done, 2)
            for group in (1, 3):
                nc.vector.tensor_tensor(up_rows[group * LOW:group * LOW + GLA_RANK, :], w_up[:, :],
                                        up_rows[0:GLA_RANK, :].bitcast(F32), ALU.subtract).then_inc(up_lo_done, 1)
            dve.wait_ge(low_part, 1)
            nc.vector.tensor_tensor(g_part[0:GLA_RANK, :], bank[0][LOW:LOW + GLA_RANK, :], g_part[LOW:LOW + GLA_RANK, :],
                                    ALU.add).then_inc(low_sum, 1)
            dve.wait_ge(low_sum, 1)
            dve.wait_ge(low_hi_done, 2)
            for group in (2, 3):
                nc.vector.tensor_tensor(low_rows[group * LOW:group * LOW + GLA_RANK, :], g_part[0:GLA_RANK, :],
                                        low_rows[0:GLA_RANK, :].bitcast(F32), ALU.subtract).then_inc(low_lo_done, 1)
            for hd in range(GLA_HEADS):
                dve.wait_ge(abs_done, hd + 1)
                if hd == 0:
                    dve.wait_ge(x_lo, 3)
                    dve.wait_ge(first_lo, len(FIRST))
                nc.vector.tensor_scalar(g_c[:, hd, :], bank[hd][:, :], b_gate[:, hd:hd + 1], 0.0, ALU.add, ALU.min).then_inc(min_done, 1)
            dve.wait_ge(min_done, GLA_HEADS)
            dve.wait_ge(log_done, 1)
            own(nc.vector.tensor_tensor(g_c[:, :, :], g_c[:, :, :], g_e[:, :, :], ALU.subtract))
            dve.wait_ge(consts, 8)
            for hd in range(GLA_HEADS):
                nc.vector.tensor_tensor_scan(g_c[:, hd, :], keep[:, :], g_c[:, hd, :], 0.0, ALU.mult, ALU.add).then_inc(cum_done, 1)
            dve.wait_ge(cum_done, GLA_HEADS)
            cum = g_c[:, :, :].rearrange("p h (c i) -> p (h c) i", i=CHUNK)
            nc.vector.tensor_tensor(g_e[:, :, :].rearrange("p h (c i) -> p (h c) i", i=CHUNK),
                                    cum[:, :, CHUNK - 1:CHUNK].to_broadcast([P, GLA_HEADS * CHUNKS, CHUNK]), cum,
                                    ALU.subtract).then_inc(rest_done, 1)
            dve.wait_ge(exps_done, 4)
            for hd in range(GLA_HEADS):
                b_q, b_k = bank[4 + 2 * (hd % 2)], bank[5 + 2 * (hd % 2)]
                dve.wait_ge(slab_done, GLA_QK + 2 * hd + 1)
                nc.vector.scalar_tensor_tensor(out=g_q[:, hd, :], in0=b_q[:, :], scalar=GLA_DK ** -0.5, in1=g_q[:, hd, :],
                                               op0=ALU.mult, op1=ALU.mult).then_inc(qk_scaled, 1)
                dve.wait_ge(slab_done, GLA_QK + 2 * hd + 2)
                nc.vector.tensor_tensor(g_ke[:, hd, :], b_k[:, :], g_ke[:, hd, :], ALU.mult).then_inc(qk_scaled, 1)
                nc.vector.tensor_tensor(g_ki[:, hd, :], b_k[:, :], g_ki[:, hd, :], ALU.mult).then_inc(qk_scaled, 1)

            def mask_scores(t):
                dve.wait_ge(sc_done, t + 1)
                if t >= 2:
                    dve.wait_ge(intra_done, t - 1)
                nc.vector.copy_predicated(g_am[:, t % 2, :], causal[:, :, :].rearrange("p h i -> p (h i)").bitcast(I32),
                                          bank[4][:, :]).then_inc(sc_masked, 1)

            def update_state(c):
                if c == CHUNKS - 1:
                    return
                dve.wait_ge(upd_done, c + 1)
                if c >= 2:
                    dve.wait_ge(inter_done, c - 1)
                if c >= 1:
                    dve.wait_ge(state_done, c)
                banks = (6, 7) if c % 2 == 0 else (2, 3)
                for hd in range(GLA_HEADS):
                    new = g_state[:, (c + 1) % 2, hd, :]
                    upd = bank[banks[hd // 2]][:, (hd % 2) * GLA_DV:(hd % 2 + 1) * GLA_DV]
                    if c == 0:
                        last = nc.vector.tensor_copy(new, upd)
                    else:
                        last = nc.vector.scalar_tensor_tensor(
                            out=new, in0=g_state[:, c % 2, hd, :], scalar=decay[:, hd * CHUNKS + c:hd * CHUNKS + c + 1],
                            in1=upd, op0=ALU.mult, op1=ALU.add)
                last.then_inc(state_done, 1)

            dve.wait_ge(zeroed, 4)
            dve.wait_ge(consts, 8)
            def gate_o(t):
                dve.wait_ge(o_out, t + 1)
                if t == 0:
                    dve.wait_ge(rg_done, 2 * TILES)
                nc.vector.tensor_tensor(g_on[:, t, :], g_on[:, t, :], g_rg[:, t, :], ALU.mult).then_inc(y_done, 1)

            mask_scores(0)
            for t in range(TILES):
                update_state(2 * t)
                if t + 1 < TILES:
                    mask_scores(t + 1)
                if t >= 1:
                    gate_o(t - 1)
                if t == TILES - 1:
                    turned_low(GLA_YT, 0, GLA_Y_BANKS)
                    turned_low(GLA_YT, 1, GLA_Y_BANKS)
                if t < TILES - 1:
                    dve.wait_ge(o_raw, 2 * t + 2)
                else:
                    dve.wait_ge(inter_done, 2 * t + 1)
                for hd in range(GLA_HEADS):
                    if t < TILES - 1:
                        o = g_on[:, t, hd * GLA_DV:(hd + 1) * GLA_DV]
                    else:
                        o = bank[hd // 2][:, (hd % 2) * GLA_DV:(hd % 2 + 1) * GLA_DV]
                    last = nc.vector.bn_stats(bn_o[:, t, hd, :], o)
                own(last)
                for hd in range(GLA_HEADS):
                    last = nc.vector.bn_aggr(mv_o[:, t, hd, :], bn_o[:, t, hd, :])
                last.then_inc(o_stats, 1)
                dve.wait_ge(o_stats, t + 1)
                update_state(2 * t + 1)
                dve.wait_ge(o_rstd, t + 1)
                nc.vector.scalar_tensor_tensor(out=shift_o[:, t, :], in0=mv_o[:, t, :, 0], scalar=-1.0,
                                               in1=rstd_o[:, t, :], op0=ALU.mult, op1=ALU.mult).then_inc(shift_done, 1)
            gate_o(TILES - 1)
            turned_low(GLA_YT, 2, GLA_Y_BANKS)
            turned_low(GLA_YT, 3, GLA_Y_BANKS)
            layer_norm(0, FFN_IN[0])
            feed_forward(0, FFN_IN[0])
            layer_norm(1, RPA_V)

            def k_low(p, hd):
                rows = own_half(hd)
                dve.wait_ge(k_hi_done, 4 * p + 2 * hd + 2)
                nc.vector.tensor_tensor(r_k_lo[rows, p % 2, hd, :], bank[0][rows, :],
                                        r_k_hi[rows, p % 2, hd, :].bitcast(F32), ALU.subtract).then_inc(k_lo_done, 1)

            def q_low(p, hd):
                rows = own_half(hd)
                dve.wait_ge(q_hi_done, 2 * p + hd + 1)
                nc.vector.scalar_tensor_tensor(out=r_q[other_half(hd), p % 2, hd, :], in0=bank[1][rows, :],
                                               scalar=RPA_D ** -0.5, in1=r_q[rows, p % 2, hd, :].bitcast(F32),
                                               op0=ALU.mult, op1=ALU.subtract).then_inc(q_lo_done, 1)

            def add_bias(s):
                p, hd, t = s // (2 * TILES), s // TILES % 2, s % TILES
                keys = (t + 1) * P
                near = min(keys, 2 * P)
                if s % (2 * TILES) == 0:
                    dve.wait_ge(bias_ready, p + 1)
                dve.wait_ge(s_done, s + 1)
                blk = bank[2 + s % 2][:, keys - near:keys]
                nc.vector.tensor_tensor(blk, blk, r_b[:, p % 2, hd, 2 * P - near:2 * P], ALU.add).then_inc(s_biased, 1)

            def max_scores(s):
                dve.wait_ge(s_biased, s + 1)
                nc.vector.tensor_reduce(neg_max[:, s:s + 1], bank[2 + s % 2][:, 0:(s % TILES + 1) * P], AX.X, ALU.max,
                                        negate=True).then_inc(max_done, 1)

            def invert_sums(s):
                dve.wait_ge(exp_done, s + 1)
                nc.vector.reciprocal(inv_sum[:, s:s + 1], row_sum[:, s:s + 1]).then_inc(inverted, 1)

            def scale_weights(s):
                dve.wait_ge(inverted, s + 1)
                w = r_p[:, s % 4, 0:(s % TILES + 1) * P]
                nc.vector.tensor_scalar(w, w, inv_sum[:, s:s + 1], None, ALU.mult).then_inc(p_scaled, 1)

            def weights_low(s):
                t = s % TILES
                dve.wait_ge(p_hi, s + 1)
                nc.vector.tensor_tensor(pt_lo[:, weight_blocks(s), :],
                                        bank[4 + s % 2][:, 0:(t + 1) * P].rearrange("p (j c) -> p j c", c=P),
                                        pt_hi[:, weight_blocks(s), :].bitcast(F32), ALU.subtract).then_inc(p_lo, 1)

            def head_sum(hd):
                p, rows = hd // 2, own_half(hd % 2)
                dve.wait_ge(o_half, hd + 1)
                if hd == RPA_HEADS - 2:
                    dve.wait_ge(o_lo, 1)
                nc.vector.tensor_tensor(r_o[rows, p % (RPA_PAIRS - 1), :], bank[6 + hd % 2][rows, :], r_half[rows, :],
                                        ALU.add).then_inc(o_summed, 1)

            def last_pair_low(hd):
                rows = own_half(hd)
                dve.wait_ge(last_hi, hd + 1)
                nc.vector.tensor_tensor(t_lo[rows, RPA_PAIRS - 1, :], r_o[rows, 0, :],
                                        t_hi[rows, RPA_PAIRS - 1, :].bitcast(F32), ALU.subtract).then_inc(last_lo, 1)

            for half in range(2):
                for t in range(TILES):
                    heads = slice(V_HEADS * half, V_HEADS * (half + 1))
                    dve.wait_ge(tok_out[2], half * TILES + t + 1)
                    nc.vector.tensor_tensor(r_v[:, t, heads, 1, :],
                                            bank[RPA_V_BANKS[4 * half + t]][:, :].rearrange("p (h d) -> p h d", d=RPA_D),
                                            r_v[:, t, heads, 0, :].bitcast(F32), ALU.subtract).then_inc(v_lo_done, 1)
            for hd in range(2):
                k_low(0, hd)
            for hd in range(2):
                q_low(0, hd)
            for s in range(UNITS + 3):
                p, step = s // (2 * TILES), s % (2 * TILES)
                ahead = p + 1 < RPA_PAIRS
                if s < UNITS:
                    add_bias(s)
                if 1 <= s <= UNITS:
                    invert_sums(s - 1)
                if s < UNITS:
                    max_scores(s)
                if 1 <= s <= UNITS:
                    scale_weights(s - 1)
                if s >= 3:
                    weights_low(s - 3)
                if ahead and step in (3, 4):
                    k_low(p + 1, step - 3)
                if ahead and step in (6, 7):
                    q_low(p + 1, step - 6)
                if 2 * TILES <= s < UNITS and s % TILES == 1:
                    head_sum(s // TILES - 2)
            head_sum(RPA_HEADS - 2)
            head_sum(RPA_HEADS - 1)
            last_pair_low(0)
            last_pair_low(1)
            layer_norm(2, FFN_IN[1])
            feed_forward(1, FFN_IN[1])
            layer_norm(3, SLABS)

        @block.tensor
        def _(pe):
            def three(out, l_hi, l_lo, r_hi, r_lo, start, stop, skip=False):
                nc.tensor.matmul(out, l_hi, r_hi, start=start, stop=False, skip_group_check=skip)
                nc.tensor.matmul(out, l_hi, r_lo, start=False, stop=False, skip_group_check=skip)
                return nc.tensor.matmul(out, l_lo, r_hi, start=False, stop=stop, skip_group_check=skip)

            def columns_piece(n, b, ks, toks=slice(0, SEQ)):
                s = n % RING
                for k in ks:
                    cols = slice(k * P, (k + 1) * P)
                    last = three(bank[b][:, toks], w_hi[:, s, cols], w_lo[:, s, cols], t_hi[:, k, toks], t_lo[:, k, toks],
                                 k == 0, k == KD - 1)
                return last

            def token_major(which, n0, bank_of, free=None, behind_ln=None, beside=None):
                def part(half, kk, t, js=range(2)):
                    n = n0 + half * (KD // 2) + kk
                    for j in js:
                        k = 2 * kk + j
                        toks = slice(t * P, (t + 1) * P)
                        cols = slice(j * HALF, (j + 1) * HALF)
                        last = three(bank[bank_of(half, t)][:, :], t_hi[:, k, toks], t_lo[:, k, toks],
                                     w_hi[:, n % RING, cols], w_lo[:, n % RING, cols], k == 0, k == KD - 1)
                    if kk == KD // 2 - 1 and t < TILES - 1:
                        last.then_inc(tok_done[which], 1)
                    return last

                for half in range(2):
                    groups = [(0, 1), (2, 3)] if half == 0 and behind_ln is not None else [(0, 1, 2, 3)]
                    for g, tiles in enumerate(groups):
                        for kk in range(KD // 2):
                            n = n0 + half * (KD // 2) + kk
                            if which == 0 and n == n0:
                                for j in range(2):
                                    for t in tiles:
                                        if t % 2 == 0:
                                            pe.wait_ge(first_lo, 2 + t // 2 if j == 0 else len(FIRST))
                                        last = part(half, kk, t, (j,))
                                last.then_inc(slab_done, 1)
                                continue
                            if g == 0:
                                pe.wait_ge(lo_done, n + 1)
                            if which == 0 and half == 0:
                                pe.wait_ge(x_lo, kk)
                            for t in tiles:
                                if kk == 0 and free is not None:
                                    free(half, t)
                                if kk == 0 and len(groups) == 2 and t % 2 == 0:
                                    pe.wait_ge(turned_lo[behind_ln], 2 * t + 4)
                                last = part(half, kk, t)
                            if g == len(groups) - 1:
                                last.then_inc(slab_done, 1)
                                if beside is not None and half == 0 and kk == 0:
                                    beside()
                            elif kk in (1, 2):
                                turn_normed(behind_ln, kk + 1)

            def turn(which, t, src, banks):
                for half in range(2):
                    for k in range(4):
                        last = nc.tensor.transpose(bank[banks[t][half]][:, k * P:(k + 1) * P],
                                                   src[:, t, (4 * half + k) * P:(4 * half + k + 1) * P], ident[:, :])
                    last.then_inc(turned[which], 1)

            def turn_normed(ln, t):
                pe.wait_ge(normed[ln], t + 1)
                turn(ln, t, h, LN_BANKS[ln])

            def out_part(n0, slabs, l_hi, l_lo, ln, k, t, halves=range(2)):
                toks = slice(t * P, (t + 1) * P)
                s = (n0 + k) % RING
                for half in halves:
                    cols = slice(half * HALF, (half + 1) * HALF)
                    last = three(bank[LN_BANKS[ln][t][half]][:, :], l_hi[:, k, toks], l_lo[:, k, toks],
                                 w_hi[:, s, cols], w_lo[:, s, cols], k == 0, k == slabs - 1)
                return last

            def out_projection(n0, slabs, l_hi, l_lo, ln, ready, free, first=None, beside=None, early=False):
                def part(k, t):
                    return out_part(n0, slabs, l_hi, l_lo, ln, k, t)

                groups = [(0, 1), (2, 3)] if first else [(0, 1, 2, 3)]
                for g, tiles in enumerate(groups):
                    for k in range(slabs - TAIL):
                        if g == 0:
                            pe.wait_ge(lo_done, n0 + k + 1)
                            ready(k)
                        for t in tiles:
                            if early and t == 0:
                                continue
                            if k == 0:
                                free(t)
                            last = part(k, t)
                        if g == len(groups) - 1:
                            last.then_inc(slab_done, 1)
                        else:
                            beside(k)
                for t in range(TILES):
                    halves = [(0,), (1,)] if ln == 3 and t == TILES - 1 else [(0, 1)]
                    for cols in halves:
                        for k in range(slabs - TAIL, slabs):
                            if t == 0:
                                pe.wait_ge(lo_done, n0 + k + 1)
                                ready(k)
                            last = out_part(n0, slabs, l_hi, l_lo, ln, k, t, cols)
                            if t == TILES - 1 and 1 in cols:
                                last.then_inc(slab_done, 1)
                            if k == slabs - TAIL // 2 - 1 and t >= 2 and ln < 3:
                                turn_normed(ln, t - 2)
                        if t < TILES - 1 or cols == (0,):
                            last.then_inc(acc_done[ln], 1)

            def feed_forward(f, n0, ln):
                def bank_of(c):
                    return (UP_BANKS if c % 2 else GATE_BANKS)[f][c // 2]

                for g in range(2):
                    pe.wait_ge(turned_lo[ln], 4 * g + 4)
                    for c in range(RING):
                        if g == 0:
                            pe.wait_ge(lo_done, n0 + c + 1)
                        last = columns_piece(n0 + c, bank_of(c), range(KD), slice(g * 2 * P, (g + 1) * 2 * P))
                        if g == 1:
                            last.then_inc(slab_done, 1)
                        elif c in (1, 2):
                            turn_normed(ln, c + 1)
                with pe.Fori(1, KF // 2) as i:
                    for c in range(RING):
                        pe.wait_ge(lo_done, i * RING + (n0 + c + 1))
                        pe.wait_ge((prod_done if c % 2 else silu_done)[f], i * 2 + (c // 2 - 1))
                        columns_piece(n0 + c, bank_of(c), range(KD)).then_inc(slab_done, 1)

            token_major(0, GLA_V, lambda half, t: 4 * half + t)
            pe.wait_ge(wg_lo_done, 1)
            pe.wait_ge(tok_out[0], 1)
            for k in range(KD):
                nc.tensor.matmul(bank[0][:, :], wg[:, k, :], t_hi[:, k, :], start=(k == 0), stop=False)
                last = nc.tensor.matmul(bank[0][:, :], wg[:, k, :], t_lo[:, k, :], start=False, stop=(k == KD - 1))
            last.then_inc(low_done, 1)

            def gate_up():
                pe.wait_ge(up_lo_done, 2)
                pe.wait_ge(low_lo_done, 2)
                pe.wait_ge(tok_out[0], TILES)
                for hd in range(GLA_HEADS):
                    nc.tensor.matmul(bank[hd][:, :], up_rows[:, hd * GLA_DK:(hd + 1) * GLA_DK], low_rows[:, :],
                                     start=True, stop=True).then_inc(up_done, 1)

            def r_free(half, t):
                if half == 0:
                    pe.wait_ge(tok_out[0], TILES + t + 1)
                else:
                    pe.wait_ge(abs_done, t + 1)
                    pe.wait_ge(min_done, t + 1)
            token_major(1, GLA_R, lambda half, t: 4 - 4 * half + t, r_free, beside=gate_up)
            for hd in range(GLA_HEADS):
                for is_k in range(2):
                    n = GLA_QK + 2 * hd + is_k
                    pe.wait_ge(lo_done, n + 1)
                    if hd < 2:
                        pe.wait_ge(tok_out[1], 2 * hd + is_k + 1)
                    else:
                        pe.wait_ge(qk_scaled, 3 * (hd - 2) + 1 + 2 * is_k)
                    columns_piece(n, 4 + 2 * (hd % 2) + is_k, range(KD)).then_inc(slab_done, 1)

            def turn_ke(t, heads=range(GLA_HEADS)):
                for hd in heads:
                    last = nc.tensor.transpose(bank[5][:, hd * P:(hd + 1) * P], g_ke[:, hd, t * P:(t + 1) * P], ident[:, :])
                    if hd == GLA_HEADS - 1:
                        last.then_inc(ke_turned, 1)

            def gla_scores(t, heads=range(GLA_HEADS)):
                toks = slice(t * P, (t + 1) * P)
                for hd in heads:
                    last = nc.tensor.matmul(bank[4][:, hd * P:(hd + 1) * P], g_ki[:, hd, toks], g_q[:, hd, toks],
                                            start=True, stop=True)
                    if hd == GLA_HEADS - 1:
                        last.then_inc(sc_done, 1)

            def updates(c):
                t, rows = c // 2, slice((c % 2) * CHUNK, (c % 2 + 1) * CHUNK)
                banks = (6, 7) if c % 2 == 0 else (2, 3)
                for hd in range(GLA_HEADS):
                    last = nc.tensor.matmul(bank[banks[hd // 2]][:, (hd % 2) * GLA_DV:(hd % 2 + 1) * GLA_DV],
                                            g_kt[rows, t % 2, hd * GLA_DK:(hd + 1) * GLA_DK],
                                            g_v[rows, t, hd * GLA_DV:(hd + 1) * GLA_DV], start=True, stop=True)
                last.then_inc(upd_done, 1)

            def inter(c):
                rows = slice((c % 2) * CHUNK, (c % 2 + 1) * CHUNK)
                for hd in range(GLA_HEADS):
                    last = nc.tensor.matmul(bank[hd // 2][rows, (hd % 2) * GLA_DV:(hd % 2 + 1) * GLA_DV],
                                            g_q[:, hd, c * CHUNK:(c + 1) * CHUNK], g_state[:, c % 2, hd, :],
                                            start=False, stop=True, skip_group_check=True)
                last.then_inc(inter_done, 1)

            def turn_y(t):
                pe.wait_ge(y_done, t + 1)
                turn(GLA_YT, t, g_on, GLA_Y_BANKS)

            pe.wait_ge(consts, 8)
            pe.wait_ge(tok_out[0], 2 * TILES)
            pe.wait_ge(qk_scaled, 3 * GLA_HEADS - 3)
            turn_ke(0, range(GLA_HEADS - 1))
            gla_scores(0, range(GLA_HEADS - 1))
            pe.wait_ge(qk_scaled, 3 * GLA_HEADS)
            turn_ke(0, (GLA_HEADS - 1,))
            gla_scores(0, (GLA_HEADS - 1,))
            pe.wait_ge(tok_out[1], 2 * TILES)
            for t in range(TILES):
                pe.wait_ge(ke_out, t + 1)
                if t >= 1:
                    pe.wait_ge(state_done, 2 * t - 1)
                updates(2 * t)
                if t + 1 < TILES:
                    pe.wait_ge(sc_masked, t + 1)
                    turn_ke(t + 1)
                    gla_scores(t + 1)
                pe.wait_ge(sc_masked, t + 1)
                if t >= 1:
                    pe.wait_ge(o_raw, 2 * t)
                for hd in range(GLA_HEADS):
                    last = nc.tensor.matmul(bank[hd // 2][:, (hd % 2) * GLA_DV:(hd % 2 + 1) * GLA_DV],
                                            g_am[:, t % 2, hd * P:(hd + 1) * P], g_v[:, t, hd * GLA_DV:(hd + 1) * GLA_DV],
                                            start=(hd % 2 == 0), stop=False, skip_group_check=True)
                last.then_inc(intra_done, 1)
                if t >= 1:
                    pe.wait_ge(state_done, 2 * t)
                    inter(2 * t)
                if t == TILES - 1:
                    pe.wait_ge(state_done, CHUNKS - 2)
                    turn_y(1)
                pe.wait_ge(state_done, 2 * t + 1)
                inter(2 * t + 1)
                if t + 1 < TILES:
                    updates(2 * t + 1)
                if t == TILES - 2:
                    pe.wait_ge(ke_out, TILES)
                    pe.wait_ge(sc_masked, TILES)
                    turn_y(0)

            def gla_out_free(t):
                if t == 0:
                    pe.wait_ge(state_done, CHUNKS - 1)
                pe.wait_ge(turned_lo[GLA_YT], 2 * t + 2)

            def gla_beside(k):
                if k == 0:
                    turn_y(2)
                if k == 2:
                    pe.wait_ge(o_out, TILES)
                    turn_y(3)
            out_projection(GLA_OUT, KD, t_hi, t_lo, 0, lambda k: None, gla_out_free, TAIL, gla_beside)
            feed_forward(0, FFN_IN[0], 0)

            def ffn_out(f, ln):
                def hidden_ready(k):
                    pe.wait_ge(a_lo_done[f], k + 1)

                def banks_free(t):
                    if t == 2:
                        pe.wait_ge(prod_done[f], KF)
                out_projection(FFN_OUT[f], KF, a_hi, a_lo, ln, hidden_ready, banks_free)
            ffn_out(0, 1)

            token_major(2, RPA_V, lambda half, t: RPA_V_BANKS[4 * half + t], behind_ln=1)

            def kq_pieces(p):
                for is_q in range(2):
                    n = RPA_KQ + 2 * p + is_q
                    for k in range(KD):
                        yield n, is_q, k, p

            def kq_piece(n, is_q, k, p):
                if k == 0:
                    pe.wait_ge(lo_done, n + 1)
                    if p >= 1:
                        pe.wait_ge(q_lo_done if is_q else k_lo_done, 2 * p)
                    else:
                        pe.wait_ge(v_lo_done, is_q + 3)
                last = columns_piece(n, is_q, [k])
                if k == KD - 1:
                    last.then_inc(slab_done, 1)

            def scores(s):
                p, hd, t = s // (2 * TILES), s // TILES % 2, s % TILES
                toks = slice(t * P, (t + 1) * P)
                keys = (t + 1) * P
                out = bank[2 + s % 2][:, 0:keys]
                if t == 0:
                    pe.wait_ge(q_lo_done, 2 * p + hd + 1)
                    pe.wait_ge(k_twice, 2 * p + hd + 1)
                if s >= 2:
                    pe.wait_ge(exp_done, s - 1)
                nc.tensor.matmul(out, r_q[:, p % 2, hd, toks], r_k_hi[:, p % 2, hd, 0:keys], start=True, stop=False)
                nc.tensor.matmul(out, r_q[:, p % 2, hd, toks], r_k_lo[:, p % 2, hd, 0:keys], start=False, stop=True).then_inc(s_done, 1)

            def turn_weights(s):
                hd, t = s // TILES, s % TILES
                pe.wait_ge(p_scaled, s + 1)
                if s >= 2:
                    pe.wait_ge(p_lo, s - 1)
                for j in range(t + 1):
                    at = j if hd % 2 == 0 else t - j
                    last = nc.tensor.transpose(bank[4 + s % 2][:, at * P:(at + 1) * P], r_p[:, s % 4, j * P:(j + 1) * P], ident[:, :])
                last.then_inc(p_turned, 1)

            def weights_v(hd, js):
                for j in js:
                    if j == 0:
                        pe.wait_ge(p_lo, TILES * (hd + 1))
                        if hd >= 2:
                            pe.wait_ge(o_summed, hd - 1)
                    out, blocks = bank[6 + hd % 2][:, j * P:SEQ], key_blocks(hd % 2, j)
                    v_parts = r_v[:, j, hd, :, :].rearrange("p a d -> p (a d)")
                    nc.tensor.matmul(out, v_parts, pt_hi[:, blocks, :], start=(j == 0), stop=False, skip_group_check=True)
                    last = nc.tensor.matmul(out, v_parts, pt_lo[:, blocks, :], start=False, stop=(j == TILES - 1),
                                            skip_group_check=True)
                    if j == TILES - 1:
                        last.then_inc(pv_done, 1)

            def rpa_out_ready(k):
                if k < RPA_PAIRS - 1:
                    pe.wait_ge(o_lo, k + 1)
                else:
                    pe.wait_ge(last_lo, 2)

            PIECES = (3, 2, 2, 1, 3, 2, 3, 0)
            for piece in kq_pieces(0):
                kq_piece(*piece)
            for piece in list(kq_pieces(1))[:PIECES[0]]:
                kq_piece(*piece)
            pe.wait_ge(v_lo_done, 2 * TILES)
            for s in range(UNITS + 1):
                p, step = s // (2 * TILES), s % (2 * TILES)
                if s >= 2 * TILES and s % TILES == 0:
                    weights_v(s // TILES - 2, (1, 2, 3))
                if s < UNITS:
                    scores(s)
                    if p + 1 < RPA_PAIRS:
                        if step == 0:
                            pieces = list(kq_pieces(p + 1))
                            if p == 0:
                                pieces = [None] * PIECES[0] + pieces[PIECES[0]:]
                        for piece in pieces[sum(PIECES[:step]):sum(PIECES[:step + 1])]:
                            if piece is not None:
                                kq_piece(*piece)
                first = s - (RPA_PAIRS - 1) * 2 * TILES - 1
                if first >= 0:
                    k = first // 2
                    pe.wait_ge(lo_done, RPA_OUT + k + 1)
                    rpa_out_ready(k)
                    if first == 0:
                        pe.wait_ge(k_lo_done, RPA_HEADS)
                        pe.wait_ge(q_lo_done, RPA_HEADS)
                    out_part(RPA_OUT, KD, t_hi, t_lo, 2, k, 0, (first % 2,))
                if s >= 2:
                    turn_weights(s - 2)
                if s >= 2 * TILES - 1 and s % TILES == 3:
                    weights_v(s // TILES - 1, (0,))

            def rpa_out_free(t):
                if t == 1:
                    pe.wait_ge(exp_done, UNITS)
                if t == 3:
                    pe.wait_ge(o_summed, RPA_HEADS)

            def rpa_beside(k):
                if k == 0:
                    turn_weights(UNITS - 1)
                if k == 1:
                    weights_v(RPA_HEADS - 1, range(TILES))
            out_projection(RPA_OUT, KD, t_hi, t_lo, 2, rpa_out_ready, rpa_out_free, TAIL, rpa_beside, early=True)
            feed_forward(1, FFN_IN[1], 2)
            ffn_out(1, 3)


def _columns(w):
    m = w.shape[1] // P
    return w.reshape(KD, P, m, P).transpose(2, 1, 0, 3).reshape(m, P, SLAB)


def _rows(w):
    return w.reshape(-1, P, SLAB)


def _token_major(w):
    return w.reshape(KD // 2, 2, P, 2, HALF).transpose(3, 0, 2, 1, 4).reshape(KD, P, SLAB)


def _paired(x, y):
    return np.stack([x, y], axis=1).reshape(-1, P, SLAB)


def kernel(x, gla_w_in, gla_w_gate_up, gla_b_gate, gla_norm_g, gla_w_out,
           rpa_w_in, rpa_rel_bias, rpa_w_out,
           mla_w_in, mla_q_norm_g, mla_kv_norm_g, mla_w_uq, mla_w_ukv, mla_w_out,
           ffn_w_in, ffn_w_out, ln_g, ln_b):
    import concourse.bacc as bacc
    from concourse.bass_utils import run_bass_kernel_spmd

    x2 = np.asarray(x)[0]
    g_in = np.asarray(gla_w_in)[0]
    q_end, k_end = GLA_HK, 2 * GLA_HK
    v_end, r_end = k_end + GLA_HV, k_end + 2 * GLA_HV
    r_in = np.asarray(rpa_w_in)[0]
    ffn_in, ffn_out = np.asarray(ffn_w_in), np.asarray(ffn_w_out)

    def ffn(i):
        return [_paired(_columns(ffn_in[i][:, :FFN]), _columns(ffn_in[i][:, FFN:])), _rows(ffn_out[i])]

    stream = np.concatenate(
        [_token_major(g_in[:, k_end:v_end]), _token_major(g_in[:, v_end:r_end]),
         _paired(_columns(g_in[:, :q_end]), _columns(g_in[:, q_end:k_end])), _rows(np.asarray(gla_w_out)[0])]
        + ffn(0)
        + [_token_major(r_in[:, 2 * D_MODEL:]),
           _paired(_columns(r_in[:, D_MODEL:2 * D_MODEL]), _columns(r_in[:, :D_MODEL])), _rows(np.asarray(rpa_w_out)[0])]
        + ffn(1))
    assert stream.shape == (SLABS, P, SLAB)
    rel = np.asarray(rpa_rel_bias)[0]
    last = rel[:, 2 * RPA_MAX_REL:]
    arrays = {
        "stream": np.ascontiguousarray(stream.reshape(SLABS // 2, 2, P, SLAB).transpose(0, 2, 1, 3)),
        "x": np.ascontiguousarray(x2),
        "x_t": np.ascontiguousarray(x2.T.reshape(KD, P, SEQ).transpose(1, 0, 2)),
        "w_gate_down": np.ascontiguousarray(g_in[:, r_end:].reshape(KD, P, GLA_RANK).transpose(1, 0, 2)),
        "w_gate_up": np.ascontiguousarray(np.asarray(gla_w_gate_up)[0]),
        "b_gate": np.ascontiguousarray(np.asarray(gla_b_gate)[0].reshape(GLA_HEADS, P).T),
        "norm_g": np.ascontiguousarray(np.asarray(gla_norm_g)[0]),
        "rel_bias": np.ascontiguousarray(np.concatenate([rel, np.repeat(last, BIAS_ROW - rel.shape[1], axis=1)], axis=1)[:, ::-1]),
        "far_bias": np.ascontiguousarray(last[:, 0]),
        "ln_gb": np.ascontiguousarray(np.stack([np.asarray(ln_g), np.asarray(ln_b)], axis=2).reshape(2 * DEPTH, 2, D_MODEL)),
    }
    nc = bacc.Bacc("TRN2", target_bir_lowering=False, num_devices=1)
    aps = {n: nc.dram_tensor(n, v.shape, mybir.dt.from_np(v.dtype), kind="ExternalInput").ap() for n, v in arrays.items()}
    aps["bias_rows"] = nc.dram_tensor("bias_rows", (RPA_HEADS, P, BIAS_ROW), F32, kind="Internal").ap()
    aps["out"] = nc.dram_tensor("out", (SEQ, D_MODEL), F32, kind="ExternalOutput").ap()
    build_program(nc, aps)
    r = run_bass_kernel_spmd(nc, [arrays], core_ids=[0])
    return r.results[0]["out"].reshape(1, SEQ, D_MODEL)
```
